# Optimizing a Trainium2 kernel written in Bass

```python
import math
import jax
import jax.numpy as jnp
from jax import lax
import numpy as np

D_MODEL = 1024
BATCH = 1
SEQ = 512
DEPTH = 1

CHUNK = 64
Q_BLOCK = 128
PLE_DIM = 256
EPS = 1e-6
NEG_INF = -1e30

MLA_HEADS = 8
MLA_Q_RANK = 256
MLA_KV_RANK = 128
MLA_NOPE = 64
MLA_ROPE = 32
MLA_QK = MLA_NOPE + MLA_ROPE
MLA_V = 64
ROPE_THETA = 10000.0

DIFF_HEADS = 4
DIFF_QK = 64
DIFF_V = 2 * DIFF_QK

MIX_WIDTH = MLA_HEADS * MLA_V + DIFF_HEADS * DIFF_V

NUM_BUCKETS = 32
MAX_DISTANCE = 1024

D_FF = 2816
CONV_WIDTH = 3

OFF_Q_LAT = 0
OFF_KV_LAT = OFF_Q_LAT + MLA_Q_RANK
OFF_K_ROPE = OFF_KV_LAT + MLA_KV_RANK
OFF_DIFF_Q = OFF_K_ROPE + MLA_ROPE
OFF_DIFF_K = OFF_DIFF_Q + DIFF_HEADS * 2 * DIFF_QK
OFF_DIFF_V = OFF_DIFF_K + DIFF_HEADS * 2 * DIFF_QK
IN_COLS = OFF_DIFF_V + DIFF_HEADS * DIFF_V


def lambda_init(layer):
    return 0.8 - 0.6 * math.exp(-0.3 * layer)

def rms_norm(x, g):
    xf = x.astype(jnp.float32)
    y = xf * lax.rsqrt(jnp.mean(xf * xf, axis=-1, keepdims=True) + EPS)
    return (y * g.astype(jnp.float32)).astype(x.dtype)

def apply_rope(t, pos):
    half = t.shape[-1] // 2
    inv_freq = ROPE_THETA ** (-jnp.arange(half, dtype=jnp.float32) / half)
    ang = pos.astype(jnp.float32)[:, None] * inv_freq[None, :]
    cos = jnp.cos(ang)[None, :, None, :].astype(t.dtype)
    sin = jnp.sin(ang)[None, :, None, :].astype(t.dtype)
    t1, t2 = t[..., :half], t[..., half:]
    return jnp.concatenate([t1 * cos - t2 * sin, t2 * cos + t1 * sin], axis=-1)

def t5_bucket(rel):
    nb = NUM_BUCKETS // 2
    max_exact = nb // 2
    sign_off = (rel > 0).astype(jnp.int32) * nb
    n = jnp.abs(rel)
    nf = jnp.maximum(n, 1).astype(jnp.float32)
    large = max_exact + (jnp.log(nf / max_exact) / math.log(MAX_DISTANCE / max_exact)
                         * (nb - max_exact)).astype(jnp.int32)
    large = jnp.minimum(large, nb - 1)
    return sign_off + jnp.where(n < max_exact, n, large)

def block_indices(blk, seq):
    q_idx = blk * Q_BLOCK + jnp.arange(Q_BLOCK, dtype=jnp.int32)
    k_idx = jnp.arange(seq, dtype=jnp.int32)
    return q_idx, k_idx

def chunk_allowed(q_idx, k_idx):
    return (k_idx[None, :] // CHUNK) <= (q_idx[:, None] // CHUNK)

def to_blocks(t):
    b, s, h, d = t.shape
    return t.reshape(b, s // Q_BLOCK, Q_BLOCK, h, d).transpose(1, 0, 3, 2, 4)

def from_blocks(t):
    n, b, h, qb, d = t.shape
    return t.transpose(1, 0, 3, 2, 4).reshape(b, n * qb, h, d)

def mla_group(q_lat, kv_lat, k_rope, pos, q_lat_g, w_uq, kv_lat_g, w_ukv, q_g, k_g):
    b, s, _ = q_lat.shape
    q = (rms_norm(q_lat, q_lat_g) @ w_uq).reshape(b, s, MLA_HEADS, MLA_QK)
    kv = (rms_norm(kv_lat, kv_lat_g) @ w_ukv).reshape(b, s, MLA_HEADS, MLA_NOPE + MLA_V)
    k_nope, v = kv[..., :MLA_NOPE], kv[..., MLA_NOPE:]
    k_r = jnp.broadcast_to(k_rope[:, :, None, :], (b, s, MLA_HEADS, MLA_ROPE))
    k = jnp.concatenate([k_nope, k_r], axis=-1)
    q = rms_norm(q, q_g)
    k = rms_norm(k, k_g)
    q = jnp.concatenate([q[..., :MLA_NOPE], apply_rope(q[..., MLA_NOPE:], pos)], axis=-1)
    k = jnp.concatenate([k[..., :MLA_NOPE], apply_rope(k[..., MLA_NOPE:], pos)], axis=-1)
    k_t = k.transpose(0, 2, 1, 3)
    v_t = v.transpose(0, 2, 1, 3)
    scale = MLA_QK ** -0.5

    def one_block(args):
        qb, blk = args
        q_idx, k_idx = block_indices(blk, s)
        allowed = chunk_allowed(q_idx, k_idx)
        logits = jnp.einsum('bhqd,bhkd->bhqk', qb, k_t).astype(jnp.float32) * scale
        logits = jnp.where(allowed[None, None], logits, NEG_INF)
        probs = jax.nn.softmax(logits, axis=-1).astype(v_t.dtype)
        return jnp.einsum('bhqk,bhkd->bhqd', probs, v_t)

    o = lax.map(one_block, (to_blocks(q), jnp.arange(s // Q_BLOCK, dtype=jnp.int32)))
    return from_blocks(o).reshape(b, s, MLA_HEADS * MLA_V)

def diff_group(dq, dk, dv, q_g, k_g, lq1, lk1, lq2, lk2, out_g, rel_bias, lam_init):
    b, s, _ = dq.shape
    q = rms_norm(dq.reshape(b, s, DIFF_HEADS, 2, DIFF_QK), q_g)
    k = rms_norm(dk.reshape(b, s, DIFF_HEADS, 2, DIFF_QK), k_g)
    k_t = k.transpose(0, 2, 3, 1, 4)
    v_t = dv.reshape(b, s, DIFF_HEADS, DIFF_V).transpose(0, 2, 1, 3)
    f32 = jnp.float32
    lam = (jnp.exp(jnp.sum(lq1.astype(f32) * lk1.astype(f32)))
           - jnp.exp(jnp.sum(lq2.astype(f32) * lk2.astype(f32))) + lam_init)
    scale = DIFF_QK ** -0.5
    table = rel_bias.astype(f32)

    def one_block(args):
        qb, blk = args
        qb = qb.reshape(b, DIFF_HEADS, Q_BLOCK, 2, DIFF_QK)
        q_idx, k_idx = block_indices(blk, s)
        allowed = chunk_allowed(q_idx, k_idx)
        bias = table[t5_bucket(k_idx[None, :] - q_idx[:, None])].transpose(2, 0, 1)
        logits = jnp.einsum('bhqmd,bhmkd->bhmqk', qb, k_t).astype(f32) * scale
        logits = logits + bias[None, :, None]
        logits = jnp.where(allowed[None, None, None], logits, NEG_INF)
        probs = jax.nn.softmax(logits, axis=-1)
        attn = (probs[:, :, 0] - lam * probs[:, :, 1]).astype(v_t.dtype)
        return jnp.einsum('bhqk,bhkd->bhqd', attn, v_t)

    qf = q.reshape(b, s, DIFF_HEADS, 2 * DIFF_QK)
    o = lax.map(one_block, (to_blocks(qf), jnp.arange(s // Q_BLOCK, dtype=jnp.int32)))
    o = rms_norm(from_blocks(o), out_g) * (1.0 - lam_init)
    return o.reshape(b, s, DIFF_HEADS * DIFF_V)

def conv_ffn(h, w_gate, w_up, conv_w, conv_b, w_down):
    s = h.shape[1]
    g = h @ w_gate
    gp = jnp.pad(g, ((0, 0), (CONV_WIDTH - 1, 0), (0, 0)))
    conv = conv_b
    for j in range(CONV_WIDTH):
        conv = conv + gp[:, j:j + s, :] * conv_w[j]
    return (jax.nn.silu(conv) * (h @ w_up)) @ w_down

def first_inputs(seed: int = 0) -> dict:
    key = jax.random.key(seed)
    ks = jax.random.split(key, 28)
    f32 = jnp.float32

    def nrm(k, shape, scale):
        return jax.random.normal(k, shape, dtype=f32) * scale

    def gain(k, shape):
        return 1.0 + 0.1 * jax.random.normal(k, shape, dtype=f32)

    return {
        'x': nrm(ks[0], (BATCH, SEQ, D_MODEL), 1.0),
        'p': nrm(ks[1], (DEPTH, BATCH, SEQ, PLE_DIM), 1.0),
        'attn_norm_g': gain(ks[2], (DEPTH, D_MODEL)),
        'w_in': nrm(ks[3], (DEPTH, D_MODEL, IN_COLS), D_MODEL ** -0.5),
        'q_lat_norm_g': gain(ks[4], (DEPTH, MLA_Q_RANK)),
        'w_uq': nrm(ks[5], (DEPTH, MLA_Q_RANK, MLA_HEADS * MLA_QK), MLA_Q_RANK ** -0.5),
        'kv_lat_norm_g': gain(ks[6], (DEPTH, MLA_KV_RANK)),
        'w_ukv': nrm(ks[7], (DEPTH, MLA_KV_RANK, MLA_HEADS * (MLA_NOPE + MLA_V)), MLA_KV_RANK ** -0.5),
        'mla_q_norm_g': gain(ks[8], (DEPTH, MLA_QK)),
        'mla_k_norm_g': gain(ks[9], (DEPTH, MLA_QK)),
        'diff_q_norm_g': gain(ks[10], (DEPTH, DIFF_QK)),
        'diff_k_norm_g': gain(ks[11], (DEPTH, DIFF_QK)),
        'lambda_q1': nrm(ks[12], (DEPTH, DIFF_QK), 0.1),
        'lambda_k1': nrm(ks[13], (DEPTH, DIFF_QK), 0.1),
        'lambda_q2': nrm(ks[14], (DEPTH, DIFF_QK), 0.1),
        'lambda_k2': nrm(ks[15], (DEPTH, DIFF_QK), 0.1),
        'diff_out_norm_g': gain(ks[16], (DEPTH, DIFF_V)),
        'rel_bias': nrm(ks[17], (NUM_BUCKETS, DIFF_HEADS), 0.5),
        'w_out': nrm(ks[18], (DEPTH, MIX_WIDTH, D_MODEL), MIX_WIDTH ** -0.5),
        'ffn_norm_g': gain(ks[19], (DEPTH, D_MODEL)),
        'w_gate': nrm(ks[20], (DEPTH, D_MODEL, D_FF), D_MODEL ** -0.5),
        'w_up': nrm(ks[21], (DEPTH, D_MODEL, D_FF), D_MODEL ** -0.5),
        'conv_w': nrm(ks[22], (DEPTH, CONV_WIDTH, D_FF), CONV_WIDTH ** -0.5),
        'conv_b': nrm(ks[23], (DEPTH, D_FF), 0.02),
        'w_down': nrm(ks[24], (DEPTH, D_FF, D_MODEL), D_FF ** -0.5),
        'ple_norm_g': gain(ks[25], (DEPTH, D_MODEL)),
        'w_ple_gate': nrm(ks[26], (DEPTH, D_MODEL, D_MODEL), D_MODEL ** -0.5),
        'w_ple_proj': nrm(ks[27], (DEPTH, PLE_DIM, D_MODEL), PLE_DIM ** -0.5),
    }

def first_block(x, p, attn_norm_g, w_in, q_lat_norm_g, w_uq, kv_lat_norm_g, w_ukv,
              mla_q_norm_g, mla_k_norm_g, diff_q_norm_g, diff_k_norm_g,
              lambda_q1, lambda_k1, lambda_q2, lambda_k2, diff_out_norm_g, rel_bias,
              w_out, ffn_norm_g, w_gate, w_up, conv_w, conv_b, w_down,
              ple_norm_g, w_ple_gate, w_ple_proj):
    s = x.shape[1]
    pos = jnp.arange(s, dtype=jnp.int32)
    for i in range(DEPTH):
        h = rms_norm(x, attn_norm_g[i])
        z = h @ w_in[i]
        y_mla = mla_group(z[..., OFF_Q_LAT:OFF_KV_LAT], z[..., OFF_KV_LAT:OFF_K_ROPE],
                          z[..., OFF_K_ROPE:OFF_DIFF_Q], pos,
                          q_lat_norm_g[i], w_uq[i], kv_lat_norm_g[i], w_ukv[i],
                          mla_q_norm_g[i], mla_k_norm_g[i])
        y_diff = diff_group(z[..., OFF_DIFF_Q:OFF_DIFF_K], z[..., OFF_DIFF_K:OFF_DIFF_V],
                            z[..., OFF_DIFF_V:IN_COLS],
                            diff_q_norm_g[i], diff_k_norm_g[i],
                            lambda_q1[i], lambda_k1[i], lambda_q2[i], lambda_k2[i],
                            diff_out_norm_g[i], rel_bias, lambda_init(i))
        x = x + jnp.concatenate([y_mla, y_diff], axis=-1) @ w_out[i]
        x = x + conv_ffn(rms_norm(x, ffn_norm_g[i]), w_gate[i], w_up[i], conv_w[i], conv_b[i], w_down[i])
        gate = jax.nn.sigmoid(rms_norm(x, ple_norm_g[i]) @ w_ple_gate[i])
        x = x + gate * (p[i] @ w_ple_proj[i])
    return x


ATT_HEADS = 8
ATT_HEAD_DIM = 128
KV_LATENT = 256
IDX_HEADS = 8
IDX_DIM = 64
TOPK_MAX = 256
ATT_SCALE = ATT_HEAD_DIM ** -0.5
INDEX_SCALE = (IDX_HEADS ** -0.5) * (IDX_DIM ** -0.5)
DN_HEADS = 8
DN_DK = 128
DN_DV = 128
CONV_WIDTH_2 = 4
N_GROUPS = 4
EXPERTS_PER_GROUP = 8
N_EXPERTS = N_GROUPS * EXPERTS_PER_GROUP
EXPERT_TOPK = 2
EXPERT_FF = 512
MOE_BLOCK = 128
LN_EPS = 1e-5
RMS_EPS = 1e-6

ATT_Q_COLS = ATT_HEADS * ATT_HEAD_DIM
IDX_Q_COLS = IDX_HEADS * IDX_DIM
DN_QK_COLS = DN_HEADS * DN_DK
DN_V_COLS = DN_HEADS * DN_DV
CONV_CH = 2 * DN_QK_COLS + DN_V_COLS
COL_SIZES = (ATT_Q_COLS, KV_LATENT, IDX_Q_COLS, IDX_DIM, IDX_HEADS,
             CONV_CH, DN_HEADS, DN_HEADS, DN_V_COLS, 2 * D_MODEL)
N_IN = sum(COL_SIZES)
SPLITS = tuple(int(v) for v in np.cumsum(COL_SIZES)[:-1])


def layer_norm(x, g, b):
    xf = x.astype(jnp.float32)
    mu = jnp.mean(xf, axis=-1, keepdims=True)
    var = jnp.mean(jnp.square(xf - mu), axis=-1, keepdims=True)
    return ((xf - mu) * lax.rsqrt(var + LN_EPS)).astype(x.dtype) * g + b

def rms_norm_2(x, g):
    xf = x.astype(jnp.float32)
    return (xf * lax.rsqrt(jnp.mean(xf * xf, axis=-1, keepdims=True) + RMS_EPS)).astype(x.dtype) * g

def l2_normalize(x):
    return x * lax.rsqrt(jnp.sum(x * x, axis=-1, keepdims=True) + RMS_EPS)

def causal_conv(x, w):
    width = w.shape[0]
    return lax.conv_general_dilated(
        x, w[:, None, :], window_strides=(1,), padding=[(width - 1, 0)],
        dimension_numbers=('NWC', 'WIO', 'NWC'), feature_group_count=x.shape[-1])

def dsa_attention(q_att, c_kv, q_idx, k_idx, w_idx, w_uk, w_uv):
    B, S = c_kv.shape[0], c_kv.shape[1]
    topk = min(TOPK_MAX, S // 4)
    nb = S // Q_BLOCK
    q_lat = jnp.einsum('bshd,hcd->bshc', q_att, w_uk)
    key_pos = jnp.arange(S)
    gather = jax.vmap(lambda table, idx: table[idx])

    def to_blocks(t):
        return jnp.moveaxis(t.reshape((B, nb, Q_BLOCK) + t.shape[2:]), 1, 0)

    def block(args):
        ql, qi, wi, t0 = args
        qpos = t0 + jnp.arange(Q_BLOCK)
        rel = jax.nn.relu(jnp.einsum('bqhd,bsd->bqhs', qi, k_idx))
        iscore = jnp.einsum('bqhs,bqh->bqs', rel, wi).astype(jnp.float32)
        causal = key_pos[None, :] <= qpos[:, None]
        iscore = jnp.where(causal[None], iscore, -jnp.inf)
        _, sel = lax.top_k(iscore, topk)
        kv = gather(c_kv, sel)
        s = jnp.einsum('bqhc,bqkc->bqhk', ql, kv).astype(jnp.float32) * ATT_SCALE
        valid = sel <= qpos[None, :, None]
        s = jnp.where(valid[:, :, None, :], s, -jnp.inf)
        p = jax.nn.softmax(s, axis=-1).astype(kv.dtype)
        return jnp.einsum('bqhk,bqkc->bqhc', p, kv)

    o_lat = lax.map(block, (to_blocks(q_lat), to_blocks(q_idx), to_blocks(w_idx),
                            jnp.arange(nb) * Q_BLOCK))
    o_lat = jnp.moveaxis(o_lat, 0, 1).reshape(B, S, ATT_HEADS, KV_LATENT)
    o = jnp.einsum('bshc,hcd->bshd', o_lat, w_uv)
    return o.reshape(B, S, ATT_HEADS * ATT_HEAD_DIM)

def chunk_gated_delta_rule(q, k, v, beta, g):
    B, S, H, Dk = q.shape
    Dv = v.shape[-1]
    n = S // CHUNK

    def chunks(t):
        return t.reshape(B, n, CHUNK, H, -1).transpose(0, 3, 1, 2, 4)

    q, k, v = chunks(q), chunks(k), chunks(v)
    beta = beta.reshape(B, n, CHUNK, H).transpose(0, 3, 1, 2)
    G = jnp.cumsum(g.reshape(B, n, CHUNK, H).transpose(0, 3, 1, 2), axis=-1)
    tril = jnp.tril(jnp.ones((CHUNK, CHUNK), dtype=bool))
    tril_strict = jnp.tril(jnp.ones((CHUNK, CHUNK), dtype=bool), -1)
    decay = jnp.exp(jnp.where(tril, G[..., :, None] - G[..., None, :], -jnp.inf))
    kb = k * beta[..., None]
    A = jnp.where(tril_strict, jnp.einsum('bhncd,bhnsd->bhncs', kb, k) * decay, 0.0)
    eye = jnp.eye(CHUNK, dtype=A.dtype)
    rhs = jnp.concatenate([v * beta[..., None], kb * jnp.exp(G)[..., None]], axis=-1)
    sol = lax.linalg.triangular_solve(eye + A, rhs, left_side=True, lower=True,
                                      unit_diagonal=True)
    u, w = sol[..., :Dv], sol[..., Dv:]
    qk = jnp.where(tril, jnp.einsum('bhncd,bhnsd->bhncs', q, k) * decay, 0.0)
    q_dec = q * jnp.exp(G)[..., None]
    k_tail = k * jnp.exp(G[..., -1:] - G)[..., None]
    g_last = jnp.exp(G[..., -1])

    def step(state, xs):
        q_n, k_n, u_n, w_n, qk_n, gl_n = xs
        v_new = u_n - jnp.einsum('bhck,bhkv->bhcv', w_n, state)
        o_n = (jnp.einsum('bhck,bhkv->bhcv', q_n, state)
               + jnp.einsum('bhcs,bhsv->bhcv', qk_n, v_new))
        state = state * gl_n[..., None, None] + jnp.einsum('bhck,bhcv->bhkv', k_n, v_new)
        return state, o_n

    xs = tuple(jnp.moveaxis(t, 2, 0) for t in (q_dec, k_tail, u, w, qk, g_last))
    state0 = jnp.zeros((B, H, Dk, Dv), jnp.float32)
    _, o = lax.scan(step, state0, xs)
    return o.transpose(1, 0, 3, 2, 4).reshape(B, S, H, Dv)

def gated_deltanet(qkv, a, b, z, conv_w, a_log, dt_bias, norm_g):
    B, S = qkv.shape[0], qkv.shape[1]
    dtype = qkv.dtype
    qkv = jax.nn.silu(causal_conv(qkv, conv_w)).astype(jnp.float32)
    q = l2_normalize(qkv[..., :DN_QK_COLS].reshape(B, S, DN_HEADS, DN_DK)) * (DN_DK ** -0.5)
    k = l2_normalize(qkv[..., DN_QK_COLS:2 * DN_QK_COLS].reshape(B, S, DN_HEADS, DN_DK))
    v = qkv[..., 2 * DN_QK_COLS:].reshape(B, S, DN_HEADS, DN_DV)
    beta = jax.nn.sigmoid(b.astype(jnp.float32))
    g = -jnp.exp(a_log.astype(jnp.float32)) * jax.nn.softplus(
        a.astype(jnp.float32) + dt_bias.astype(jnp.float32))
    o = chunk_gated_delta_rule(q, k, v, beta, g)
    zf = z.astype(jnp.float32).reshape(B, S, DN_HEADS, DN_DV)
    o = rms_norm_2(o, norm_g.astype(jnp.float32)) * jax.nn.silu(zf)
    return o.reshape(B, S, DN_V_COLS).astype(dtype)

def token_mixer(h, w_in, kv_norm_g, w_uk, w_uv, conv_w, a_log, dt_bias, dn_norm_g,
                w_br_att, w_br_dn, w_out):
    B, S = h.shape[0], h.shape[1]
    proj = h @ w_in
    (q_att, c_kv, q_idx, k_idx, w_idx, qkv, a, b, z, gates) = jnp.split(proj, SPLITS, axis=-1)
    c_kv = rms_norm_2(c_kv, kv_norm_g)
    y_att = dsa_attention(q_att.reshape(B, S, ATT_HEADS, ATT_HEAD_DIM), c_kv,
                          q_idx.reshape(B, S, IDX_HEADS, IDX_DIM), k_idx,
                          w_idx * INDEX_SCALE, w_uk, w_uv)
    y_dn = gated_deltanet(qkv, a, b, z, conv_w, a_log, dt_bias, dn_norm_g)
    gates = jax.nn.sigmoid(gates)
    g_att, g_dn = gates[..., :D_MODEL], gates[..., D_MODEL:]
    merged = g_att * (y_att @ w_br_att) + g_dn * (y_dn @ w_br_dn)
    return merged @ w_out

def hier_moe(h, w_route_grp, w_route_exp, w_gate, w_up, w_down):
    B, S, D = h.shape
    n_tok = B * S
    xt = h.reshape(n_tok, D)
    p_grp = jax.nn.softmax((xt @ w_route_grp).astype(jnp.float32), axis=-1)
    top_gp, g_idx = lax.top_k(p_grp, 1)
    exp_logits = (xt @ w_route_exp).astype(jnp.float32).reshape(n_tok, N_GROUPS, EXPERTS_PER_GROUP)
    in_grp = jnp.take_along_axis(exp_logits, g_idx[:, :, None], axis=1)[:, 0]
    top_pe, e_local = lax.top_k(jax.nn.softmax(in_grp, axis=-1), EXPERT_TOPK)
    gates = top_pe / jnp.sum(top_pe, axis=-1, keepdims=True) * top_gp
    e_idx = g_idx * EXPERTS_PER_GROUP + e_local

    m = n_tok * EXPERT_TOPK
    flat_e = e_idx.reshape(m)
    flat_tok = jnp.repeat(jnp.arange(n_tok), EXPERT_TOPK)
    flat_gate = gates.reshape(m)
    order = jnp.argsort(flat_e)
    se = flat_e[order]
    counts = jnp.bincount(flat_e, length=N_EXPERTS)
    pcounts = (counts + MOE_BLOCK - 1) // MOE_BLOCK * MOE_BLOCK
    starts = jnp.cumsum(counts) - counts
    pends = jnp.cumsum(pcounts)
    pstarts = pends - pcounts
    dest = pstarts[se] + jnp.arange(m) - starts[se]
    nb = -(-m // MOE_BLOCK) + N_EXPERTS
    rows = nb * MOE_BLOCK
    tok_buf = jnp.full((rows,), n_tok, jnp.int32).at[dest].set(flat_tok[order])
    gate_buf = jnp.zeros((rows,), jnp.float32).at[dest].set(flat_gate[order])
    blk_e = jnp.minimum(jnp.searchsorted(pends, jnp.arange(nb) * MOE_BLOCK, side='right'),
                        N_EXPERTS - 1)
    x_pad = jnp.concatenate([xt, jnp.zeros((1, D), xt.dtype)], axis=0)
    xs = x_pad[tok_buf].reshape(nb, MOE_BLOCK, D)

    def expert_block(args):
        xb, e = args
        hb = jax.nn.silu(xb @ w_gate[e]) * (xb @ w_up[e])
        return hb @ w_down[e]

    yb = lax.map(expert_block, (xs, blk_e)).reshape(rows, D)
    yb = yb * gate_buf[:, None].astype(yb.dtype)
    out = jnp.zeros((n_tok + 1, D), yb.dtype).at[tok_buf].add(yb)[:n_tok]
    return out.reshape(B, S, D)

def second_inputs(seed: int = 0) -> dict:
    key = jax.random.key(seed)
    ks = jax.random.split(key, 24)
    f32 = jnp.float32
    L, D = DEPTH, D_MODEL
    beta = (8.0 * DEPTH) ** -0.25

    def nrm(k, shape, scale):
        return jax.random.normal(k, shape, f32) * scale

    dt = jnp.exp(jax.random.uniform(ks[10], (L, DN_HEADS), f32, math.log(1e-3), math.log(1e-1)))
    return {
        'x': nrm(ks[0], (BATCH, SEQ, D), 1.0),
        'c': nrm(ks[1], (BATCH, D), 1.0),
        'w_ada': nrm(ks[2], (L, D, 6 * D), 0.1 * D ** -0.5),
        'b_ada': nrm(ks[3], (L, 6 * D), 0.01),
        'w_in': nrm(ks[4], (L, D, N_IN), D ** -0.5),
        'kv_norm_g': 1.0 + nrm(ks[5], (L, KV_LATENT), 0.02),
        'w_uk': nrm(ks[6], (L, ATT_HEADS, KV_LATENT, ATT_HEAD_DIM), KV_LATENT ** -0.5),
        'w_uv': nrm(ks[7], (L, ATT_HEADS, KV_LATENT, ATT_HEAD_DIM), KV_LATENT ** -0.5),
        'conv_w': nrm(ks[8], (L, CONV_WIDTH_2, CONV_CH), CONV_WIDTH_2 ** -0.5),
        'a_log': jnp.log(jax.random.uniform(ks[9], (L, DN_HEADS), f32, 1.0, 16.0)),
        'dt_bias': dt + jnp.log(-jnp.expm1(-dt)),
        'dn_norm_g': 1.0 + nrm(ks[11], (L, DN_DV), 0.02),
        'w_br_att': nrm(ks[12], (L, ATT_Q_COLS, D), ATT_Q_COLS ** -0.5),
        'w_br_dn': nrm(ks[13], (L, DN_V_COLS, D), DN_V_COLS ** -0.5),
        'w_out': nrm(ks[14], (L, D, D), beta * D ** -0.5),
        'w_route_grp': nrm(ks[15], (L, D, N_GROUPS), D ** -0.5),
        'w_route_exp': nrm(ks[16], (L, D, N_EXPERTS), D ** -0.5),
        'w_gate': nrm(ks[17], (L, N_EXPERTS, D, EXPERT_FF), D ** -0.5),
        'w_up': nrm(ks[18], (L, N_EXPERTS, D, EXPERT_FF), D ** -0.5),
        'w_down': nrm(ks[19], (L, N_EXPERTS, EXPERT_FF, D), beta * EXPERT_FF ** -0.5),
        'ln_g': 1.0 + nrm(ks[20], (L, 2, D), 0.02),
        'ln_b': nrm(ks[21], (L, 2, D), 0.02),
    }

def second_block(x, c, w_ada, b_ada, w_in, kv_norm_g, w_uk, w_uv, conv_w, a_log, dt_bias,
              dn_norm_g, w_br_att, w_br_dn, w_out, w_route_grp, w_route_exp, w_gate,
              w_up, w_down, ln_g, ln_b):
    alpha = (2.0 * DEPTH) ** 0.25
    cond = jax.nn.silu(c)
    for l in range(DEPTH):
        mod = cond @ w_ada[l] + b_ada[l]
        sh1, sc1, gt1, sh2, sc2, gt2 = [m[:, None, :] for m in jnp.split(mod, 6, axis=-1)]
        h = x * (1.0 + sc1) + sh1
        y = token_mixer(h, w_in[l], kv_norm_g[l], w_uk[l], w_uv[l], conv_w[l], a_log[l],
                        dt_bias[l], dn_norm_g[l], w_br_att[l], w_br_dn[l], w_out[l])
        x = layer_norm(alpha * x + (1.0 + gt1) * y, ln_g[l, 0], ln_b[l, 0])
        h = x * (1.0 + sc2) + sh2
        y = hier_moe(h, w_route_grp[l], w_route_exp[l], w_gate[l], w_up[l], w_down[l])
        x = layer_norm(alpha * x + (1.0 + gt2) * y, ln_g[l, 1], ln_b[l, 1])
    return x


def setup_inputs(seed=0):
    out = dict(first_inputs(seed))
    for name, value in second_inputs(seed + 1).items():
        if name != "x":
            out[name + "_2"] = value
    return out


def reference(
    x, p, attn_norm_g, w_in, q_lat_norm_g, w_uq, kv_lat_norm_g, w_ukv, mla_q_norm_g,
    mla_k_norm_g, diff_q_norm_g, diff_k_norm_g, lambda_q1, lambda_k1, lambda_q2, lambda_k2,
    diff_out_norm_g, rel_bias, w_out, ffn_norm_g, w_gate, w_up, conv_w, conv_b, w_down,
    ple_norm_g, w_ple_gate, w_ple_proj, c_2, w_ada_2, b_ada_2, w_in_2, kv_norm_g_2, w_uk_2,
    w_uv_2, conv_w_2, a_log_2, dt_bias_2, dn_norm_g_2, w_br_att_2, w_br_dn_2, w_out_2,
    w_route_grp_2, w_route_exp_2, w_gate_2, w_up_2, w_down_2, ln_g_2, ln_b_2,
):
    x = first_block(
        x, p, attn_norm_g, w_in, q_lat_norm_g, w_uq, kv_lat_norm_g, w_ukv, mla_q_norm_g,
        mla_k_norm_g, diff_q_norm_g, diff_k_norm_g, lambda_q1, lambda_k1, lambda_q2, lambda_k2,
        diff_out_norm_g, rel_bias, w_out, ffn_norm_g, w_gate, w_up, conv_w, conv_b, w_down,
        ple_norm_g, w_ple_gate, w_ple_proj,
    )
    return second_block(
        x, c_2, w_ada_2, b_ada_2, w_in_2, kv_norm_g_2, w_uk_2, w_uv_2, conv_w_2, a_log_2,
        dt_bias_2, dn_norm_g_2, w_br_att_2, w_br_dn_2, w_out_2, w_route_grp_2, w_route_exp_2,
        w_gate_2, w_up_2, w_down_2, ln_g_2, ln_b_2,
    )


_drawn_inputs = setup_inputs


def setup_inputs(seed=0):
    import zlib

    import numpy as np

    out = dict(_drawn_inputs(seed))
    spreads = {}
    factors = {'q_lat_norm_g': 4.518,
     'kv_lat_norm_g': 3.022,
     'mla_q_norm_g': 3.865,
     'mla_k_norm_g': 3.995,
     'lambda_q2': 7.09,
     'conv_b': 4.727,
     'ple_norm_g': 2.765,
     'b_ada_2': 3.912,
     'kv_norm_g_2': 22.82,
     'dn_norm_g_2': 22.091}
    for name, (base, spread) in spreads.items():
        noise = np.random.default_rng([zlib.crc32(name.encode()), seed]).standard_normal(out[name].shape)
        drawn = base * np.exp(spread * noise) if base else spread * noise
        out[name] = jnp.asarray(drawn.astype(out[name].dtype))
    for name, factor in factors.items():
        out[name] = (out[name] * factor).astype(out[name].dtype)
    return out
```

```python
import math
from collections import Counter
from contextlib import ExitStack

import numpy as np

import concourse.bass as bass
from concourse import mybir

ALU = mybir.AluOpType
ACT = mybir.ActivationFunctionType
AX = mybir.AxisListType
F32 = mybir.dt.float32
I32 = mybir.dt.int32

P = 128
SEQ, D = 512, 1024
NT, KD = SEQ // P, D // P
EPS, LN_EPS, NEG = 1e-6, 1e-5, -1e30

Q_RANK, KV_RANK, NOPE, ROPE, MLA_H = 256, 128, 64, 32, 8
QK = NOPE + ROPE
MLA_V = 64
DIFF_H, DIFF_QK, DIFF_V = 4, 64, 128
LAT = Q_RANK + KV_RANK + ROPE
CHUNK, BUCKETS, MAX_DISTANCE = 64, 32, 1024
D_FF, CONV1 = 2816, 3
FT = D_FF // P
PLE = 256
LAM_INIT = 0.8 - 0.6 * math.exp(0.0)

H2, DH = 8, 128
KV_LAT, IDX_H, IDX_D = 256, 8, 64
TOPK = min(256, SEQ // 4)
CONV2 = 4
GROUPS, PER_GROUP = 4, 8
EXPERTS, EFF = 32, 512
OFF_QATT = 0
OFF_CKV = 1024
OFF_QIDX = OFF_CKV + KV_LAT
OFF_KIDX = OFF_QIDX + IDX_H * IDX_D
OFF_WIDX = OFF_KIDX + IDX_D
OFF_QKV = OFF_WIDX + IDX_H
OFF_AB = OFF_QKV + 3 * 1024
OFF_Z = OFF_AB + 16
OFF_GATE = OFF_Z + 1024
N_IN2 = OFF_GATE + 2048
HG = 4
BLOCKS = 40
BIG = -3e38


def layout(parts):
    at, out = 0, {}
    for name, n in parts:
        out[name] = (at, n)
        at += n
    return out, at


CONSTS, N_CONST = layout([
    ("ident", 128), ("cos", NT * 16), ("sin", NT * 16), ("chunk_mask", 512), ("causal_mask", 512),
    ("upper", 128), ("upper_strict", 128), ("lower", 128), ("ones", 128), ("iota", 128),
    ("token", NT), ("block_start", BLOCKS + 1),
    ("level0", 128), ("level0_t", 128), ("levels_t", 6 * 128)])
COLS, N_COLS = layout([
    ("attn_norm_g", KD), ("ffn_norm_g", KD), ("ple_norm_g", KD), ("q_lat_norm_g", 2),
    ("kv_lat_norm_g", 1), ("kv_norm_g_2", 2), ("c_2", KD), ("conv_b", FT), ("b_ada_2", 48),
    ("conv_w", CONV1 * FT), ("conv_w_2", CONV2 * 24)])
ROWS, N_ROWS = layout([
    ("mla_q_norm_g", QK), ("mla_k_norm_g", QK), ("diff_q_norm_g", 64), ("diff_k_norm_g", 64),
    ("diff_out_norm_g", 128), ("dn_norm_g_2", 128), ("a_log_2", 8), ("dt_bias_2", 8),
    ("lambda_q1", 64), ("lambda_k1", 64), ("lambda_q2", 64), ("lambda_k2", 64)])


def shape_constants():
    c = np.zeros((P, N_CONST), np.float32)

    def put(name, v):
        a, n = CONSTS[name]
        c[:, a:a + n] = np.asarray(v, np.float32).reshape(P, n)

    i, j = np.arange(P)[:, None], np.arange(P)[None, :]
    put("ident", i == j)
    freq = (np.float32(10000.0) ** (-np.arange(16, dtype=np.float32) / np.float32(16))).astype(np.float32)
    ang = np.arange(SEQ, dtype=np.float32)[:, None] * freq
    put("cos", np.cos(ang).reshape(NT, P, 16).transpose(1, 0, 2))
    put("sin", np.sin(ang).reshape(NT, P, 16).transpose(1, 0, 2))
    diag = np.zeros((P, 512), np.float32)
    diag[:, 384:] = np.where(j // CHUNK <= i // CHUNK, 0.0, NEG)
    put("chunk_mask", diag)
    diag[:, 384:] = np.where(j <= i, 0.0, NEG)
    put("causal_mask", diag)
    put("upper", i <= j)
    put("upper_strict", i < j)
    put("lower", i >= j)
    put("ones", np.ones((P, P)))
    put("iota", np.broadcast_to(j, (P, P)))
    put("token", i + P * np.arange(NT)[None, :])
    put("block_start", np.broadcast_to(P * np.arange(BLOCKS + 1)[None, :], (P, BLOCKS + 1)))

    def level(n):
        b = 1 << n
        return (i // (2 * b) == j // (2 * b)) & ((i // b) % 2 == 1) & ((j // b) % 2 == 0)
    put("level0", level(0))
    put("level0_t", level(0).T)
    put("levels_t", np.concatenate([level(n).T for n in range(1, 7)], axis=1))
    rel = np.arange(640) - 511
    half, exact = BUCKETS // 2, BUCKETS // 4
    n = np.abs(rel)
    big = exact + (np.log(np.maximum(n, 1).astype(np.float32) / np.float32(exact))
                   / np.float32(math.log(MAX_DISTANCE / exact)) * np.float32(half - exact)).astype(np.int32)
    bucket = (rel > 0) * half + np.where(n < exact, n, np.minimum(big, half - 1))
    one_hot = (bucket[None, :] == np.arange(BUCKETS)[:, None]).astype(np.float32)
    return c, one_hot


def build(nc, t, out):
    SC1 = [nc.dram_tensor("relative_bias_lines", (P, DIFF_H, 640), F32, kind="Internal").ap(),
           nc.dram_tensor("x_rows", (SEQ, D), F32, kind="Internal").ap(),
           nc.dram_tensor("expert_rows", (BLOCKS * P, D), F32, kind="Internal").ap()]
    bias_line, x_rows, y_rows = SC1

    with ExitStack() as ctx:
        def sem(name):
            return ctx.enter_context(nc.semaphore(name))

        FREE_FLOATS = 53100
        mem = ctx.enter_context(nc.sbuf_tensor("mem", [P, FREE_FLOATS], F32))
        top = [0]

        def place(at, *dims):
            n = int(np.prod(dims))
            assert at + n <= FREE_FLOATS, (at, dims)
            v = mem[:, at:at + n]
            if len(dims) == 2:
                v = v.rearrange("p (a b) -> p a b", a=dims[0])
            if len(dims) == 3:
                v = v.rearrange("p (a b c) -> p a b c", a=dims[0], b=dims[1])
            return v

        def keep(*dims):
            at = top[0]
            top[0] += int(np.prod(dims))
            return place(at, *dims)

        cst = keep(N_CONST)
        col = keep(384)
        row = keep(N_ROWS)
        gate_rows = keep(2, D)
        mod = keep(4, KD)
        small = keep(640)
        x = keep(NT, D)
        work = top[0]

        def const(name, *dims):
            a, n = CONSTS[name]
            v = cst[:, a:a + n]
            return v.rearrange("p (a b) -> p a b", a=dims[0]) if dims else v

        def column(name, k=None):
            a, n = COLS[name]
            return col[:, a:a + n] if k is None else col[:, a + k:a + k + 1]

        def rows(name):
            a, n = ROWS[name]
            return row[:, a:a + n]

        ident = const("ident")
        cut = Counter()

        def tiny(n):
            a = cut["tiny"]
            cut["tiny"] += n
            assert cut["tiny"] <= 640
            return small[:, a:a + n]
        stat = tiny(8)
        stat8 = tiny(16)
        neg_max = tiny(8)
        row_sum = tiny(8)
        lam = tiny(4)
        cond = tiny(KD)
        eps_col = tiny(1)
        beta = tiny(NT * 8).rearrange("p (a b) -> p a b", a=NT)
        gdec = tiny(NT * 8).rearrange("p (a b) -> p a b", a=NT)
        gsum = tiny(NT * 8).rearrange("p (a b) -> p a b", a=NT)
        eg = tiny(NT * 8).rearrange("p (a b) -> p a b", a=NT)
        beg = tiny(NT * 8).rearrange("p (a b) -> p a b", a=NT)
        a_neg = tiny(8)
        tail = tiny(HG)
        g_last = tiny(HG)
        top8 = tiny(8)
        w_idx = tiny(NT * 8).rearrange("p (a b) -> p a b", a=NT)

        SLOT, SLOTS = 4096, 3
        ring = work
        hT = place(ring + SLOTS * SLOT, KD, SEQ)
        A0 = ring + (SLOTS + 1) * SLOT

        def areas(parts):
            at, o = A0, {}
            for name, dims in parts:
                o[name] = place(at, *dims)
                at += int(np.prod(dims))
            assert at <= FREE_FLOATS, (at, FREE_FLOATS)
            return o

        S1 = areas([("lat", (NT, LAT)), ("dq", (NT, 512)), ("dk", (NT, 512)), ("dv", (NT, 512)),
                    ("kT", (MLA_H, SEQ)), ("v", (NT, 512)), ("yT", (KD, SEQ)),
                    ("pT", (2, NT, SEQ)), ("s", (4, SEQ))])
        pT_at = A0 + NT * LAT + 3 * 2048 + 4096 + 2048 + 4096
        heads = place(pT_at, 2, 768)
        square = place(pT_at + 1536, 1024)
        latT = place(pT_at + 2560, 3, SEQ)
        rope_t = S1["s"][:, 0, :].rearrange("p (a b c) -> p a b c", a=4, b=8)
        xn = S1["pT"].rearrange("p a b c -> p (a b c)")[:, 0:2 * D].rearrange("p (a b) -> p a b", a=2)
        bias_t = None
        diff_bias = S1["kT"].rearrange("p a b -> p (a b)")[:, 0:4 * 512].rearrange("p (a b) -> p a b", a=4)
        diff_o = S1["v"]
        staging = place(ring + SLOTS * SLOT, 3, P)
        cond_b = place(ring + SLOTS * SLOT + 512, KD, P)
        one_hot = place(ring + SLOTS * SLOT + 512 + 1024, 640)
        rel_table = place(ring + SLOTS * SLOT + 512 + 1024 + 640, 4)
        rel_wide = place(ring + SLOTS * SLOT + 512 + 1024 + 1280, 4, P)
        bias_head = S1["yT"].rearrange("p a b -> p (a b)")[:, 0:4 * 640].rearrange("p (a b) -> p a b", a=4)
        S2 = areas([("act", (FT, SEQ)), ("gpad", (2, SEQ + 4)), ("conv", (2, SEQ)),
                    ("sig", (2, SEQ)), ("tmp", (SEQ,)), ("p", (NT, PLE)), ("pleT", (2, SEQ)), ("xn", (2, D))])
        S3 = areas([("qT", (8, SEQ)), ("q_idx", (4, SEQ)), ("k_idx", (SEQ,)), ("small", (NT, 344)),
                    ("kvT", (2, SEQ)), ("kT", (8, SEQ)), ("v", (NT, D)), ("sel", (3, SEQ)),
                    ("score", (SEQ,)), ("s", (3, SEQ)), ("pT", (1, NT, SEQ))])
        S4 = areas([("yT", (8, SEQ)), ("dnT", (8, SEQ)), ("q", (HG, SEQ)), ("k", (HG, SEQ)), ("v", (HG, SEQ)),
                    ("z", (NT, HG * DH))]
                   + [(n, (HG, P)) for n in ("tmp", "decay", "A", "AT", "qk", "qkT", "k_tail", "k_bg", "v_b",
                                             "X", "XT", "L0", "L1", "u", "wT", "state")]
                   + [("gpad", (2, SEQ + 4))])
        S5 = areas([("yT", (8, SEQ)), ("dnT", (8, SEQ)), ("sig", (4, SEQ)), ("mg", (8, SEQ)), ("tmp", (SEQ,)),
                    ("ln", (4, D)), ("sq", (D,))])

        wg_s = [place(work + n * SLOT, KD, EFF) for n in range(2)]
        wu_s = [place(work + (2 + n) * SLOT, KD, EFF) for n in range(2)]
        wd_s = [place(work + (4 + n) * SLOT, EFF // P, D) for n in range(2)]
        M0 = work + 6 * SLOT
        at = [M0]

        def moe(*dims):
            a = at[0]
            at[0] += int(np.prod(dims))
            return place(a, *dims)
        xg = moe(2, D)
        xgT = moe(2, KD, P)
        hb = moe(2, EFF)
        hbT = moe(2, EFF // P, P)
        yb = moe(2, D)
        yg = moe(2, D)
        ln_rows = moe(4, D)
        logit = moe(NT, 36)
        g_hot, e_in, e_tmp = moe(NT, 4), moe(NT, 8), moe(NT, 8)
        hot = [moe(NT, 8), moe(NT, 8)]
        choice = [moe(NT, 32), moe(NT, 32)]
        both, rank, wide = moe(NT, 32), moe(NT, 32), moe(NT, 32)
        nb, b_end, b_at = moe(32), moe(32), moe(32)
        dest = [moe(NT), moe(NT)]
        gate_of = [moe(NT), moe(NT)]
        r_m1, r_m2, r_t = moe(NT), moe(NT), moe(NT)
        ge, in_block, slot_hot = moe(BLOCKS + 1), moe(BLOCKS), moe(P)
        ebw = moe(BLOCKS, 32)
        eb_f = moe(BLOCKS)
        rev = moe(8)
        w_route = moe(KD, 36)
        ints = ctx.enter_context(nc.sbuf_tensor("ints", [P, 2 * BLOCKS + 2 * NT], I32))
        slot_token = ints[:, 0:BLOCKS]
        block_expert = ints[:, BLOCKS:2 * BLOCKS]
        dest_i = [ints[:, 2 * BLOCKS + j * NT:2 * BLOCKS + (j + 1) * NT] for j in range(2)]
        sq2 = yg[:, 1, :]

        banks = [ctx.enter_context(nc.psum_tensor(f"bank{i}", [P, 512], F32)) for i in range(8)]
        dve_full, dve_free = sem("dve_ring_full"), sem("dve_ring_free")
        act_full, act_free = sem("act_ring_full"), sem("act_ring_free")

        loaded = sem("inputs_loaded")
        x_loaded = sem("x_loaded")
        p_loaded = sem("p_loaded")
        ln_loaded = sem("ln_rows_loaded")
        ln2_loaded = sem("ln_rows_2_loaded")
        route_loaded = sem("route_weights_loaded")
        w_full = [sem(f"weights_in_slot{i}") for i in range(SLOTS)]
        w_free = sem("weights_used_early")
        dve_step, act_step, pool_step = sem("dve_step"), sem("act_step"), sem("pool_step")
        var_ready, std_ready = sem("variance_ready"), sem("deviation_ready")
        tp_ready = sem("rows_to_transpose_ready")
        s_ready, e_ready, p_ready = sem("scores_masked"), sem("scores_exp"), sem("probabilities_ready")
        silu_in, silu_out = sem("conv_ready"), sem("silu_ready")
        sig_out, sig_used = sem("gates_ready"), sem("gates_used")
        to_act, from_act = sem("dve_to_act"), sem("act_to_dve")
        to_pe = sem("dve_to_pe")
        to_pool, from_pool = sem("dve_to_pool"), sem("pool_to_pe")
        line_out, bias_in = sem("bias_line_written"), sem("bias_loaded")
        x_spilled = sem("x_rows_written")

        items = []

        def w3(ap):
            return ap.rearrange("(k p) n -> p k n", p=P)

        def item(name, *loads):
            items.append((name, loads))

        def slot_view(n, k, width, extra=0):
            return place(ring + (n % SLOTS) * SLOT + extra, k, width)

        def add(name, src, k, width):
            n = len(items)
            item(name, (slot_view(n, k, width), w3(src)))

        W = {k: v[0] if len(v.shape) > 2 or k.startswith("w_") else v for k, v in t.items()}
        for c in range(12):
            add("ada", W["w_ada_2"][:, c * 512:(c + 1) * 512], KD, 512)
        for name, a, b in (("lat", 0, LAT), ("dq", LAT, LAT + 512), ("dk", LAT + 512, LAT + 1024),
                           ("dv", LAT + 1024, LAT + 1536)):
            add(name, W["w_in"][:, a:b], KD, b - a)
        add("uq", W["w_uq"], 2, 768)
        add("ukv", W["w_ukv"], 1, 1024)
        for c in range(2):
            add("out", W["w_out"][:, c * 512:(c + 1) * 512], KD, 512)
        ff_chunks = [(a, min(512, D_FF - a)) for a in range(0, D_FF, 512)]
        for a, n in ff_chunks:
            add("gate", W["w_gate"][:, a:a + n], KD, n)
            add("up", W["w_up"][:, a:a + n], KD, n)
        down_parts = [(0, 8), (8, 8), (16, 6)]
        for c in range(2):
            for k0, nk in down_parts:
                add("down", W["w_down"][k0 * P:(k0 + nk) * P, c * 512:(c + 1) * 512], nk, 512)
        add("ple_proj", W["w_ple_proj"], 2, D)
        for c in range(2):
            add("ple_gate", W["w_ple_gate"][:, c * 512:(c + 1) * 512], KD, 512)
        wi2 = W["w_in_2"]
        n = len(items)
        mixed = slot_view(n, KD, 344)
        item("mixed", (mixed[:, :, 0:256], w3(wi2[:, OFF_CKV:OFF_CKV + 256])),
             (mixed[:, :, 256:328], w3(wi2[:, OFF_KIDX:OFF_KIDX + 72])),
             (mixed[:, :, 328:344], w3(wi2[:, OFF_AB:OFF_AB + 16])))
        add("q_idx", wi2[:, OFF_QIDX:OFF_QIDX + 512], KD, 512)
        for c in range(2):
            add("q_att", wi2[:, c * 512:(c + 1) * 512], KD, 512)
        n = len(items)
        uk_v = slot_view(n, 2, 8 * 128).rearrange("p a (h d) -> p a h d", h=8)
        uv_v = slot_view(n, 2, 8 * 128, 2048).rearrange("p a (h d) -> p a h d", h=8)
        item("ukuv", *[(v[:, a, :, :], W[w][:, a * P:(a + 1) * P, :].rearrange("h p d -> p h d"))
                       for v, w in ((uk_v, "w_uk_2"), (uv_v, "w_uv_2")) for a in range(2)])
        for g in range(2):
            for part in range(3):
                a = OFF_QKV + part * 1024 + g * 512
                add("qkv", wi2[:, a:a + 512], KD, 512)
            add("z", wi2[:, OFF_Z + g * 512:OFF_Z + (g + 1) * 512], KD, 512)
        for c in range(2):
            for name, src in (("gate_a", wi2[:, OFF_GATE + c * 512:OFF_GATE + (c + 1) * 512]),
                              ("br_a", W["w_br_att_2"][:, c * 512:(c + 1) * 512]),
                              ("gate_d", wi2[:, OFF_GATE + D + c * 512:OFF_GATE + D + (c + 1) * 512]),
                              ("br_d", W["w_br_dn_2"][:, c * 512:(c + 1) * 512])):
                add(name, src, KD, 512)
        for c in range(2):
            add("out2", W["w_out_2"][:, c * 512:(c + 1) * 512], KD, 512)
        slot_total, slot_need = Counter(), []
        for n, (_, loads) in enumerate(items):
            slot_total[n % SLOTS] += 16 * len(loads)
            slot_need.append(slot_total[n % SLOTS])
        item_done = []
        mark = {}

        units = [(h, q) for h in range(8) for q in range(NT)]
        diff_units = [(h, q) for h in range(DIFF_H) for q in range(NT)]

        PAIRS = BLOCKS // 2
        xt_full, xt_taken, x_scaled = sem("x_turned"), sem("x_turned_taken"), sem("x_scaled")
        x_gathered = [sem(f"x_gathered{i}") for i in range(2)]
        wg_in, wu_in, wd_in = ([sem(f"{n}{i}") for i in range(2)] for n in ("gate_in", "up_in", "down_in"))
        gate_full, up_full, silu_done, hb_ready = (sem(n) for n in ("gate_full", "up_full", "silu_done", "hidden"))
        ht_full, ht_taken, y_full = sem("hidden_turned"), sem("hidden_turned_taken"), sem("y_full")
        y0_taken, y1_taken = sem("y_left_taken"), sem("y_right_taken")
        y_stored = [sem(f"y_stored{i}") for i in range(2)]
        y_back = [sem(f"y_gathered{i}") for i in range(2)]
        y_used, x_done, out_stored = sem("y_used"), sem("x_done"), sem("out_stored")
        tables_ready, place_used = sem("tables_ready"), sem("placement_used")

        def flat(v):
            return v.rearrange("p a b -> p (a b)")

        def inner_at(v, n):
            return v.to_broadcast([P, v.shape[1], n])

        def spread(name, n, offset=0):
            return bass.AP(tensor=t[name].tensor, offset=offset, ap=[[0, P], [1, n]])
        first_loads = [(cst, t["shape_constants"]), (one_hot[0:BUCKETS, :], t["distance_buckets"]),
                       (rel_table[0:BUCKETS, :], t["rel_bias"])]
        for name, (a, n) in COLS.items():
            k = 0
            src = t[name]
            src = src.rearrange("a b n -> (a b n)") if len(src.shape) == 3 else src.rearrange("a n -> (a n)")
            src = src.rearrange("(r p) -> r p", p=P)
            while k < n:
                g, r = divmod(a + k, P)
                m = min(n - k, P - r)
                first_loads.append((staging[r:r + m, g, :], src[k:k + m, :]))
                k += m
        for name, (a, n) in ROWS.items():
            first_loads.append((rows(name), spread(name, n)))
        for j in range(2):
            first_loads.append((gate_rows[:, j, :], spread("b_ada_2", D, (2 + 3 * j) * D)))
        n_loads = len(first_loads)
        one_hot_free = S1["s"][:, 0, 0:64]

        block = ctx.enter_context(nc.Block())

        @block.tensor
        def _(pe):
            done = Counter()
            nxt = Counter()

            def bank(ring_name):
                n = done[ring_name]
                free = dve_free if ring_name == "dve" else act_free
                if n >= 4:
                    pe.wait_ge(free, n - 3)
                return banks[n % 4 + (0 if ring_name == "dve" else 4)]

            def full(last, ring_name):
                done[ring_name] += 1
                last.then_inc(dve_full if ring_name == "dve" else act_full, 1)

            def taken(ring_name):
                pe.wait_ge(dve_free if ring_name == "dve" else act_free, done[ring_name])

            def weights(name):
                n = nxt["item"]
                assert items[n][0] == name, (items[n][0], name)
                pe.wait_ge(w_full[n % SLOTS], slot_need[n])
                nxt["item"] += 1
                return [v for v, _ in items[n][1]]

            def used(ring_name=None):
                item_done.append((dve_full, done["dve"]) if ring_name == "dve" else (act_full, done["act"]))

            def to_wait(s, n=1):
                nxt[s] += n
                pe.wait_ge(s, nxt[s])

            def product(o, pairs):
                for i, (l, r) in enumerate(pairs):
                    last = pe.matmul(o, l, r, start=(i == 0), stop=(i == len(pairs) - 1))
                return last

            def by_token(ring_name, w, lhs, width, kk=KD, at=0):
                for q in range(NT):
                    b = bank(ring_name)
                    full(product(b[:, 0:width], [(lhs[:, k, q * P:(q + 1) * P], w[:, k, at:at + width])
                                                 for k in range(kk)]), ring_name)

            def by_feature(ring_name, w, rhs, tiles, kk=KD):
                for m in range(tiles):
                    b = bank(ring_name)
                    full(product(b[:, :], [(w[:, k, m * P:(m + 1) * P], rhs[:, k, :]) for k in range(kk)]),
                         ring_name)

            def turn(ring_name, sources, width=P):
                b = bank(ring_name)
                for i, s in enumerate(sources):
                    last = pe.transpose(b[0:width, i * P:(i + 1) * P], s, ident)
                full(last, ring_name)

            def turn_x(from_xn):
                for q in range(NT):
                    if from_xn:
                        to_wait(tp_ready)
                        src = xnb[:, q % 2, :]
                    else:
                        src = x[:, q, :]
                    for hf in range(2):
                        turn("dve", [src[:, (4 * hf + k) * P:(4 * hf + k + 1) * P] for k in range(4)])
                taken("dve")

            pe.wait_ge(loaded, 16 * n_loads)
            for g in range(3):
                n = min(P, N_COLS - g * P)
                b = bank("dve")
                full(pe.transpose(b[:, 0:n], staging[0:n, g, :], ident[0:n, 0:n]), "dve")
            to_wait(to_pe)
            for h in range(DIFF_H):
                for a, n in ((0, 512), (512, 128)):
                    b = bank("dve")
                    full(pe.matmul(b[:, 0:n], rel_wide[0:BUCKETS, h, :], one_hot[0:BUCKETS, a:a + n],
                                   start=True, stop=True), "dve")
            to_wait(to_pe)
            for c in range(12):
                w = weights("ada")[0]
                if c in (4, 5, 10, 11):
                    b = bank("dve")
                    full(product(b[:, :], [(cond_b[:, k, :], w[:, k, :]) for k in range(KD)]), "dve")
                else:
                    b = bank("dve")
                    for m in range(4):
                        last = product(b[:, m:m + 1], [(w[:, k, m * P:(m + 1) * P], cond[:, k:k + 1])
                                                       for k in range(KD)])
                    full(last, "dve")
                used("dve")

            xnb = xn
            turn_x(True)
            for name, width in (("lat", LAT), ("dq", 512), ("dk", 512), ("dv", 512)):
                by_token("act", weights(name)[0], hT, width)
                used("act")
            for q in range(NT):
                if q == 0:
                    to_wait(to_pe)
                turn("dve", [S1["lat"][:, q, k * P:(k + 1) * P] for k in range(3)])
            taken("dve")
            wq = weights("uq")[0]
            wkv = weights("ukv")[0]

            def head_turns(G, width):
                to_wait(tp_ready)
                u = nxt["unit"]
                nxt["unit"] += 1
                src = heads[:, u % 2, 0:G * width].rearrange("p (g d) -> p g d", g=G)
                per = 4
                for a in range(0, G, per):
                    turn("act", [src[:, a + i, :] for i in range(per)], width)
                mark["heads", u] = done["act"]
            for q in range(NT):
                lq = [latT[:, k, q * P:(q + 1) * P] for k in range(3)]
                b = bank("dve")
                full(product(b[:, :], [(lq[k], wq[:, k, 0:512]) for k in range(2)]), "dve")
                b = bank("dve")
                full(product(b[:, 0:256], [(lq[k], wq[:, k, 512:768]) for k in range(2)]), "dve")
                if q == NT - 1:
                    used("dve")
                for a in range(2):
                    b = bank("dve")
                    full(product(b[:, :], [(lq[2], wkv[:, 0, a * 512:(a + 1) * 512])]), "dve")
                if q == NT - 1:
                    used("dve")
                head_turns(8, QK)
                head_turns(8, QK)
            taken("act")

            def attention(name, qT, kT, K, v_of, out_of, pT):
                nbuf = pT.shape[1]

                def scores(n):
                    h, q = units[n]
                    b = bank("dve")
                    full(product(b[:, 0:(q + 1) * P], [(qT[0:K, h, q * P:(q + 1) * P],
                                                        kT[0:K, h, 0:(q + 1) * P])]), "dve")

                def turns(n):
                    h, q = units[n]
                    to_wait(p_ready)
                    src = sbuf[:, n % 3, :]
                    turn("act", [src[:, k * P:(k + 1) * P] for k in range(q + 1)])
                    mark[name, "T", n] = done["act"]

                def values(h):
                    b = bank("dve")
                    pe.wait_ge(act_free, mark[name, "T", 4 * h + 3])
                    o = out_of(b, h)
                    for k in range(NT):
                        last = pe.matmul(o[:, k * P:SEQ], v_of(k, h), pT[:, h % nbuf, k, k * P:SEQ],
                                         start=(k == 0), stop=(k == NT - 1))
                    full(last, "dve")
                    mark[name, "PV", h] = done["dve"]

                sbuf = (S1 if name == "mla" else S3)["s"]
                N = len(units)
                scores(0)
                scores(1)
                for n in range(N + 1):
                    if n + 2 < N:
                        scores(n + 2)
                    if n < N:
                        turns(n)
                    if n >= 1 and units[n - 1][1] == NT - 1:
                        values(units[n - 1][0])
                taken("dve")

            attention("mla", hT, S1["kT"], QK,
                      lambda k, h: S1["v"][:, k, h * 64:(h + 1) * 64],
                      lambda b, h: b[64 * (h % 2):64 * (h % 2) + 64, :], S1["pT"])

            for q in range(NT):
                head_turns2 = head_turns
                for _ in range(2):
                    to_wait(tp_ready)
                    u = nxt["unit"]
                    nxt["unit"] += 1
                    turn("act", [heads[:, u % 2, a * P:(a + 1) * P] for a in range(4)])
                    mark["heads", u] = done["act"]
            taken("act")

            def diff_scores(n):
                h, q = diff_units[n]
                for m in range(2):
                    b = bank("dve")
                    full(product(b[:, 0:(q + 1) * P], [(hT[64 * m:64 * m + 64, h, q * P:(q + 1) * P],
                                                        hT[64 * m:64 * m + 64, 4 + h, 0:(q + 1) * P])]), "dve")

            def diff_turns(n):
                h, q = diff_units[n]
                to_wait(p_ready)
                turn("act", [S1["s"][:, 2 * (n % 2), k * P:(k + 1) * P] for k in range(q + 1)])
                mark["diff", "T", n] = done["act"]

            def diff_values(n):
                h, q = diff_units[n]
                b = bank("dve")
                pe.wait_ge(act_free, mark["diff", "T", n])
                full(product(b[:, 0:P], [(S1["pT"][:, n % 2, k, 0:P], S1["dv"][:, k, h * P:(h + 1) * P])
                                         for k in range(q + 1)]), "dve")
                mark["diff", "PV", n] = done["dve"]

            diff_scores(0)
            for n in range(16):
                if n + 1 < 16:
                    diff_scores(n + 1)
                diff_turns(n)
                diff_values(n)
            for q in range(NT):
                to_wait(tp_ready)
                turn("act", [diff_o[:, q, h * P:(h + 1) * P] for h in range(4)])
            taken("act")
            for c in range(2):
                by_token("dve", weights("out")[0], S1["yT"], 512)
                used("dve")
            mark["attention added"] = done["dve"]
            xnb = S2["xn"]
            turn_x(True)
            for a, n in ff_chunks:
                for name in ("gate", "up"):
                    by_feature("dve", weights(name)[0], hT, n // P)
                    used("dve")
            taken("dve")
            for c in range(2):
                open_banks = []
                for i, (k0, nk) in enumerate(down_parts):
                    w = weights("down")[0]
                    for q in range(NT):
                        if i == 0:
                            n = done["dve"] + q
                            pe.wait_ge(dve_free, n - 3)
                            open_banks.append(banks[n % 4])
                        for k in range(nk):
                            last = pe.matmul(open_banks[q][:, :], S2["act"][:, k0 + k, q * P:(q + 1) * P],
                                             w[:, k, :], start=(i == 0 and k == 0),
                                             stop=(i == 2 and k == nk - 1))
                        if i == 2:
                            last.then_inc(dve_full, 1)
                    if i < 2:
                        last.then_inc(w_free, 1)
                        nxt["wfree"] += 1
                        item_done.append((w_free, nxt["wfree"]))
                done["dve"] += 4
                used("dve")
            turn_x(True)
            pe.wait_ge(p_loaded, 16)
            for q in range(NT):
                turn("dve", [S2["p"][:, q, k * P:(k + 1) * P] for k in range(2)])
            taken("dve")
            wp = weights("ple_proj")[0]
            item_done.append(None)
            at_item = len(item_done) - 1
            for c in range(2):
                w = weights("ple_gate")[0]
                for q in range(NT):
                    lq = slice(q * P, (q + 1) * P)
                    b = bank("act")
                    full(product(b[:, :], [(hT[:, k, lq], w[:, k, :]) for k in range(KD)]), "act")
                    b = bank("dve")
                    full(product(b[:, :], [(S2["pleT"][:, k, lq], wp[:, k, c * 512:(c + 1) * 512])
                                           for k in range(2)]), "dve")
                used("act")
            item_done[at_item] = (dve_full, done["dve"])
            taken("dve")
            pe.wait_ge(sig_used, 8)
            turn_x(False)
            w = weights("mixed")[0]
            wmix = mixed
            by_token("dve", wmix, hT, 344)
            b = bank("act")
            for hf in range(2):
                for k in range(KD):
                    last = pe.matmul(b[64 * hf:64 * hf + 64, :], wmix[:, k, 256:320], hT[:, k, :],
                                     start=(k == 0), stop=(k == KD - 1))
            full(last, "act")
            used("act")
            by_feature("act", weights("q_idx")[0], hT, 4)
            used("act")
            to_wait(to_pe)
            b = bank("dve")
            for q in range(NT):
                last = pe.matmul(b[:, q * 8:(q + 1) * 8], const("upper"), gdec[:, q, :], start=True, stop=True)
            full(last, "dve")
            for q in range(NT):
                turn("dve", [S3["small"][:, q, k * P:(k + 1) * P] for k in range(2)])
            taken("act")
            for q in (1, 2, 3):
                for h in range(IDX_H):
                    o = slice(64 * (h % 2), 64 * (h % 2) + 64)
                    b = bank("dve")
                    full(product(b[:, 0:(q + 1) * P], [(S3["q_idx"][o, h // 2, q * P:(q + 1) * P],
                                                        S3["k_idx"][o, 0:(q + 1) * P])]), "dve")
            for c in range(2):
                by_feature("act", weights("q_att")[0], hT, 4)
                used("act")
            weights("ukuv")
            for h in range(8):
                b = bank("act")
                full(product(b[:, :], [(uk_v[:, a, h, :], S3["kvT"][:, a, :]) for a in range(2)]), "act")
            for q in range(NT):
                for hf in range(2):
                    b = bank("act")
                    full(product(b[:, :], [(S3["kvT"][:, a, q * P:(q + 1) * P],
                                            uv_v[:, a, 4 * hf:4 * hf + 4, :].rearrange("p h d -> p (h d)"))
                                           for a in range(2)]), "act")
            used("act")
            taken("act")
            attention("dsa", S3["qT"], S3["kT"], P, lambda k, h: S3["v"][:, k, h * P:(h + 1) * P],
                      lambda b, h: b[:, :], S3["pT"])

            for g in range(2):
                for part in range(3):
                    by_feature("dve", weights("qkv")[0], hT, 4)
                    used("dve")
                    if part < 2:
                        for i in range(4):
                            to_wait(to_pe)
                            b = bank("act")
                            full(product(b[:, :], [(const("ones"), flat(S4[("tmp", "decay")[i % 2]]))]), "act")
                by_token("act", weights("z")[0], hT, 512)
                used("act")
                B = S4

                def four(ring_name, lhs, rhs):
                    b = bank(ring_name)
                    for h in range(HG):
                        last = pe.matmul(b[:, h * P:(h + 1) * P], lhs(h), rhs(h), start=True, stop=True)
                    full(last, ring_name)
                pe.wait_ge(silu_out, FT + 12 * (g + 1))
                for ch in range(NT):
                    cs = slice(ch * P, (ch + 1) * P)
                    to_wait(to_pe)
                    four("dve", lambda h: B["tmp"][:, h, :], lambda h: const("upper"))
                    four("dve", lambda h: B["k"][:, h, cs], lambda h: B["k"][:, h, cs])
                    four("dve", lambda h: B["q"][:, h, cs], lambda h: B["k"][:, h, cs])
                    turn("dve", [B["k"][:, h, cs] for h in range(HG)])
                    turn("dve", [B["v"][:, h, cs] for h in range(HG)])
                    to_wait(to_pe)
                    turn("act", [B["A"][:, h, :] for h in range(HG)])
                    mark["AT", g, ch] = done["act"]
                    turn("act", [B["qk"][:, h, :] for h in range(HG)])
                    to_wait(to_pe)
                    for lv in range(6):
                        to_wait(from_pool)
                        four("act", lambda h: B[f"L{lv % 2}"][:, h, :], lambda h: B["X"][:, h, :])
                        mark["T", g, ch, lv] = done["act"]
                        taken("act")
                        if lv < 5:
                            four("dve", lambda h: B["XT"][:, h, :], lambda h: B["qk"][:, h, :])
                        four("dve", lambda h: B["qk"][:, h, :], lambda h: B["XT"][:, h, :])
                        taken("dve")
                    four("act", lambda h: B["XT"][:, h, :], lambda h: B["v_b"][:, h, :])
                    four("act", lambda h: B["k_bg"][:, h, :], lambda h: B["XT"][:, h, :])
                    four("dve", lambda h: B["q"][:, h, cs], lambda h: B["state"][:, h, :])
                    taken("act")
                    four("dve", lambda h: B["wT"][:, h, :], lambda h: B["state"][:, h, :])
                    taken("dve")
                    four("dve", lambda h: B["qkT"][:, h, :], lambda h: B["decay"][:, h, :])
                    four("dve", lambda h: B["k_tail"][:, h, :], lambda h: B["decay"][:, h, :])
                    to_wait(tp_ready)
                    turn("act", [B["A"][:, h, :] for h in range(HG)])
                    mark["dn", g, ch] = done["act"]
            taken("act")
            taken("dve")
            for c in range(2):
                by_feature("act", weights("gate_a")[0], hT, 4)
                used("act")
                by_feature("dve", weights("br_a")[0], S5["yT"], 4)
                mark["branch", 2 * c] = done["dve"]
                used("dve")
                by_feature("act", weights("gate_d")[0], hT, 4)
                used("act")
                by_feature("dve", weights("br_d")[0], S5["dnT"], 4)
                mark["branch", 2 * c + 1] = done["dve"]
                used("dve")
            taken("dve")
            for c in range(2):
                by_token("dve", weights("out2")[0], S5["mg"], 512)
                used("dve")
            taken("dve")
            to_wait(to_pe)
            mark["x normalised"] = nxt[to_pe]
            turn_x(False)
            pe.wait_ge(route_loaded, 32)
            by_token("dve", w_route, hT, 36)
            to_wait(to_pe)
            b = bank("dve")
            for q in range(NT):
                last = product(b[:, q * 32:(q + 1) * 32],
                               [(const("upper_strict") if r == q else const("ones"), both[:, r, :])
                                for r in range(q + 1)])
            full(last, "dve")
            b = bank("dve")
            full(product(b[:, 0:32], [(const("ones"), both[:, r, :]) for r in range(NT)]), "dve")
            b = bank("dve")
            for n in range(2 * NT):
                to_wait(to_pe)
                last = pe.matmul(b[:, 0:BLOCKS], slot_hot, in_block, start=(n == 0), stop=(n == 2 * NT - 1))
                if n < 2 * NT - 1:
                    last.then_inc(place_used, 1)
            full(last, "dve")
            taken("dve")
            taken("act")
            assert nxt["item"] == len(items) == len(item_done)

            def expert_turns(i, s):
                pe.wait_ge(x_gathered[s], (i + 1) * 16)
                for hf in range(2):
                    for k in range(4):
                        last = pe.transpose(banks[hf][:, k * P:(k + 1) * P],
                                            xg[:, s, (4 * hf + k) * P:(4 * hf + k + 1) * P], ident)
                    last.then_inc(xt_full, 1)

            def expert_block(i, s, first=False, last=False):
                n = 2 * i + s
                pe.wait_ge(xt_taken, 2 * n + 2)
                pe.wait_ge(wg_in[s], (i + 1) * 16)
                product(banks[2][:, :], [(xgT[:, s, k, :], wg_s[s][:, k, :]) for k in range(KD)])\
                    .then_inc(gate_full, 1)
                pe.wait_ge(wu_in[s], (i + 1) * 16)
                product(banks[3][:, :], [(xgT[:, s, k, :], wu_s[s][:, k, :]) for k in range(KD)])\
                    .then_inc(up_full, 1)
                if not last:
                    expert_turns(i + s, 1 - s)
                pe.wait_ge(hb_ready, n + 1)
                for k in range(EFF // P):
                    turned = pe.transpose(banks[4][:, k * P:(k + 1) * P], hb[:, s, k * P:(k + 1) * P], ident)
                turned.then_inc(ht_full, 1)
                pe.wait_ge(ht_taken, n + 1)
                pe.wait_ge(wd_in[s], (i + 1) * 16)
                if not (first and s == 0):
                    pe.wait_ge(y0_taken, n)
                product(banks[5][:, :], [(hbT[:, s, k, :], wd_s[s][:, k, 0:512]) for k in range(4)])\
                    .then_inc(y_full, 1)
                if not (first and s == 0):
                    pe.wait_ge(y1_taken, n)
                product(banks[6][:, :], [(hbT[:, s, k, :], wd_s[s][:, k, 512:D]) for k in range(4)])\
                    .then_inc(y_full, 1)

            expert_turns(0, 0)
            for s in range(2):
                expert_block(0, s, first=True)
            with pe.Fori(1, PAIRS - 1) as i:
                for s in range(2):
                    expert_block(i, s)
            for s in range(2):
                expert_block(PAIRS - 1, s, last=(s == 1))

        @block.vector
        def _(dve):
            n_of = Counter()

            def V(ins, signal=None):
                signal = dve_step if signal is None else signal
                ins.then_inc(signal, 1)
                n_of[signal] += 1
                dve.wait_ge(signal, n_of[signal])

            def take():
                n = n_of["taken"]
                n_of["taken"] += 1
                dve.wait_ge(dve_full, n + 1)
                return banks[n % 4]

            def wait_next(s, n=1):
                n_of["w", s] += n
                dve.wait_ge(s, n_of["w", s])

            tt, ts, stt = dve.tensor_tensor, dve.tensor_scalar, dve.scalar_tensor_tensor

            def inner(v, n):
                return v[:, :, None].to_broadcast([P, v.shape[1], n])

            def over(v, g):
                return v[:, None, :].to_broadcast([P, g, v.shape[1]])

            def invert(s):
                wait_next(std_ready)
                V(dve.reciprocal(s, s))

            def scale_var(s, width, eps, signal=None):
                V(ts(s, s, 1.0 / width, eps, ALU.mult, ALU.add), signal)

            def norm_heads(dst, src, G, width, gain, sq, signal=None):
                sq = sq[:, 0:G * width].rearrange("p (g d) -> p g d", g=G)
                V(tt(sq, src, src, ALU.mult))
                V(dve.tensor_reduce(stat8[:, 0:G], sq, AX.X, ALU.add))
                scale_var(stat8[:, 0:G], width, EPS, var_ready)
                invert(stat8[:, 0:G])
                V(tt(dst, src, inner(stat8[:, 0:G], width), ALU.mult))
                V(tt(dst, dst, over(gain, G), ALU.mult), signal)

            def turned_in(q, gain, shift=None):
                for hf in range(2):
                    b = take()
                    o = hT[:, 4 * hf:4 * hf + 4, q * P:(q + 1) * P]
                    b4 = b[:, :].rearrange("p (a b) -> p a b", a=4)
                    if shift is None:
                        V(tt(o, b4, inner(gain[:, 4 * hf:4 * hf + 4], P), ALU.mult), dve_free)
                    else:
                        V(tt(o, b4, inner(gain[:, 4 * hf:4 * hf + 4], P), ALU.mult))
                        V(tt(o, o, inner(shift[:, 4 * hf:4 * hf + 4], P), ALU.add), dve_free)

            def norm_x(buf, sq, gain):
                for q in range(NT):
                    V(dve.tensor_tensor_reduce(sq, x[:, q, :], x[:, q, :], 1.0, 0.0, ALU.mult, ALU.add,
                                               stat[:, q:q + 1]))
                scale_var(stat[:, 0:NT], D, EPS, var_ready)
                invert(stat[:, 0:NT])
                for q in range(NT + 1):
                    if q < NT:
                        V(ts(buf[:, q % 2, :], x[:, q, :], stat[:, q:q + 1], None, ALU.mult), tp_ready)
                    if q >= 1:
                        turned_in(q - 1, gain)

            dve.wait_ge(loaded, 16 * n_loads)
            V(dve.memset(eps_col, EPS))
            for j in range(2):
                V(dve.tensor_tensor_reduce(one_hot_free, rows(f"lambda_q{j + 1}"), rows(f"lambda_k{j + 1}"),
                                           1.0, 0.0, ALU.mult, ALU.add, lam[:, j:j + 1]))
            V(ts(rows("diff_out_norm_g"), rows("diff_out_norm_g"), 1.0 - LAM_INIT, None, ALU.mult), to_act)
            for g in range(3):
                n = min(P, N_COLS - g * P)
                V(dve.tensor_copy(col[:, g * P:g * P + n], take()[:, 0:n]), dve_free)
            V(dve.tensor_copy(rel_wide[0:BUCKETS, :, :],
                              rel_table[0:BUCKETS, :, None].to_broadcast([BUCKETS, DIFF_H, P])), to_pe)
            for h in range(DIFF_H):
                for a, n in ((0, 512), (512, 128)):
                    V(dve.tensor_copy(bias_head[:, h, a:a + n], take()[:, 0:n]), dve_free)
            wait_next(from_act)
            V(dve.tensor_copy(cond_b, inner(cond, P)), to_pe)
            V(ts(a_neg, a_neg, -1.0, None, ALU.mult))
            V(tt(lam[:, 2:3], lam[:, 0:1], lam[:, 1:2], ALU.subtract))
            V(ts(lam[:, 2:3], lam[:, 2:3], LAM_INIT, None, ALU.add))
            for c in range(12):
                b = take()
                if c in (4, 5, 10, 11):
                    o = gate_rows[:, c // 10, (c % 2) * 512:(c % 2) * 512 + 512]
                    V(stt(o, b[:, :], 1.0, o, ALU.add, ALU.add), dve_free)
                else:
                    j = {0: 0, 1: 1, 3: 2, 4: 3}[c // 2]
                    V(stt(mod[:, j, (c % 2) * 4:(c % 2) * 4 + 4], b[:, 0:4], float(j % 2),
                          column("b_ada_2")[:, 4 * c:4 * c + 4], ALU.add, ALU.add), dve_free)
            dve.wait_ge(x_loaded, 16)
            dve.wait_ge(line_out, 16)
            norm_x(xn, flat(S1["yT"])[:, 3 * D:4 * D], column("attn_norm_g"))
            lat = S1["lat"]
            dve.wait_ge(act_free, 4)
            for a, w, o in ((0, Q_RANK, 0), (Q_RANK, KV_RANK, 4)):
                sq = square[:, 0:NT * w].rearrange("p (g d) -> p g d", g=NT)
                V(tt(sq, lat[:, :, a:a + w], lat[:, :, a:a + w], ALU.mult))
                V(dve.tensor_reduce(stat8[:, o:o + 4], sq, AX.X, ALU.add))
                scale_var(stat8[:, o:o + 4], w, EPS, var_ready if o else None)
            invert(stat8[:, 0:8])
            V(tt(lat[:, :, 0:Q_RANK], lat[:, :, 0:Q_RANK], inner(stat8[:, 0:4], Q_RANK), ALU.mult))
            V(tt(lat[:, :, Q_RANK:384], lat[:, :, Q_RANK:384], inner(stat8[:, 4:8], KV_RANK), ALU.mult), to_pe)
            a = COLS["q_lat_norm_g"][0]
            for q in range(NT):
                b = take()
                V(tt(latT[:, :, q * P:(q + 1) * P], b[:, 0:384].rearrange("p (a b) -> p a b", a=3),
                     inner(col[:, a:a + 3], P), ALU.mult), dve_free)

            def rope(v, q, signal):
                c = over(const("cos", NT)[:, q, :], 8)
                s = over(const("sin", NT)[:, q, :], 8)
                t1, t2 = v[:, :, 64:80], v[:, :, 80:96]
                r = [rope_t[:, i, :, :] for i in range(4)]
                V(tt(r[0], t1, c, ALU.mult))
                V(tt(r[1], t2, s, ALU.mult))
                V(tt(r[2], t2, c, ALU.mult))
                V(tt(r[3], t1, s, ALU.mult))
                V(tt(t1, r[0], r[1], ALU.subtract))
                V(tt(t2, r[2], r[3], ALU.add), signal)

            def heads_free(u):
                if u >= 2 and ("heads", u - 2) in mark:
                    dve.wait_ge(act_full, mark["heads", u - 2])

            for q in range(NT):
                u = 2 * q
                heads_free(u)
                v = heads[:, 0, :]
                V(dve.tensor_copy(v[:, 0:512], take()[:, :]), dve_free)
                V(dve.tensor_copy(v[:, 512:768], take()[:, 0:256]), dve_free)
                v = v.rearrange("p (g d) -> p g d", g=8)
                norm_heads(v, v, 8, QK, rows("mla_q_norm_g"), square)
                rope(v, q, tp_ready)
                heads_free(u + 1)
                v = heads[:, 1, :].rearrange("p (g d) -> p g d", g=8)
                for a in range(2):
                    b4 = take()[:, :].rearrange("p (a b) -> p a b", a=4)
                    V(dve.tensor_copy(v[:, 4 * a:4 * a + 4, 0:64], b4[:, :, 0:64]))
                    V(dve.tensor_copy(S1["v"][:, q, 256 * a:256 * a + 256].rearrange("p (a b) -> p a b", a=4),
                                      b4[:, :, 64:128]), dve_free)
                V(dve.tensor_copy(v[:, :, 64:96], over(lat[:, q, 384:416], 8)))
                norm_heads(v, v, 8, QK, rows("mla_k_norm_g"), square)
                rope(v, q, tp_ready)

            def attention(name, s, scale, bias_of, put):
                def score(n):
                    h, q = units[n]
                    w = (q + 1) * P
                    if n >= 3:
                        dve.wait_ge(act_full, mark[name, "T", n - 3])
                    b = take()
                    V(stt(s[:, n % 3, 0:w], b[:, 0:w], scale, bias_of(q), ALU.mult, ALU.add), dve_free)
                    V(dve.tensor_reduce(neg_max[:, n % 4:n % 4 + 1], s[:, n % 3, 0:w], AX.X, ALU.max))
                    V(ts(neg_max[:, n % 4:n % 4 + 1], neg_max[:, n % 4:n % 4 + 1], -1.0, None, ALU.mult), s_ready)

                def share(n):
                    w = (units[n][1] + 1) * P
                    wait_next(e_ready)
                    r = row_sum[:, n % 4:n % 4 + 1]
                    V(dve.reciprocal(r, r))
                    V(ts(s[:, n % 3, 0:w], s[:, n % 3, 0:w], r, None, ALU.mult), p_ready)

                N = len(units)
                score(0)
                for n in range(N + 1):
                    if n + 1 < N:
                        score(n + 1)
                    if n < N:
                        share(n)
                    if n >= 5 and (n - 5) % 4 == 0:
                        put(take(), (n - 5) // 4)
                put(take(), 7)

            def put_mla(b, h):
                o = slice(64 * (h % 2), 64 * (h % 2) + 64)
                V(dve.tensor_copy(S1["yT"][o, h // 2, :], b[o, :]), dve_free)
            attention("mla", S1["s"], QK ** -0.5, lambda q: const("chunk_mask")[:, 384 - q * P:512], put_mla)

            for q in range(NT):
                for j, (src, g) in enumerate(((S1["dq"], "diff_q_norm_g"), (S1["dk"], "diff_k_norm_g"))):
                    u = 8 + 2 * q + j
                    heads_free(u)
                    norm_heads(heads[:, j, 0:512].rearrange("p (g d) -> p g d", g=8),
                               src[:, q, :].rearrange("p (g d) -> p g d", g=8), 8, 64, rows(g), square, tp_ready)
            dve.wait_ge(bias_in, 16 * DIFF_H)
            V(tt(diff_bias, diff_bias, over(const("chunk_mask"), DIFF_H), ALU.add))
            s = S1["s"]

            def diff_score(n):
                h, q = diff_units[n]
                w = (q + 1) * P
                if n >= 2:
                    dve.wait_ge(act_full, mark["diff", "T", n - 2])
                for m in range(2):
                    j = 2 * (n % 2) + m
                    V(stt(s[:, j, 0:w], take()[:, 0:w], DIFF_QK ** -0.5, diff_bias[:, h, 384 - q * P:512],
                          ALU.mult, ALU.add), dve_free)
                    V(dve.tensor_reduce(neg_max[:, j:j + 1], s[:, j, 0:w], AX.X, ALU.max))
                    V(ts(neg_max[:, j:j + 1], neg_max[:, j:j + 1], -1.0, None, ALU.mult), s_ready)

            diff_score(0)
            for n, (h, q) in enumerate(diff_units):
                if n + 1 < len(diff_units):
                    diff_score(n + 1)
                w, j = (q + 1) * P, 2 * (n % 2)
                wait_next(e_ready, 2)
                V(dve.reciprocal(row_sum[:, j:j + 2], row_sum[:, j:j + 2]))
                V(ts(s[:, j + 1, 0:w], s[:, j + 1, 0:w], row_sum[:, j + 1:j + 2], lam[:, 2:3], ALU.mult, ALU.mult))
                V(stt(s[:, j, 0:w], s[:, j, 0:w], row_sum[:, j:j + 1], s[:, j + 1, 0:w],
                      ALU.mult, ALU.subtract), p_ready)
                V(dve.tensor_copy(diff_o[:, q, h * P:(h + 1) * P], take()[:, 0:P]), dve_free)
            for q in range(NT):
                v = diff_o[:, q, :].rearrange("p (g d) -> p g d", g=4)
                norm_heads(v, v, 4, P, rows("diff_out_norm_g"), square, tp_ready)

            def add_to_x():
                for c in range(2):
                    for q in range(NT):
                        o = x[:, q, c * 512:(c + 1) * 512]
                        V(tt(o, o, take()[:, :], ALU.add), dve_free)
            add_to_x()

            norm_x(S2["xn"], flat(S2["conv"]), column("ffn_norm_g"))

            def conv(b, gp, dst, taps_, w_col, bias, signal):
                V(dve.tensor_copy(gp[:, taps_ - 1:taps_ - 1 + SEQ], b[:, :]), dve_free)
                if bias is None:
                    V(ts(dst, gp[:, 0:SEQ], w_col(0), None, ALU.mult))
                else:
                    V(ts(dst, gp[:, 0:SEQ], w_col(0), bias, ALU.mult, ALU.add))
                for j in range(1, taps_):
                    V(stt(dst, gp[:, j:j + SEQ], w_col(j), dst, ALU.mult, ALU.add),
                      signal if j == taps_ - 1 else None)

            V(dve.memset(S2["gpad"][:, :, 0:CONV1 - 1], 0.0))
            for a, n in ff_chunks:
                ms = range(a // P, (a + n) // P)
                for m in ms:
                    if m >= 2:
                        dve.wait_ge(silu_out, m - 1)
                    conv(take(), S2["gpad"][:, m % 2, :], S2["conv"][:, m % 2, :], CONV1,
                         lambda j: column("conv_w", j * FT + m), column("conv_b", m), silu_in)
                for m in ms:
                    dve.wait_ge(silu_out, m + 1)
                    V(tt(S2["act"][:, m, :], take()[:, :], S2["act"][:, m, :], ALU.mult), dve_free)
            add_to_x()
            norm_x(S2["xn"], flat(S2["conv"]), column("ple_norm_g"))
            for q in range(NT):
                b = take()
                V(dve.tensor_copy(S2["pleT"][:, :, q * P:(q + 1) * P],
                                  b[:, 0:256].rearrange("p (a b) -> p a b", a=2)), dve_free)
            for i in range(8):
                c, q = divmod(i, NT)
                b = take()
                wait_next(sig_out)
                V(tt(S2["tmp"], b[:, :], S2["sig"][:, i % 2, :], ALU.mult), dve_free)
                o = x[:, q, c * 512:(c + 1) * 512]
                V(tt(o, o, S2["tmp"], ALU.add), sig_used)

            for q in range(NT):
                turned_in(q, mod[:, 1, :], mod[:, 0, :])
            sm = S3["small"]
            for q in range(NT):
                V(dve.tensor_copy(sm[:, q, :], take()[:, 0:344]), dve_free)
            sq = S3["v"][:, 0, :].rearrange("p (g d) -> p g d", g=NT)
            V(tt(sq, sm[:, :, 0:256], sm[:, :, 0:256], ALU.mult))
            V(dve.tensor_reduce(stat[:, 0:NT], sq, AX.X, ALU.add))
            scale_var(stat[:, 0:NT], KV_LAT, EPS, var_ready)
            invert(stat[:, 0:NT])
            V(tt(sm[:, :, 0:256], sm[:, :, 0:256], inner(stat[:, 0:NT], 256), ALU.mult))
            V(ts(w_idx, sm[:, :, 320:328], (IDX_H ** -0.5) * (IDX_D ** -0.5), None, ALU.mult))
            u, au = sm[:, :, 256:264], sm[:, :, 264:272]
            V(tt(u, sm[:, :, 328:336], over(rows("dt_bias_2"), NT), ALU.add))
            V(ts(au, u, -1.0, None, ALU.mult))
            V(tt(au, au, u, ALU.max), to_act)
            wait_next(from_act)
            V(stt(gdec, u, 0.0, au, ALU.max, ALU.add))
            V(tt(gdec, gdec, over(a_neg, NT), ALU.mult), to_pe)
            V(dve.tensor_copy(gsum.rearrange("p a b -> p (a b)"), take()[:, 0:32]), dve_free)
            V(ts(eg, gsum, 1.0, None, ALU.mult), to_act)
            wait_next(from_act)
            V(tt(beg, beta, eg, ALU.mult))
            for q in range(NT):
                b = take()
                V(tt(S3["kvT"][:, :, q * P:(q + 1) * P], b[:, 0:256].rearrange("p (a b) -> p a b", a=2),
                     inner(column("kv_norm_g_2"), P), ALU.mult), dve_free)
            for q in (1, 2, 3):
                w = (q + 1) * P
                sc, tm = S3["score"][:, 0:w], S3["s"][:, 0, 0:w]
                for h in range(IDX_H):
                    V(ts(sc if h == 0 else tm, take()[:, 0:w], 0.0, w_idx[:, q, h:h + 1], ALU.max, ALU.mult),
                      dve_free)
                    if h:
                        V(tt(sc, sc, tm, ALU.add))
                V(tt(sc, sc, const("causal_mask")[:, 384 - q * P:512], ALU.add))
                for _ in range(TOPK // 8):
                    V(dve.max(top8, sc))
                    V(dve.match_replace(sc, top8, sc, BIG))
                V(ts(S3["sel"][:, q - 1, 0:w], sc, BIG / 2, NEG, ALU.is_gt, ALU.mult))

            def put_dsa(b, h):
                V(dve.tensor_copy(S3["qT"][:, h, :], b[:, :]), dve_free)
            attention("dsa", S3["s"], DH ** -0.5,
                      lambda q: const("causal_mask")[:, 384 - q * P:512] if q == 0
                      else S3["sel"][:, q - 1, 0:(q + 1) * P], put_dsa)

            B = S4
            for g in range(2):
                gh = slice(g * HG, g * HG + HG)
                V(dve.memset(B["gpad"][:, :, 0:CONV2 - 1], 0.0))
                for part, name in enumerate("qkv"):
                    for i in range(4):
                        m = part * 8 + g * 4 + i
                        conv(take(), B["gpad"][:, i % 2, :], B[name][:, i, :], CONV2,
                             lambda j: column("conv_w_2", j * 24 + m), None, silu_in)
                    if part == 2:
                        break
                    for i in range(4):
                        dve.wait_ge(silu_out, FT + 12 * g + 4 * part + i + 1)
                        sq = flat(B[("tmp", "decay")[i % 2]])
                        V(tt(sq, B[name][:, i, :], B[name][:, i, :], ALU.mult), to_pe)
                        wait_next(from_act)
                        V(dve.reciprocal(sq, sq))
                        V(stt(B[name][:, i, :], B[name][:, i, :], DH ** -0.5 if part == 0 else 1.0, sq,
                              ALU.mult, ALU.mult))
                for ch in range(NT):
                    if ch == 0:
                        V(dve.memset(B["state"], 0.0))
                    V(dve.tensor_copy(B["tmp"], inner(gdec[:, ch, gh], P)), to_pe)
                    b = take()[:, :].rearrange("p (a b) -> p a b", a=HG)
                    V(tt(B["decay"], inner(gsum[:, ch, gh], P), b, ALU.subtract))
                    V(dve.tensor_copy(g_last, b[:, :, P - 1]), dve_free)
                    V(tt(tail, g_last, gsum[:, ch, gh], ALU.subtract))
                    V(ts(B["decay"], B["decay"], 0.0, None, ALU.min), to_act)
                    wait_next(from_act)
                    V(tt(B["decay"], B["decay"], over(const("lower"), HG), ALU.mult))
                    b = take()[:, :].rearrange("p (a b) -> p a b", a=HG)
                    V(tt(B["A"], b, B["decay"], ALU.mult), dve_free)
                    b = take()[:, :].rearrange("p (a b) -> p a b", a=HG)
                    V(tt(B["qk"], b, B["decay"], ALU.mult), dve_free)
                    V(tt(B["A"], B["A"], inner(beta[:, ch, gh], P), ALU.mult), to_pe)
                    b = take()[:, :].rearrange("p (a b) -> p a b", a=HG)
                    V(tt(B["k_tail"], b, inner(tail, P), ALU.mult))
                    V(tt(B["k_bg"], b, inner(beg[:, ch, gh], P), ALU.mult), dve_free)
                    b = take()[:, :].rearrange("p (a b) -> p a b", a=HG)
                    V(tt(B["v_b"], b, inner(beta[:, ch, gh], P), ALU.mult), dve_free)
                    V(tt(B["X"], B["A"], over(const("level0"), HG), ALU.mult))
                    V(tt(B["X"], over(ident, HG), B["X"], ALU.subtract))
                    dve.wait_ge(act_free, mark["AT", g, ch])
                    V(tt(B["XT"], B["AT"], over(const("level0_t"), HG), ALU.mult))
                    V(tt(B["XT"], over(ident, HG), B["XT"], ALU.subtract), to_pe)
                    for lv in range(6):
                        if lv < 5:
                            b = take()[:, :].rearrange("p (a b) -> p a b", a=HG)
                            V(tt(B["X"], B["X"], b, ALU.subtract), dve_free)
                        b = take()[:, :].rearrange("p (a b) -> p a b", a=HG)
                        V(tt(B["XT"], B["XT"], b, ALU.subtract), dve_free)
                    b = take()[:, :].rearrange("p (a b) -> p a b", a=HG)
                    V(tt(B["A"], b, inner(eg[:, ch, gh], P), ALU.mult), dve_free)
                    b = take()[:, :].rearrange("p (a b) -> p a b", a=HG)
                    V(tt(B["decay"], B["u"], b, ALU.subtract), dve_free)
                    b = take()[:, :].rearrange("p (a b) -> p a b", a=HG)
                    V(tt(B["A"], B["A"], b, ALU.add), dve_free)
                    b = take()[:, :].rearrange("p (a b) -> p a b", a=HG)
                    V(tt(B["state"], B["state"], inner(g_last, P), ALU.mult))
                    V(tt(B["state"], B["state"], b, ALU.add), dve_free)
                    norm_heads(B["A"], B["A"], HG, P, rows("dn_norm_g_2"), flat(B["tmp"]))
                    V(tt(B["A"], B["A"], B["z"][:, ch, :].rearrange("p (a b) -> p a b", a=HG), ALU.mult),
                      tp_ready)
            for c in range(2):
                for part in range(2):
                    for m in range(4):
                        b = take()
                        wait_next(sig_out)
                        o = S5["mg"][:, 4 * c + m, :]
                        if part == 0:
                            V(tt(o, b[:, :], S5["sig"][:, m, :], ALU.mult), dve_free)
                        else:
                            V(tt(S5["tmp"], b[:, :], S5["sig"][:, m, :], ALU.mult))
                            V(tt(o, o, S5["tmp"], ALU.add), dve_free)
            ALPHA = 2.0 ** 0.25
            for c in range(2):
                for q in range(NT):
                    o = x[:, q, c * 512:(c + 1) * 512]
                    V(tt(S5["tmp"], take()[:, :], gate_rows[:, 0, c * 512:(c + 1) * 512], ALU.mult), dve_free)
                    V(stt(o, o, ALPHA, S5["tmp"], ALU.mult, ALU.add))

            def layer_norm(g, b, sq, signal):
                for q in range(NT):
                    V(dve.tensor_reduce(stat[:, q:q + 1], x[:, q, :], AX.X, ALU.add))
                V(ts(stat[:, 0:NT], stat[:, 0:NT], -1.0 / D, None, ALU.mult))
                for q in range(NT):
                    V(ts(x[:, q, :], x[:, q, :], stat[:, q:q + 1], None, ALU.add))
                    V(dve.tensor_tensor_reduce(sq, x[:, q, :], x[:, q, :], 1.0, 0.0, ALU.mult, ALU.add,
                                               stat[:, 4 + q:5 + q]))
                scale_var(stat[:, 4:8], D, LN_EPS, var_ready)
                invert(stat[:, 4:8])
                for q in range(NT):
                    V(stt(x[:, q, :], x[:, q, :], stat[:, 4 + q:5 + q], g, ALU.mult, ALU.mult))
                    V(tt(x[:, q, :], x[:, q, :], b, ALU.add), signal if q == NT - 1 else None)

            dve.wait_ge(ln_loaded, 32)
            layer_norm(S5["ln"][:, 0, :], S5["ln"][:, 1, :], S5["sq"], to_pe)
            for q in range(NT):
                turned_in(q, mod[:, 3, :], mod[:, 2, :])
            for q in range(NT):
                V(dve.tensor_copy(logit[:, q, :], take()[:, 0:36]), dve_free)

            def first_max(hot_, v, m, width):
                V(dve.tensor_reduce(m, v, AX.X, ALU.max))
                V(tt(hot_, v, inner(m, width), ALU.is_equal))
                V(tt(hot_, hot_, over(rev[:, 0:width], NT), ALU.mult))
                V(dve.tensor_reduce(r_t, hot_, AX.X, ALU.max))
                V(tt(hot_, hot_, inner(r_t, width), ALU.is_equal))

            V(ts(rev, const("iota")[:, 0:8], -1.0, 16.0, ALU.mult, ALU.add))
            V(dve.tensor_copy(e_tmp[:, :, 0:4], logit[:, :, 0:4]))
            first_max(g_hot, e_tmp[:, :, 0:4], r_m1, 4)
            V(tt(e_tmp[:, :, 0:4], e_tmp[:, :, 0:4], inner(r_m1, 4), ALU.subtract), to_act)
            wait_next(from_act)
            V(dve.tensor_reduce(r_m1, e_tmp[:, :, 0:4], AX.X, ALU.add))
            V(dve.reciprocal(gate_of[0], r_m1))
            for j in range(GROUPS):
                lg = logit[:, :, 4 + 8 * j:12 + 8 * j]
                hj = inner_at(g_hot[:, :, j:j + 1], 8)
                V(tt(e_tmp if j else e_in, lg, hj, ALU.mult))
                if j:
                    V(tt(e_in, e_in, e_tmp, ALU.add))
            first_max(hot[0], e_in, r_m1, 8)
            V(stt(e_in, hot[0], -1e30, e_in, ALU.mult, ALU.add))
            first_max(hot[1], e_in, r_m2, 8)
            V(tt(r_m2, r_m2, r_m1, ALU.subtract), to_act)
            wait_next(from_act)
            V(ts(r_m1, r_m2, 1.0, None, ALU.add))
            V(dve.reciprocal(r_m1, r_m1))
            V(tt(gate_of[0], gate_of[0], r_m1, ALU.mult))
            V(tt(gate_of[1], gate_of[0], r_m2, ALU.mult))
            for j in range(2):
                for k in range(GROUPS):
                    V(tt(choice[j][:, :, 8 * k:8 * k + 8], hot[j], inner_at(g_hot[:, :, k:k + 1], 8), ALU.mult))
            V(tt(both, choice[0], choice[1], ALU.add), to_pe)
            V(dve.tensor_copy(rank.rearrange("p a b -> p (a b)"), take()[:, 0:P]), dve_free)
            V(dve.tensor_copy(b_at, take()[:, 0:32]), dve_free)
            V(ts(nb, b_at, 0.0, None, ALU.is_gt))
            for k in range(1, NT):
                V(ts(b_end, b_at, float(k * P), None, ALU.is_gt))
                V(tt(nb, nb, b_end, ALU.add))
            V(dve.tensor_tensor_scan(b_end, const("ones")[:, 0:32], nb, 0.0, ALU.mult, ALU.add))
            V(tt(b_at, b_end, nb, ALU.subtract))
            V(ts(b_at, b_at, float(P), None, ALU.mult))
            for j in range(2):
                V(tt(wide, rank, over(b_at, NT), ALU.add))
                V(tt(wide, wide, choice[j], ALU.mult))
                V(dve.tensor_reduce(dest[j], wide, AX.X, ALU.add))
                V(dve.tensor_copy(dest_i[j], dest[j]))
            for n in range(2 * NT):
                j, q = divmod(n, NT)
                if n:
                    dve.wait_ge(place_used, n)
                dq = dest[j][:, q:q + 1]
                V(ts(ge, const("block_start"), dq, None, ALU.is_le))
                V(dve.tensor_reduce(r_t[:, 0:1], ge[:, 1:BLOCKS + 1], AX.X, ALU.add))
                V(tt(in_block, ge[:, 0:BLOCKS], ge[:, 1:BLOCKS + 1], ALU.subtract))
                V(ts(in_block, in_block, const("token")[:, q:q + 1], None, ALU.mult))
                V(stt(r_t[:, 1:2], r_t[:, 0:1], -float(P), dq, ALU.mult, ALU.add))
                V(ts(slot_hot, const("iota"), r_t[:, 1:2], None, ALU.is_equal), to_pe)
            V(tt(ebw, over(b_end, BLOCKS), inner(const("iota")[:, 0:BLOCKS], 32), ALU.is_le))
            V(dve.tensor_reduce(eb_f, ebw, AX.X, ALU.add))
            V(ts(eb_f, eb_f, float(EXPERTS - 1), None, ALU.min))
            V(dve.tensor_copy(block_expert, eb_f))
            V(dve.tensor_copy(slot_token, take()[:, 0:BLOCKS]), dve_free)
            V(dve.memset(eps_col, EPS), tables_ready)

            def x_in(n, s):
                for hf in range(2):
                    dve.wait_ge(xt_full, 2 * n + hf + 1)
                    o = xgT[:, s, 4 * hf:4 * hf + 4, :]
                    b4 = banks[hf][:, :].rearrange("p (a b) -> p a b", a=4)
                    tt(o, b4, inner(mod[:, 3, 4 * hf:4 * hf + 4], P), ALU.mult).then_inc(x_scaled, 1)
                    dve.wait_ge(x_scaled, 2 * n + hf + 1)
                    tt(o, o, inner(mod[:, 2, 4 * hf:4 * hf + 4], P), ALU.add).then_inc(xt_taken, 1)

            def block_out(i, s, first=False, last=False):
                n = 2 * i + s
                dve.wait_ge(silu_done, n + 1)
                dve.wait_ge(up_full, n + 1)
                tt(hb[:, s, :], hb[:, s, :], banks[3][:, :], ALU.mult).then_inc(hb_ready, 1)
                if not last:
                    x_in(n + 1, 1 - s)
                dve.wait_ge(y_full, 2 * n + 1)
                if not first:
                    dve.wait_ge(y_stored[s], 16 * i)
                dve.tensor_copy(yb[:, s, 0:512], banks[5][:, :]).then_inc(y0_taken, 1)

            x_in(0, 0)
            for s in range(2):
                block_out(0, s, first=True)
            with dve.Fori(1, PAIRS - 1) as i:
                for s in range(2):
                    block_out(i, s)
            for s in range(2):
                block_out(PAIRS - 1, s, last=(s == 1))
            for q in range(NT):
                dve.wait_ge(y_back[0], 16 * (q + 1))
                dve.wait_ge(y_back[1], 16 * (q + 1))
                y = yb[:, 0, :]
                V(ts(y, yg[:, 0, :], gate_of[0][:, q:q + 1], None, ALU.mult))
                V(stt(y, yg[:, 1, :], gate_of[1][:, q:q + 1], y, ALU.mult, ALU.add), y_used)
                V(tt(y, y, gate_rows[:, 1, :], ALU.mult))
                V(stt(x[:, q, :], x[:, q, :], ALPHA, y, ALU.mult, ALU.add))
            dve.wait_ge(ln2_loaded, 32)
            layer_norm(ln_rows[:, 0, :], ln_rows[:, 1, :], yb[:, 1, :], x_done)

        @block.scalar
        def _(act):
            n_of = Counter()

            def C(ins, signal=None):
                signal = act_step if signal is None else signal
                ins.then_inc(signal, 1)
                n_of[signal] += 1
                act.wait_ge(signal, n_of[signal])

            def take():
                n = n_of["taken"]
                n_of["taken"] += 1
                act.wait_ge(act_full, n + 1)
                return banks[4 + n % 4]

            def wait_next(s, n=1):
                n_of["w", s] += n
                act.wait_ge(s, n_of["w", s])

            def root(s):
                wait_next(var_ready)
                C(act.activation(s, s, ACT.Sqrt), std_ready)

            def copy_out(dst, src):
                C(act.activation(dst, src, ACT.Copy), act_free)

            act.wait_ge(loaded, 16 * n_loads)
            wait_next(to_act)
            C(act.activation(lam[:, 0:2], lam[:, 0:2], ACT.Exp))
            C(act.activation(a_neg, rows("a_log_2"), ACT.Exp))
            act.wait_ge(dve_free, 3)
            C(act.activation(cond, column("c_2"), ACT.Silu), from_act)
            root(stat[:, 0:NT])
            for name, w in (("lat", LAT), ("dq", 512), ("dk", 512), ("dv", 512)):
                for q in range(NT):
                    copy_out(S1[name][:, q, :], take()[:, 0:w])
            root(stat8[:, 0:8])
            for q in range(NT):
                for dst in (hT, S1["kT"]):
                    root(stat8[:, 0:8])
                    for a in range(2):
                        copy_out(dst[0:QK, 4 * a:4 * a + 4, q * P:(q + 1) * P],
                                 take()[0:QK, :].rearrange("p (a b) -> p a b", a=4))

            def attention(name, s, pT):
                nbuf = pT.shape[1]

                def exp(n):
                    w = (units[n][1] + 1) * P
                    wait_next(s_ready)
                    v = s[:, n % 3, 0:w]
                    C(act.activation(v, v, ACT.Exp, bias=neg_max[:, n % 4:n % 4 + 1],
                                     accum_out=row_sum[:, n % 4:n % 4 + 1]), e_ready)

                def turned(n):
                    h, q = units[n]
                    if h >= nbuf and q == 0:
                        act.wait_ge(dve_full, mark[name, "PV", h - nbuf])
                    copy_out(pT[:, h % nbuf, 0:q + 1, q * P:(q + 1) * P],
                             take()[:, 0:(q + 1) * P].rearrange("p (a b) -> p a b", a=q + 1))
                N = len(units)
                for n in range(N + 1):
                    if n < N:
                        exp(n)
                    if n >= 1:
                        turned(n - 1)

            attention("mla", S1["s"], S1["pT"])
            for q in range(NT):
                for j in range(2):
                    root(stat8[:, 0:8])
                    copy_out(hT[:, 4 * j:4 * j + 4, q * P:(q + 1) * P],
                             take()[:, :].rearrange("p (a b) -> p a b", a=4))
            for n in range(len(diff_units) + 1):
                if n < len(diff_units):
                    w = (diff_units[n][1] + 1) * P
                    for m in range(2):
                        j = 2 * (n % 2) + m
                        wait_next(s_ready)
                        v = S1["s"][:, j, 0:w]
                        C(act.activation(v, v, ACT.Exp, bias=neg_max[:, j:j + 1],
                                         accum_out=row_sum[:, j:j + 1]), e_ready)
                if n >= 1:
                    q = diff_units[n - 1][1]
                    if n >= 3:
                        act.wait_ge(dve_full, mark["diff", "PV", n - 3])
                    copy_out(S1["pT"][:, (n - 1) % 2, 0:q + 1, 0:P],
                             take()[:, 0:(q + 1) * P].rearrange("p (a b) -> p a b", a=q + 1))
            for q in range(NT):
                root(stat8[:, 0:4])
                copy_out(S1["yT"][:, 4:8, q * P:(q + 1) * P], take()[:, :].rearrange("p (a b) -> p a b", a=4))
            root(stat[:, 0:NT])
            for m in range(FT):
                wait_next(silu_in)
                C(act.activation(S2["act"][:, m, :], S2["conv"][:, m % 2, :], ACT.Silu), silu_out)
            root(stat[:, 0:NT])
            for i in range(8):
                if i >= 2:
                    act.wait_ge(sig_used, i - 1)
                C(act.activation(S2["sig"][:, i % 2, :], take()[:, :], ACT.Sigmoid), act_free)
                C(act.activation(stat8[:, 15:16], eps_col, ACT.Copy), sig_out)
            copy_out(S3["k_idx"], take()[:, :])
            for m in range(4):
                copy_out(S3["q_idx"][:, m, :], take()[:, :])
            root(stat[:, 0:NT])
            wait_next(to_act)
            sm = S3["small"]
            C(act.activation(beta, sm[:, :, 336:344], ACT.Sigmoid))
            au = sm[:, :, 264:272]
            C(act.activation(au, au, ACT.Exp, scale=-1.0))
            C(act.activation(au, au, ACT.Ln, bias=const("ones")[:, 0:1]), from_act)
            wait_next(to_act)
            C(act.activation(eg, eg, ACT.Exp), from_act)
            for m in range(8):
                copy_out(S3["qT"][:, m, :], take()[:, :])
            for m in range(8):
                copy_out(S3["kT"][:, m, :], take()[:, :])
            for q in range(NT):
                for hf in range(2):
                    copy_out(S3["v"][:, q, hf * 512:(hf + 1) * 512], take()[:, :])
            attention("dsa", S3["s"], S3["pT"])
            B = S4
            for g in range(2):
                for part, name in enumerate("qkv"):
                    for i in range(4):
                        wait_next(silu_in)
                        C(act.activation(B[name][:, i, :], B[name][:, i, :], ACT.Silu), silu_out)
                    if part < 2:
                        for i in range(4):
                            C(act.activation(flat(B[("tmp", "decay")[i % 2]]), take()[:, :], ACT.Sqrt,
                                             bias=eps_col), act_free)
                            C(act.activation(stat8[:, 15:16], eps_col, ACT.Copy), from_act)
                for q in range(NT):
                    C(act.activation(B["z"][:, q, :], take()[:, :], ACT.Silu), act_free)
                for ch in range(NT):
                    wait_next(to_act)
                    C(act.activation(tail, tail, ACT.Exp))
                    C(act.activation(g_last, g_last, ACT.Exp))
                    C(act.activation(B["decay"], B["decay"], ACT.Exp), from_act)

                    def four_out(dst):
                        copy_out(dst, take()[:, :].rearrange("p (a b) -> p a b", a=HG))
                    four_out(B["AT"])
                    four_out(B["qkT"])
                    for lv in range(6):
                        four_out(B["qk"])
                    four_out(B["u"])
                    four_out(B["wT"])
                    root(stat8[:, 0:HG])
                    four_out(B["dnT"][:, g * HG:(g + 1) * HG, ch * P:(ch + 1) * P])
            for c in range(2):
                for part in range(2):
                    for m in range(4):
                        j = 2 * c + part
                        if j:
                            act.wait_ge(dve_free, mark["branch", j - 1] - 3 + m)
                        C(act.activation(S5["sig"][:, m, :], take()[:, :], ACT.Sigmoid), act_free)
                        C(act.activation(stat8[:, 15:16], eps_col, ACT.Copy), sig_out)
            root(stat[:, 4:8])
            wait_next(to_act)
            C(act.activation(e_tmp[:, :, 0:4], e_tmp[:, :, 0:4], ACT.Exp), from_act)
            wait_next(to_act)
            C(act.activation(r_m2, r_m2, ACT.Exp), from_act)

            def expert_block(i, s, first=False):
                n = 2 * i + s
                act.wait_ge(gate_full, n + 1)
                act.activation(hb[:, s, :], banks[2][:, :], ACT.Silu).then_inc(silu_done, 1)
                act.wait_ge(ht_full, n + 1)
                act.activation(hbT[:, s, :, :].rearrange("p a b -> p (a b)"), banks[4][:, :], ACT.Copy)\
                    .then_inc(ht_taken, 1)
                act.wait_ge(y_full, 2 * n + 2)
                if not first:
                    act.wait_ge(y_stored[s], 16 * i)
                act.activation(yb[:, s, 512:D], banks[6][:, :], ACT.Copy).then_inc(y1_taken, 1)
                act.wait_ge(y0_taken, n + 1)
                act.wait_ge(y1_taken, n + 1)
                act.dma_start(y_rows[bass.ds(n * P, P), :], yb[:, s, :]).then_inc(y_stored[s], 16)

            for s in range(2):
                expert_block(0, s, first=True)
            with act.Fori(1, PAIRS) as i:
                for s in range(2):
                    expert_block(i, s)
            root(stat[:, 4:8])

        @block.gpsimd
        def _(pool):
            n_of = Counter()
            pool.wait_ge(dve_free, 3 + 2 * DIFF_H)
            pool.dma_start(bias_line, bias_head).then_inc(line_out, 16)
            pool.wait_ge(line_out, 16)
            pool.wait_ge(dve_full, mark["mla", "PV", 7])
            for h in range(DIFF_H):
                src = bass.AP(tensor=bias_line.tensor, offset=h * 640 + 127,
                              ap=[[DIFF_H * 640 - 1, P], [1, 512]])
                pool.dma_start(diff_bias[:, h, :], src).then_inc(bias_in, 16)
            pool.wait_ge(dve_free, mark["attention added"])
            pool.dma_start(S2["p"], t["p"][0, 0].rearrange("(q p) n -> p q n", p=P)).then_inc(p_loaded, 16)
            for g in range(2):
                for ch in range(NT):
                    pool.wait_ge(act_free, mark["AT", g, ch])
                    for lv in range(6):
                        if lv >= 2:
                            pool.wait_ge(act_full, mark["T", g, ch, lv - 2])
                        mask = const("levels_t", 6)[:, lv, :][:, None, :].to_broadcast([P, HG, P])
                        pool.tensor_tensor(S4[f"L{lv % 2}"], S4["AT"], mask, ALU.mult).then_inc(from_pool, 1)
            pool.wait_ge(dve_full, mark["branch", 0])
            for j, name in enumerate(("ln_g_2", "ln_b_2")):
                src = bass.AP(tensor=t[name].tensor, offset=0, ap=[[0, P], [1, D]])
                pool.dma_start(S5["ln"][:, j, :], src).then_inc(ln_loaded, 16)
            pool.wait_ge(to_pe, mark["x normalised"])
            pool.dma_start(x_rows.rearrange("(q p) n -> p q n", p=P), x).then_inc(x_spilled, 16)
            pool.dma_start(w_route[:, :, 0:4], w3(W["w_route_grp_2"])).then_inc(route_loaded, 16)
            pool.dma_start(w_route[:, :, 4:36], w3(W["w_route_exp_2"])).then_inc(route_loaded, 16)
            for j, name in enumerate(("ln_g_2", "ln_b_2")):
                src = bass.AP(tensor=t[name].tensor, offset=D, ap=[[0, P], [1, D]])
                pool.dma_start(ln_rows[:, j, :], src).then_inc(ln2_loaded, 16)

            pool.wait_ge(x_spilled, 16)
            pool.wait_ge(tables_ready, 1)
            for n in range(BLOCKS):
                if n >= 2:
                    pool.wait_ge(xt_full, 2 * n - 2)
                pool.indirect_dma_start(out=xg[:, n % 2, :], out_offset=None, in_=x_rows,
                                        in_offset=bass.IndirectOffsetOnAxis(ap=slot_token[:, n:n + 1], axis=0))\
                    .then_inc(x_gathered[n % 2], 16)
            for s in range(2):
                pool.wait_ge(y_stored[s], 16 * PAIRS)
            for q in range(NT):
                if q:
                    pool.wait_ge(y_used, q)
                for j in range(2):
                    pool.indirect_dma_start(out=yg[:, j, :], out_offset=None, in_=y_rows,
                                            in_offset=bass.IndirectOffsetOnAxis(ap=dest_i[j][:, q:q + 1], axis=0))\
                        .then_inc(y_back[j], 16)

        @block.sync
        def _(sp):
            for dst, src in first_loads:
                sp.dma_start(dst, src).then_inc(loaded, 16)
            sp.dma_start(x, t["x"][0].rearrange("(q p) n -> p q n", p=P)).then_inc(x_loaded, 16)
            for n, (_, loads) in enumerate(items):
                if n >= SLOTS:
                    sp.wait_ge(*item_done[n - SLOTS])
                for dst, src in loads:
                    sp.dma_start(dst, src).then_inc(w_full[n % SLOTS], 16)

            def load(i, s, first):
                n = 2 * i + s
                e = sp.value_load(block_expert[0:1, bass.ds(n, 1)], min_val=0, max_val=EXPERTS - 1)
                for dst, w, sem_, used_ in ((wg_s[s], "w_gate_2", wg_in[s], gate_full),
                                            (wu_s[s], "w_up_2", wu_in[s], up_full),
                                            (wd_s[s], "w_down_2", wd_in[s], y_full)):
                    if not first:
                        sp.wait_ge(used_, 2 * n - 2 if w == "w_down_2" else n - 1)
                    src = t[w][0][bass.ds(e, 1), :, :].rearrange("e (k p) n -> p (e k) n", p=P)
                    sp.dma_start(dst, src).then_inc(sem_, 16)
            sp.wait_ge(tables_ready, 1)
            load(0, 0, True)
            load(0, 1, True)
            with sp.Fori(1, PAIRS) as i:
                load(i, 0, False)
                load(i, 1, False)
            sp.wait_ge(x_done, 1)
            sp.dma_start(out.rearrange("a (q p) n -> p (a q) n", p=P), x).then_inc(out_stored, 16)
            sp.wait_ge(out_stored, 16)


_CONST_NAMES = ("shape_constants", "distance_buckets")
_NAMES = [
    "x", "p", "attn_norm_g", "w_in", "q_lat_norm_g", "w_uq", "kv_lat_norm_g", "w_ukv", "mla_q_norm_g",
    "mla_k_norm_g", "diff_q_norm_g", "diff_k_norm_g", "lambda_q1", "lambda_k1", "lambda_q2", "lambda_k2",
    "diff_out_norm_g", "rel_bias", "w_out", "ffn_norm_g", "w_gate", "w_up", "conv_w", "conv_b", "w_down",
    "ple_norm_g", "w_ple_gate", "w_ple_proj", "c_2", "w_ada_2", "b_ada_2", "w_in_2", "kv_norm_g_2",
    "w_uk_2", "w_uv_2", "conv_w_2", "a_log_2", "dt_bias_2", "dn_norm_g_2", "w_br_att_2", "w_br_dn_2",
    "w_out_2", "w_route_grp_2", "w_route_exp_2", "w_gate_2", "w_up_2", "w_down_2", "ln_g_2", "ln_b_2"]


def program(nc, inputs):
    arrays, t = {}, {}
    consts = dict(zip(_CONST_NAMES, shape_constants()))
    for name in (*_CONST_NAMES, *_NAMES):
        a = np.ascontiguousarray(consts[name] if name in consts else inputs[name])
        arrays[f"in_{name}"] = a
        t[name] = nc.dram_tensor(f"in_{name}", a.shape, F32, kind="ExternalInput").ap()
    out = nc.dram_tensor("out", (1, SEQ, D), F32, kind="ExternalOutput").ap()
    build(nc, t, out)
    return arrays


def kernel(**inputs):
    import concourse.bacc as bacc
    from concourse.bass_utils import run_bass_kernel_spmd
    nc = bacc.Bacc("TRN2", target_bir_lowering=False, num_devices=1)
    arrays = program(nc, inputs)
    r = run_bass_kernel_spmd(nc, [arrays], core_ids=[0])
    return r.results[0]["out"]
```

```python
import math
from collections import Counter
from contextlib import ExitStack

import numpy as np

import concourse.bass as bass
from concourse import mybir

ALU = mybir.AluOpType
ACT = mybir.ActivationFunctionType
AX = mybir.AxisListType
F32 = mybir.dt.float32
I32 = mybir.dt.int32

P = 128
SEQ, D = 512, 1024
NT, KD = SEQ // P, D // P
EPS, LN_EPS, NEG = 1e-6, 1e-5, -1e30

Q_RANK, KV_RANK, NOPE, ROPE, MLA_H = 256, 128, 64, 32, 8
QK = NOPE + ROPE
MLA_V = 64
DIFF_H, DIFF_QK, DIFF_V = 4, 64, 128
LAT = Q_RANK + KV_RANK + ROPE
CHUNK, BUCKETS, MAX_DISTANCE = 64, 32, 1024
D_FF, CONV1 = 2816, 3
FT = D_FF // P
PLE = 256
LAM_INIT = 0.8 - 0.6 * math.exp(0.0)

H2, DH = 8, 128
KV_LAT, IDX_H, IDX_D = 256, 8, 64
TOPK = min(256, SEQ // 4)
CONV2 = 4
GROUPS, PER_GROUP = 4, 8
EXPERTS, EFF = 32, 512
OFF_QATT = 0
OFF_CKV = 1024
OFF_QIDX = OFF_CKV + KV_LAT
OFF_KIDX = OFF_QIDX + IDX_H * IDX_D
OFF_WIDX = OFF_KIDX + IDX_D
OFF_QKV = OFF_WIDX + IDX_H
OFF_AB = OFF_QKV + 3 * 1024
OFF_Z = OFF_AB + 16
OFF_GATE = OFF_Z + 1024
N_IN2 = OFF_GATE + 2048
HG = 4
HALVES = ((0, 1), (2, 3))
BLOCKS = 40
PAIRS, ALL_PAIRS = 16, BLOCKS // 2
BIG = -3e38


def layout(parts):
    at, out = 0, {}
    for name, n in parts:
        out[name] = (at, n)
        at += n
    return out, at


CONSTS, N_CONST = layout([
    ("ident", 128), ("cos", NT * 16), ("sin", NT * 16), ("chunk_mask", 512), ("causal_mask", 512),
    ("upper", 128), ("upper_strict", 128), ("lower", 128), ("ones", 128), ("iota", 128),
    ("token", NT), ("block_start", BLOCKS + 1),
    ("level0", 128), ("level0_t", 128), ("levels_t", 6 * 128)])
COLS, N_COLS = layout([
    ("attn_norm_g", KD), ("ffn_norm_g", KD), ("ple_norm_g", KD), ("q_lat_norm_g", 2),
    ("kv_lat_norm_g", 1), ("kv_norm_g_2", 2), ("c_2", KD), ("conv_b", FT), ("b_ada_2", 48),
    ("conv_w", CONV1 * FT), ("conv_w_2", CONV2 * 24)])
ROWS, N_ROWS = layout([
    ("mla_q_norm_g", QK), ("mla_k_norm_g", QK), ("diff_q_norm_g", 64), ("diff_k_norm_g", 64),
    ("diff_out_norm_g", 128), ("dn_norm_g_2", 128), ("a_log_2", 8), ("dt_bias_2", 8),
    ("lambda_q1", 64), ("lambda_k1", 64), ("lambda_q2", 64), ("lambda_k2", 64)])


def shape_constants():
    c = np.zeros((P, N_CONST), np.float32)

    def put(name, v):
        a, n = CONSTS[name]
        c[:, a:a + n] = np.asarray(v, np.float32).reshape(P, n)

    i, j = np.arange(P)[:, None], np.arange(P)[None, :]
    put("ident", i == j)
    freq = (np.float32(10000.0) ** (-np.arange(16, dtype=np.float32) / np.float32(16))).astype(np.float32)
    ang = np.arange(SEQ, dtype=np.float32)[:, None] * freq
    put("cos", np.cos(ang).reshape(NT, P, 16).transpose(1, 0, 2))
    put("sin", np.sin(ang).reshape(NT, P, 16).transpose(1, 0, 2))
    diag = np.zeros((P, 512), np.float32)
    diag[:, 384:] = np.where(j // CHUNK <= i // CHUNK, 0.0, NEG)
    put("chunk_mask", diag)
    diag[:, 384:] = np.where(j <= i, 0.0, NEG)
    put("causal_mask", diag)
    put("upper", i <= j)
    put("upper_strict", i < j)
    put("lower", i >= j)
    put("ones", np.ones((P, P)))
    put("iota", np.broadcast_to(j, (P, P)))
    put("token", i + P * np.arange(NT)[None, :])
    put("block_start", np.broadcast_to(P * np.arange(BLOCKS + 1)[None, :], (P, BLOCKS + 1)))

    def level(n):
        b = 1 << n
        return (i // (2 * b) == j // (2 * b)) & ((i // b) % 2 == 1) & ((j // b) % 2 == 0)
    put("level0", level(0))
    put("level0_t", level(0).T)
    put("levels_t", np.concatenate([level(n).T for n in range(1, 7)], axis=1))
    rel = np.arange(640) - 511
    half, exact = BUCKETS // 2, BUCKETS // 4
    n = np.abs(rel)
    big = exact + (np.log(np.maximum(n, 1).astype(np.float32) / np.float32(exact))
                   / np.float32(math.log(MAX_DISTANCE / exact)) * np.float32(half - exact)).astype(np.int32)
    bucket = (rel > 0) * half + np.where(n < exact, n, np.minimum(big, half - 1))
    one_hot = (bucket[None, :] == np.arange(BUCKETS)[:, None]).astype(np.float32)
    return c, one_hot


def build(nc, t, out):
    SC1 = [nc.dram_tensor("relative_bias_lines", (P, DIFF_H, 640), F32, kind="Internal").ap(),
           nc.dram_tensor("x_rows", (SEQ, D), F32, kind="Internal").ap(),
           nc.dram_tensor("expert_rows", (BLOCKS * P, D), F32, kind="Internal").ap()]
    bias_line, x_rows, y_rows = SC1

    with ExitStack() as ctx:
        def sem(name):
            return ctx.enter_context(nc.semaphore(name))

        FREE_FLOATS = 53100
        mem = ctx.enter_context(nc.sbuf_tensor("mem", [P, FREE_FLOATS], F32))
        top = [0]

        def place(at, *dims):
            n = int(np.prod(dims))
            assert at + n <= FREE_FLOATS, (at, dims)
            v = mem[:, at:at + n]
            if len(dims) == 2:
                v = v.rearrange("p (a b) -> p a b", a=dims[0])
            if len(dims) == 3:
                v = v.rearrange("p (a b c) -> p a b c", a=dims[0], b=dims[1])
            return v

        def keep(*dims):
            at = top[0]
            top[0] += int(np.prod(dims))
            return place(at, *dims)

        cst = keep(N_CONST)
        col = keep(384)
        row = keep(N_ROWS)
        gate_rows = keep(2, D)
        mod = keep(4, KD)
        small = keep(640)
        x = keep(NT, D)
        work = top[0]

        def const(name, *dims):
            a, n = CONSTS[name]
            v = cst[:, a:a + n]
            return v.rearrange("p (a b) -> p a b", a=dims[0]) if dims else v

        def column(name, k=None):
            a, n = COLS[name]
            return col[:, a:a + n] if k is None else col[:, a + k:a + k + 1]

        def rows(name):
            a, n = ROWS[name]
            return row[:, a:a + n]

        ident = const("ident")
        cut = Counter()

        def tiny(n):
            a = cut["tiny"]
            cut["tiny"] += n
            assert cut["tiny"] <= 640
            return small[:, a:a + n]
        stat = tiny(8)
        stat8 = tiny(16)
        neg_max = tiny(8)
        row_sum = tiny(8)
        lam = tiny(4)
        cond = tiny(KD)
        eps_col = tiny(1)
        beta = tiny(NT * 8).rearrange("p (a b) -> p a b", a=NT)
        gdec = tiny(NT * 8).rearrange("p (a b) -> p a b", a=NT)
        gsum = tiny(NT * 8).rearrange("p (a b) -> p a b", a=NT)
        eg = tiny(NT * 8).rearrange("p (a b) -> p a b", a=NT)
        beg = tiny(NT * 8).rearrange("p (a b) -> p a b", a=NT)
        a_neg = tiny(8)
        tail = tiny(HG)
        g_last = [tiny(HG), tiny(HG)]
        top8 = tiny(8)
        w_idx = tiny(NT * 8).rearrange("p (a b) -> p a b", a=NT)

        SLOT, SLOTS = 4096, 3
        ring = work
        hT = place(ring + SLOTS * SLOT, KD, SEQ)
        A0 = ring + (SLOTS + 1) * SLOT

        def areas(parts):
            at, o = A0, {}
            for name, dims in parts:
                o[name] = place(at, *dims)
                at += int(np.prod(dims))
            assert at <= FREE_FLOATS, (at, FREE_FLOATS)
            return o

        S1 = areas([("lat", (NT, LAT)), ("dq", (NT, 512)), ("dk", (NT, 512)), ("dv", (NT, 512)),
                    ("kT", (MLA_H, SEQ)), ("v", (NT, 512)), ("yT", (KD, SEQ)),
                    ("pT", (2, NT, SEQ)), ("s", (4, SEQ))])
        pT_at = A0 + NT * LAT + 3 * 2048 + 4096 + 2048 + 4096
        heads = place(pT_at, 2, 768)
        square = place(pT_at + 1536, 1024)
        latT = place(pT_at + 2560, 3, SEQ)
        rope_t = S1["s"][:, 0, :].rearrange("p (a b c) -> p a b c", a=4, b=8)
        xn = S1["pT"].rearrange("p a b c -> p (a b c)")[:, 0:2 * D].rearrange("p (a b) -> p a b", a=2)
        bias_t = None
        diff_bias = S1["kT"].rearrange("p a b -> p (a b)")[:, 0:4 * 512].rearrange("p (a b) -> p a b", a=4)
        diff_o = S1["v"]
        staging = place(ring + SLOTS * SLOT, 3, P)
        cond_b = place(A0 + 24192, KD, P)
        one_hot = place(ring + SLOTS * SLOT + 512 + 1024, 640)
        rel_table = place(ring + SLOTS * SLOT + 512 + 1024 + 640, 4)
        rel_wide = place(ring + SLOTS * SLOT + 512 + 1024 + 1280, 4, P)
        bias_head = S1["yT"].rearrange("p a b -> p (a b)")[:, 0:4 * 640].rearrange("p (a b) -> p a b", a=4)
        S2 = areas([("act", (FT, SEQ)), ("gpad", (2, SEQ + 4)), ("conv", (2, SEQ)),
                    ("sig", (2, SEQ)), ("tmp", (SEQ,)), ("p", (NT, PLE)), ("pleT", (2, SEQ)), ("xn", (2, D))])
        S3 = areas([("qT", (8, SEQ)), ("q_idx", (4, SEQ)), ("k_idx", (SEQ,)), ("small", (NT, 344)),
                    ("kvT", (2, SEQ)), ("kT", (8, SEQ)), ("v", (NT, D)), ("sel", (3, SEQ)),
                    ("score", (SEQ,)), ("s", (3, SEQ)), ("pT", (1, NT, SEQ))])
        S4 = areas([("yT", (8, SEQ)), ("dnT", (8, SEQ)), ("q", (HG, SEQ)), ("k", (HG, SEQ)), ("v", (HG, SEQ)),
                    ("z", (NT, HG * DH))]
                   + [(n, (HG, P)) for n in ("tmp", "decay", "A", "AT", "qk", "qkT", "k_tail", "k_bg", "v_b",
                                             "X", "XT", "L0", "L1", "u", "wT", "state")]
                   + [("gpad", (2, SEQ + 4))])
        flat_pad = S4["gpad"].rearrange("p a b -> p (a b)")
        result = flat_pad[:, 0:HG * P].rearrange("p (a b) -> p a b", a=HG)
        result_sq = flat_pad[:, HG * P:2 * HG * P]
        S5 = areas([("yT", (8, SEQ)), ("dnT", (8, SEQ)), ("sig", (4, SEQ)), ("mg", (8, SEQ)), ("tmp", (SEQ,)),
                    ("ln", (4, D)), ("sq", (D,))])

        wg_s = [place(work + n * SLOT, KD, EFF) for n in range(2)]
        wu_s = [place(work + (2 + n) * SLOT, KD, EFF) for n in range(2)]
        wd_s = [place(work + (4 + n) * SLOT, EFF // P, D) for n in range(2)]
        M0 = work + 6 * SLOT
        at = [M0]

        def moe(*dims):
            a = at[0]
            at[0] += int(np.prod(dims))
            return place(a, *dims)
        xg = moe(2, D)
        xgT = moe(2, KD, P)
        hb = moe(2, EFF)
        hbT = moe(2, EFF // P, P)
        yb = moe(2, D)
        zeros = moe(D)
        y_of = place(work, 2 * NT, D)
        ln_rows = moe(4, D)
        logit = moe(NT, 36)
        g_hot, e_in, e_tmp = moe(NT, 4), moe(NT, 8), moe(NT, 8)
        hot = [moe(NT, 8), moe(NT, 8)]
        choice = [moe(NT, 32), moe(NT, 32)]
        both, rank, wide = moe(NT, 32), moe(NT, 32), moe(NT, 32)
        nb, b_end, b_at = moe(32), moe(32), moe(32)
        dest_all = moe(2 * NT)
        dest = [dest_all[:, 0:NT], dest_all[:, NT:2 * NT]]
        count, place_in = moe(2 * NT), moe(2 * NT)
        gate_of = [moe(NT), moe(NT)]
        r_m1, r_m2, r_t = moe(NT), moe(NT), moe(NT)
        ge, in_block = moe(2 * NT, BLOCKS + 1), moe(2 * NT, BLOCKS)
        slot_hot = xg[:, 0, :].rearrange("p (a b) -> p a b", a=2 * NT)
        ebw = moe(BLOCKS, 32)
        eb_f = moe(BLOCKS)
        rev = moe(8)
        w_route = moe(KD, 36)
        ints = ctx.enter_context(nc.sbuf_tensor("ints", [P, 2 * BLOCKS + 2 * NT + 4], I32))
        slot_token = ints[:, 0:BLOCKS]
        block_expert = ints[:, BLOCKS:2 * BLOCKS]
        dest_i = [ints[:, 2 * BLOCKS + j * NT:2 * BLOCKS + (j + 1) * NT] for j in range(2)]
        gather_i = ints[:, 2 * BLOCKS + 2 * NT:2 * BLOCKS + 2 * NT + 2]
        used_i = ints[:, 2 * BLOCKS + 2 * NT + 2:2 * BLOCKS + 2 * NT + 3]
        pool_note = moe(2)

        banks = [ctx.enter_context(nc.psum_tensor(f"bank{i}", [P, 512], F32)) for i in range(8)]
        dve_full, dve_free = sem("dve_ring_full"), sem("dve_ring_free")
        act_full, act_free = sem("act_ring_full"), sem("act_ring_free")

        loaded = sem("inputs_loaded")
        x_loaded = sem("x_loaded")
        p_loaded = sem("p_loaded")
        ln_loaded = sem("ln_rows_loaded")
        ln2_loaded = sem("ln_rows_2_loaded")
        route_loaded = sem("route_weights_loaded")
        w_full = [sem(f"weights_in_slot{i}") for i in range(SLOTS)]
        w_free = sem("weights_used_early")
        dve_step, act_step, pool_step = sem("dve_step"), sem("act_step"), sem("pool_step")
        var_ready, std_ready = sem("variance_ready"), sem("deviation_ready")
        tp_ready = sem("rows_to_transpose_ready")
        s_ready, e_ready, p_ready = sem("scores_masked"), sem("scores_exp"), sem("probabilities_ready")
        silu_in, silu_out = sem("conv_ready"), sem("silu_ready")
        sig_out, sig_used = sem("gates_ready"), sem("gates_used")
        to_act, from_act = sem("dve_to_act"), sem("act_to_dve")
        to_pe = sem("dve_to_pe")
        to_pool, from_pool = sem("dve_to_pool"), sem("pool_to_pe")
        line_out, bias_in = sem("bias_line_written"), sem("bias_loaded")
        x_spilled = sem("x_rows_written")
        expand_loaded = sem("expansion_weights_loaded")

        items = []

        def w3(ap):
            return ap.rearrange("(k p) n -> p k n", p=P)

        def item(name, *loads):
            items.append((name, loads))

        def slot_view(n, k, width, extra=0):
            return place(ring + (n % SLOTS) * SLOT + extra, k, width)

        def add(name, src, k, width):
            n = len(items)
            item(name, (slot_view(n, k, width), w3(src)))

        W = {k: v[0] if len(v.shape) > 2 or k.startswith("w_") else v for k, v in t.items()}
        for name, a, b in (("lat", 0, LAT), ("dq", LAT, LAT + 512), ("dk", LAT + 512, LAT + 1024),
                           ("dv", LAT + 1024, LAT + 1536)):
            add(name, W["w_in"][:, a:b], KD, b - a)
        for c in range(12):
            add("ada", W["w_ada_2"][:, c * 512:(c + 1) * 512], KD, 512)
        for c in range(2):
            add("out", W["w_out"][:, c * 512:(c + 1) * 512], KD, 512)
        ff_chunks = [(a, min(512, D_FF - a)) for a in range(0, D_FF, 512)]
        for a, n in ff_chunks:
            add("gate", W["w_gate"][:, a:a + n], KD, n)
            add("up", W["w_up"][:, a:a + n], KD, n)
        down_parts = [(0, 8), (8, 8), (16, 6)]
        for c in range(2):
            for k0, nk in down_parts:
                add("down", W["w_down"][k0 * P:(k0 + nk) * P, c * 512:(c + 1) * 512], nk, 512)
        add("ple_proj", W["w_ple_proj"], 2, D)
        for c in range(2):
            add("ple_gate", W["w_ple_gate"][:, c * 512:(c + 1) * 512], KD, 512)
        wi2 = W["w_in_2"]
        n = len(items)
        mixed = slot_view(n, KD, 344)
        item("mixed", (mixed[:, :, 0:256], w3(wi2[:, OFF_CKV:OFF_CKV + 256])),
             (mixed[:, :, 256:328], w3(wi2[:, OFF_KIDX:OFF_KIDX + 72])),
             (mixed[:, :, 328:344], w3(wi2[:, OFF_AB:OFF_AB + 16])))
        add("q_idx", wi2[:, OFF_QIDX:OFF_QIDX + 512], KD, 512)
        for c in range(2):
            add("q_att", wi2[:, c * 512:(c + 1) * 512], KD, 512)
        n = len(items)
        uk_v = slot_view(n, 2, 8 * 128).rearrange("p a (h d) -> p a h d", h=8)
        uv_v = slot_view(n, 2, 8 * 128, 2048).rearrange("p a (h d) -> p a h d", h=8)
        item("ukuv", *[(v[:, a, :, :], W[w][:, a * P:(a + 1) * P, :].rearrange("h p d -> p h d"))
                       for v, w in ((uk_v, "w_uk_2"), (uv_v, "w_uv_2")) for a in range(2)])
        for g in range(2):
            for part in range(3):
                a = OFF_QKV + part * 1024 + g * 512
                add("qkv", wi2[:, a:a + 512], KD, 512)
            add("z", wi2[:, OFF_Z + g * 512:OFF_Z + (g + 1) * 512], KD, 512)
        for c in range(2):
            for name, src in (("gate_a", wi2[:, OFF_GATE + c * 512:OFF_GATE + (c + 1) * 512]),
                              ("br_a", W["w_br_att_2"][:, c * 512:(c + 1) * 512]),
                              ("gate_d", wi2[:, OFF_GATE + D + c * 512:OFF_GATE + D + (c + 1) * 512]),
                              ("br_d", W["w_br_dn_2"][:, c * 512:(c + 1) * 512])):
                add(name, src, KD, 512)
        for c in range(2):
            add("out2", W["w_out_2"][:, c * 512:(c + 1) * 512], KD, 512)
        slot_total, slot_need = Counter(), []
        for n, (_, loads) in enumerate(items):
            slot_total[n % SLOTS] += 16 * len(loads)
            slot_need.append(slot_total[n % SLOTS])
        item_done = []
        mark = {}

        units = [(h, q) for h in range(8) for q in range(NT)]
        diff_units = [(h, q) for h in range(DIFF_H) for q in range(NT)]


        def blocks_used(eng):
            return eng.value_load(used_i[0:1, 0:1], min_val=1, max_val=BLOCKS)

        xt_full, xt_taken, x_scaled = sem("x_turned"), sem("x_turned_taken"), sem("x_scaled")
        x_gathered = [sem(f"x_gathered{i}") for i in range(2)]
        wg_in, wu_in, wd_in = ([sem(f"{n}{i}") for i in range(2)] for n in ("gate_in", "up_in", "down_in"))
        gate_full, up_full, silu_done, hb_ready = (sem(n) for n in ("gate_full", "up_full", "silu_done", "hidden"))
        ht_full, ht_taken, y_full = sem("hidden_turned"), sem("hidden_turned_taken"), sem("y_full")
        y0_taken, y1_taken = sem("y_left_taken"), sem("y_right_taken")
        y_stored = [sem(f"y_stored{i}") for i in range(2)]
        y_back = [sem(f"y_gathered{q}") for q in range(NT)]
        x_done, out_stored = sem("x_done"), sem("out_stored")
        tables_ready, experts_known = sem("tables_ready"), sem("experts_known")
        idx_ready, rows_stored = sem("indices_ready"), sem("expert_rows_stored")
        zeros_stored = sem("zero_rows_stored")

        def flat(v):
            return v.rearrange("p a b -> p (a b)")

        def inner_at(v, n):
            return v.to_broadcast([P, v.shape[1], n])

        flat_y = S1["yT"].rearrange("p a b -> p (a b)")
        wq = flat_y[:, 0:1536].rearrange("p (a b) -> p a b", a=2)
        wkv = flat_y[:, 1536:2560].rearrange("p (a b) -> p a b", a=1)

        def spread(name, n, offset=0):
            return bass.AP(tensor=t[name].tensor, offset=offset, ap=[[0, P], [1, n]])
        first_loads = [(cst, t["shape_constants"]), (one_hot[0:BUCKETS, :], t["distance_buckets"]),
                       (rel_table[0:BUCKETS, :], t["rel_bias"])]
        for name, (a, n) in COLS.items():
            k = 0
            src = t[name]
            src = src.rearrange("a b n -> (a b n)") if len(src.shape) == 3 else src.rearrange("a n -> (a n)")
            src = src.rearrange("(r p) -> r p", p=P)
            while k < n:
                g, r = divmod(a + k, P)
                m = min(n - k, P - r)
                first_loads.append((staging[r:r + m, g, :], src[k:k + m, :]))
                k += m
        for name, (a, n) in ROWS.items():
            first_loads.append((rows(name), spread(name, n)))
        for j in range(2):
            first_loads.append((gate_rows[:, j, :], spread("b_ada_2", D, (2 + 3 * j) * D)))
        n_loads = len(first_loads)
        one_hot_free = S1["s"][:, 0, 0:64]

        block = ctx.enter_context(nc.Block())

        @block.tensor
        def _(pe):
            done = Counter()
            nxt = Counter()

            def bank(ring_name):
                n = done[ring_name]
                free = dve_free if ring_name == "dve" else act_free
                if n >= 4:
                    pe.wait_ge(free, n - 3)
                return banks[n % 4 + (0 if ring_name == "dve" else 4)]

            def full(last, ring_name):
                done[ring_name] += 1
                last.then_inc(dve_full if ring_name == "dve" else act_full, 1)

            def taken(ring_name):
                pe.wait_ge(dve_free if ring_name == "dve" else act_free, done[ring_name])

            def weights(name):
                n = nxt["item"]
                assert items[n][0] == name, (items[n][0], name)
                pe.wait_ge(w_full[n % SLOTS], slot_need[n])
                nxt["item"] += 1
                return [v for v, _ in items[n][1]]

            def used(ring_name=None):
                item_done.append((dve_full, done["dve"]) if ring_name == "dve" else (act_full, done["act"]))

            def to_wait(s, n=1):
                nxt[s] += n
                pe.wait_ge(s, nxt[s])

            def product(o, pairs):
                for i, (l, r) in enumerate(pairs):
                    last = pe.matmul(o, l, r, start=(i == 0), stop=(i == len(pairs) - 1))
                return last

            def by_token(ring_name, w, lhs, width, kk=KD, at=0):
                for q in range(NT):
                    b = bank(ring_name)
                    full(product(b[:, 0:width], [(lhs[:, k, q * P:(q + 1) * P], w[:, k, at:at + width])
                                                 for k in range(kk)]), ring_name)

            def by_feature(ring_name, w, rhs, tiles, kk=KD):
                for m in range(tiles):
                    b = bank(ring_name)
                    full(product(b[:, :], [(w[:, k, m * P:(m + 1) * P], rhs[:, k, :]) for k in range(kk)]),
                         ring_name)

            def turn(ring_name, sources, width=P):
                b = bank(ring_name)
                for i, s in enumerate(sources):
                    last = pe.transpose(b[0:width, i * P:(i + 1) * P], s, ident)
                full(last, ring_name)

            def turn_x(from_xn):
                for q in range(NT):
                    if from_xn:
                        to_wait(tp_ready)
                        src = xnb[:, q % 2, :]
                    else:
                        src = x[:, q, :]
                    for hf in range(2):
                        turn("dve", [src[:, (4 * hf + k) * P:(4 * hf + k + 1) * P] for k in range(4)])
                taken("dve")

            pe.wait_ge(loaded, 16 * n_loads)
            for g in range(3):
                n = min(P, N_COLS - g * P)
                b = bank("dve")
                full(pe.transpose(b[:, 0:n], staging[0:n, g, :], ident[0:n, 0:n]), "dve")
            to_wait(to_pe)
            for h in range(DIFF_H):
                for a, n in ((0, 512), (512, 128)):
                    b = bank("dve")
                    full(pe.matmul(b[:, 0:n], rel_wide[0:BUCKETS, h, :], one_hot[0:BUCKETS, a:a + n],
                                   start=True, stop=True), "dve")
            to_wait(to_pe)

            def modulation(c):
                w = weights("ada")[0]
                if c in (4, 5, 10, 11):
                    b = bank("dve")
                    full(product(b[:, :], [(cond_b[:, k, :], w[:, k, :]) for k in range(KD)]), "dve")
                else:
                    b = bank("dve")
                    for m in range(4):
                        last = product(b[:, m:m + 1], [(w[:, k, m * P:(m + 1) * P], cond[:, k:k + 1])
                                                       for k in range(KD)])
                    full(last, "dve")
                used("dve")

            xnb = xn
            turn_x(True)
            for name, width in (("lat", LAT), ("dq", 512), ("dk", 512), ("dv", 512)):
                by_token("act", weights(name)[0], hT, width)
                used("act")
            for q in range(NT):
                if q == 0:
                    to_wait(to_pe)
                turn("dve", [S1["lat"][:, q, k * P:(k + 1) * P] for k in range(3)])
            taken("dve")
            pe.wait_ge(expand_loaded, 32)

            def head_turns(G, width):
                to_wait(tp_ready)
                u = nxt["unit"]
                nxt["unit"] += 1
                src = heads[:, u % 2, 0:G * width].rearrange("p (g d) -> p g d", g=G)
                per = 4
                for a in range(0, G, per):
                    turn("act", [src[:, a + i, :] for i in range(per)], width)
                mark["heads", u] = done["act"]
            def expand(q):
                lq = [latT[:, k, q * P:(q + 1) * P] for k in range(3)]
                b = bank("dve")
                full(product(b[:, :], [(lq[k], wq[:, k, 0:512]) for k in range(2)]), "dve")
                b = bank("dve")
                full(product(b[:, 0:256], [(lq[k], wq[:, k, 512:768]) for k in range(2)]), "dve")
                for a in range(2):
                    b = bank("dve")
                    full(product(b[:, :], [(lq[2], wkv[:, 0, a * 512:(a + 1) * 512])]), "dve")
            expand(0)
            for q in range(NT):
                modulation(2 * q)
                head_turns(8, QK)
                modulation(2 * q + 1)
                if q < NT - 1:
                    expand(q + 1)
                head_turns(8, QK)
            taken("act")

            def attention(name, qT, kT, K, v_of, out_of, pT, beside=None):
                nbuf = pT.shape[1]

                def scores(n):
                    h, q = units[n]
                    b = bank("dve")
                    full(product(b[:, 0:(q + 1) * P], [(qT[0:K, h, q * P:(q + 1) * P],
                                                        kT[0:K, h, 0:(q + 1) * P])]), "dve")

                def turns(n):
                    h, q = units[n]
                    to_wait(p_ready)
                    src = sbuf[:, n % 3, :]
                    turn("act", [src[:, k * P:(k + 1) * P] for k in range(q + 1)])
                    mark[name, "T", n] = done["act"]

                def values(h):
                    b = bank("dve")
                    pe.wait_ge(act_free, mark[name, "T", 4 * h + 3])
                    o = out_of(b, h)
                    for k in range(NT):
                        last = pe.matmul(o[:, k * P:SEQ], v_of(k, h), pT[:, h % nbuf, k, k * P:SEQ],
                                         start=(k == 0), stop=(k == NT - 1))
                    full(last, "dve")
                    mark[name, "PV", h] = done["dve"]

                sbuf = (S1 if name == "mla" else S3)["s"]
                N = len(units)
                scores(0)
                scores(1)
                for n in range(N + 1):
                    if n + 2 < N:
                        scores(n + 2)
                    if beside and n % 4 == 0 and n // 4 < 4:
                        beside(8 + n // 4)
                    if n < N:
                        turns(n)
                    if n >= 1 and units[n - 1][1] == NT - 1:
                        values(units[n - 1][0])
                taken("dve")

            attention("mla", hT, S1["kT"], QK,
                      lambda k, h: S1["v"][:, k, h * 64:(h + 1) * 64],
                      lambda b, h: b[64 * (h % 2):64 * (h % 2) + 64, :], S1["pT"], modulation)

            for q in range(NT):
                head_turns2 = head_turns
                for _ in range(2):
                    to_wait(tp_ready)
                    u = nxt["unit"]
                    nxt["unit"] += 1
                    turn("act", [heads[:, u % 2, a * P:(a + 1) * P] for a in range(4)])
                    mark["heads", u] = done["act"]
            taken("act")

            def diff_scores(n):
                h, q = diff_units[n]
                for m in range(2):
                    b = bank("dve")
                    full(product(b[:, 0:(q + 1) * P], [(hT[64 * m:64 * m + 64, h, q * P:(q + 1) * P],
                                                        hT[64 * m:64 * m + 64, 4 + h, 0:(q + 1) * P])]), "dve")

            def diff_turns(n):
                h, q = diff_units[n]
                to_wait(p_ready)
                turn("act", [S1["s"][:, 2 * (n % 2), k * P:(k + 1) * P] for k in range(q + 1)])
                mark["diff", "T", n] = done["act"]

            def diff_values(n):
                h, q = diff_units[n]
                b = bank("dve")
                pe.wait_ge(act_free, mark["diff", "T", n])
                full(product(b[:, 0:P], [(S1["pT"][:, n % 2, k, 0:P], S1["dv"][:, k, h * P:(h + 1) * P])
                                         for k in range(q + 1)]), "dve")
                mark["diff", "PV", n] = done["dve"]

            diff_scores(0)
            diff_scores(1)
            for n in range(17):
                if n < 16:
                    diff_turns(n)
                if n >= 1:
                    diff_values(n - 1)
                if n + 2 < 16:
                    diff_scores(n + 2)
            for q in range(NT):
                to_wait(tp_ready)
                turn("act", [diff_o[:, q, h * P:(h + 1) * P] for h in range(4)])
            taken("act")
            for c in range(2):
                by_token("dve", weights("out")[0], S1["yT"], 512)
                used("dve")
            mark["attention added"] = done["dve"]
            xnb = S2["xn"]
            turn_x(True)
            for a, n in ff_chunks:
                for name in ("gate", "up"):
                    by_feature("dve", weights(name)[0], hT, n // P)
                    used("dve")
            taken("dve")
            for c in range(2):
                open_banks = []
                for i, (k0, nk) in enumerate(down_parts):
                    w = weights("down")[0]
                    for q in range(NT):
                        if i == 0:
                            n = done["dve"] + q
                            pe.wait_ge(dve_free, n - 3)
                            open_banks.append(banks[n % 4])
                        for k in range(nk):
                            last = pe.matmul(open_banks[q][:, :], S2["act"][:, k0 + k, q * P:(q + 1) * P],
                                             w[:, k, :], start=(i == 0 and k == 0),
                                             stop=(i == 2 and k == nk - 1))
                        if i == 2:
                            last.then_inc(dve_full, 1)
                    if i < 2:
                        last.then_inc(w_free, 1)
                        nxt["wfree"] += 1
                        item_done.append((w_free, nxt["wfree"]))
                done["dve"] += 4
                used("dve")
            turn_x(True)
            pe.wait_ge(p_loaded, 16)
            for q in range(NT):
                turn("dve", [S2["p"][:, q, k * P:(k + 1) * P] for k in range(2)])
            taken("dve")
            wp = weights("ple_proj")[0]
            item_done.append(None)
            at_item = len(item_done) - 1
            for c in range(2):
                w = weights("ple_gate")[0]
                for q in range(NT):
                    lq = slice(q * P, (q + 1) * P)
                    b = bank("act")
                    full(product(b[:, :], [(hT[:, k, lq], w[:, k, :]) for k in range(KD)]), "act")
                    b = bank("dve")
                    full(product(b[:, :], [(S2["pleT"][:, k, lq], wp[:, k, c * 512:(c + 1) * 512])
                                           for k in range(2)]), "dve")
                used("act")
            item_done[at_item] = (dve_full, done["dve"])
            taken("dve")
            pe.wait_ge(sig_used, 8)
            turn_x(False)
            w = weights("mixed")[0]
            wmix = mixed
            by_token("dve", wmix, hT, 344)
            b = bank("act")
            for hf in range(2):
                for k in range(KD):
                    last = pe.matmul(b[64 * hf:64 * hf + 64, :], wmix[:, k, 256:320], hT[:, k, :],
                                     start=(k == 0), stop=(k == KD - 1))
            full(last, "act")
            used("act")
            by_feature("act", weights("q_idx")[0], hT, 4)
            used("act")
            to_wait(to_pe)
            b = bank("dve")
            for q in range(NT):
                last = pe.matmul(b[:, q * 8:(q + 1) * 8], const("upper"), gdec[:, q, :], start=True, stop=True)
            full(last, "dve")
            for q in range(NT):
                turn("dve", [S3["small"][:, q, k * P:(k + 1) * P] for k in range(2)])
            taken("act")
            def index_scores(q):
                for h in range(IDX_H):
                    o = slice(64 * (h % 2), 64 * (h % 2) + 64)
                    b = bank("dve")
                    full(product(b[:, 0:(q + 1) * P], [(S3["q_idx"][o, h // 2, q * P:(q + 1) * P],
                                                        S3["k_idx"][o, 0:(q + 1) * P])]), "dve")
            index_scores(1)
            for c in range(2):
                by_feature("act", weights("q_att")[0], hT, 4)
                used("act")
                index_scores(2 + c)
            weights("ukuv")
            for h in range(8):
                b = bank("act")
                full(product(b[:, :], [(uk_v[:, a, h, :], S3["kvT"][:, a, :]) for a in range(2)]), "act")
            for q in range(NT):
                for hf in range(2):
                    b = bank("act")
                    full(product(b[:, :], [(S3["kvT"][:, a, q * P:(q + 1) * P],
                                            uv_v[:, a, 4 * hf:4 * hf + 4, :].rearrange("p h d -> p (h d)"))
                                           for a in range(2)]), "act")
            used("act")
            taken("act")
            attention("dsa", S3["qT"], S3["kT"], P, lambda k, h: S3["v"][:, k, h * P:(h + 1) * P],
                      lambda b, h: b[:, :], S3["pT"])

            for g in range(2):
                for part in range(3):
                    w = weights("qkv")[0]
                    for i in range(4):
                        b = bank("dve")
                        full(product(b[:, :], [(w[:, k, i * P:(i + 1) * P], hT[:, k, :]) for k in range(KD)]), "dve")
                        if i == 3:
                            used("dve")
                        if part:
                            to_wait(to_pe)
                            b = bank("act")
                            full(product(b[:, :], [(const("ones"), flat(S4[("tmp", "decay")[i % 2]]))]), "act")
                by_token("act", weights("z")[0], hT, 512)
                used("act")
                B = S4

                def some(ring_name, heads_, lhs, rhs):
                    b = bank(ring_name)
                    for i, h in enumerate(heads_):
                        last = pe.matmul(b[:, i * P:(i + 1) * P], lhs(h), rhs(h), start=True, stop=True)
                    full(last, ring_name)

                def four(ring_name, lhs, rhs):
                    some(ring_name, range(HG), lhs, rhs)
                updated = {}

                def result_turn(g):
                    to_wait(tp_ready)
                    turn("act", [result[:, h, :] for h in range(HG)])
                    mark["result", g] = done["act"]
                pe.wait_ge(silu_out, FT + 12 * (g + 1))
                for ch in range(NT):
                    cs = slice(ch * P, (ch + 1) * P)
                    if ch == 0:
                        to_wait(to_pe)
                        four("dve", lambda h: B["tmp"][:, h, :], lambda h: const("upper"))
                    four("dve", lambda h: B["k"][:, h, cs], lambda h: B["k"][:, h, cs])
                    four("dve", lambda h: B["q"][:, h, cs], lambda h: B["k"][:, h, cs])
                    turn("dve", [B["k"][:, h, cs] for h in range(HG)])
                    turn("dve", [B["v"][:, h, cs] for h in range(HG)])
                    to_wait(to_pe)
                    turn("act", [B["A"][:, h, :] for h in range(HG)])
                    mark["AT", g, ch] = done["act"]
                    to_wait(to_pe)
                    for lv in range(6):
                        to_wait(from_pool)
                        turned_at = []
                        for half in HALVES:
                            if lv:
                                pe.wait_ge(dve_free, updated[half[0]])
                                turn("act", [B["X"][:, h, :] for h in half])
                            some("act", half, lambda h: B[f"L{lv % 2}"][:, h, :], lambda h: B["X"][:, h, :])
                            turned_at.append(done["act"])
                        mark["T", g, ch, lv] = done["act"]
                        if lv == 0:
                            to_wait(to_pe)
                            turn("act", [B["qk"][:, h, :] for h in range(HG)])
                        for half, at_ in zip(HALVES, turned_at):
                            pe.wait_ge(act_free, at_)
                            if lv < 5:
                                some("dve", half, lambda h: B["XT"][:, h, :], lambda h: B["u"][:, h, :])
                            else:
                                some("dve", half, lambda h: B["u"][:, h, :], lambda h: B["XT"][:, h, :])
                            updated[half[0]] = done["dve"]
                        if lv == 2 and ch < NT - 1:
                            to_wait(to_pe)
                            four("dve", lambda h: B["tmp"][:, h, :], lambda h: const("upper"))
                    taken("dve")
                    if ch:
                        result_turn(g)
                    four("act", lambda h: B["XT"][:, h, :], lambda h: B["v_b"][:, h, :])
                    four("act", lambda h: B["k_bg"][:, h, :], lambda h: B["XT"][:, h, :])
                    four("dve", lambda h: B["q"][:, h, cs], lambda h: B["state"][:, h, :])
                    taken("act")
                    four("dve", lambda h: B["wT"][:, h, :], lambda h: B["state"][:, h, :])
                    taken("dve")
                    four("dve", lambda h: B["qkT"][:, h, :], lambda h: B["v_b"][:, h, :])
                    four("dve", lambda h: B["k_tail"][:, h, :], lambda h: B["v_b"][:, h, :])
                result_turn(g)
            taken("act")
            taken("dve")
            for c in range(2):
                by_feature("act", weights("gate_a")[0], hT, 4)
                used("act")
                by_feature("dve", weights("br_a")[0], S5["yT"], 4)
                mark["branch", 2 * c] = done["dve"]
                used("dve")
                by_feature("act", weights("gate_d")[0], hT, 4)
                used("act")
                by_feature("dve", weights("br_d")[0], S5["dnT"], 4)
                mark["branch", 2 * c + 1] = done["dve"]
                used("dve")
            taken("dve")
            for c in range(2):
                by_token("dve", weights("out2")[0], S5["mg"], 512)
                used("dve")
            taken("dve")
            for q in range(NT):
                to_wait(to_pe)
                for hf in range(2):
                    turn("dve", [x[:, q, (4 * hf + k) * P:(4 * hf + k + 1) * P] for k in range(4)])
            mark["x normalised"] = nxt[to_pe]
            taken("dve")
            pe.wait_ge(route_loaded, 32)
            by_token("dve", w_route, hT, 36)
            to_wait(to_pe)
            b = bank("dve")
            for q in range(NT):
                last = product(b[:, q * 32:(q + 1) * 32],
                               [(const("upper_strict") if r == q else const("ones"), both[:, r, :])
                                for r in range(q + 1)])
            full(last, "dve")
            b = bank("dve")
            full(product(b[:, 0:32], [(const("ones"), both[:, r, :]) for r in range(NT)]), "dve")
            b = bank("dve")
            to_wait(to_pe)
            full(product(b[:, 0:BLOCKS], [(slot_hot[:, n, :], in_block[:, n, :]) for n in range(2 * NT)]), "dve")
            taken("dve")
            taken("act")
            assert nxt["item"] == len(items) == len(item_done)

            def expert_turns(i, s):
                pe.wait_ge(x_gathered[s], (i + 1) * 16)
                for hf in range(2):
                    for k in range(4):
                        last = pe.transpose(banks[hf][:, k * P:(k + 1) * P],
                                            xg[:, s, (4 * hf + k) * P:(4 * hf + k + 1) * P], ident)
                    last.then_inc(xt_full, 1)

            def expert_block(i, s, first=False, last=False):
                n = 2 * i + s
                pe.wait_ge(xt_taken, 2 * n + 2)
                pe.wait_ge(wg_in[s], (i + 1) * 16)
                product(banks[2][:, :], [(xgT[:, s, k, :], wg_s[s][:, k, :]) for k in range(KD)])\
                    .then_inc(gate_full, 1)
                pe.wait_ge(wu_in[s], (i + 1) * 16)
                product(banks[3][:, :], [(xgT[:, s, k, :], wu_s[s][:, k, :]) for k in range(KD)])\
                    .then_inc(up_full, 1)
                if not last:
                    expert_turns(i + s, 1 - s)
                pe.wait_ge(hb_ready, n + 1)
                for k in range(EFF // P):
                    turned = pe.transpose(banks[4][:, k * P:(k + 1) * P], hb[:, s, k * P:(k + 1) * P], ident)
                turned.then_inc(ht_full, 1)
                pe.wait_ge(ht_taken, n + 1)
                pe.wait_ge(wd_in[s], (i + 1) * 16)
                if not (first and s == 0):
                    pe.wait_ge(y0_taken, n)
                product(banks[5][:, :], [(hbT[:, s, k, :], wd_s[s][:, k, 0:512]) for k in range(4)])\
                    .then_inc(y_full, 1)
                if not (first and s == 0):
                    pe.wait_ge(y1_taken, n)
                product(banks[6][:, :], [(hbT[:, s, k, :], wd_s[s][:, k, 512:D]) for k in range(4)])\
                    .then_inc(y_full, 1)

            expert_turns(0, 0)
            for s in range(2):
                expert_block(0, s, first=True)
            with pe.Fori(1, PAIRS - 1) as i:
                for s in range(2):
                    expert_block(i, s)
            for s in range(2):
                expert_block(PAIRS - 1, s, last=(s == 1))
            pe.wait_ge(tables_ready, 1)
            with pe.If(blocks_used(pe) > 2 * PAIRS):
                expert_turns(PAIRS, 0)
                with pe.Fori(PAIRS, ALL_PAIRS - 1) as i:
                    for s in range(2):
                        expert_block(i, s)
                for s in range(2):
                    expert_block(ALL_PAIRS - 1, s, last=(s == 1))

        @block.vector
        def _(dve):
            n_of = Counter()

            def V(ins, signal=None):
                signal = dve_step if signal is None else signal
                ins.then_inc(signal, 1)
                n_of[signal] += 1
                dve.wait_ge(signal, n_of[signal])

            def take():
                n = n_of["taken"]
                n_of["taken"] += 1
                dve.wait_ge(dve_full, n + 1)
                return banks[n % 4]

            def wait_next(s, n=1):
                n_of["w", s] += n
                dve.wait_ge(s, n_of["w", s])

            tt, ts, stt = dve.tensor_tensor, dve.tensor_scalar, dve.scalar_tensor_tensor

            def inner(v, n):
                return v[:, :, None].to_broadcast([P, v.shape[1], n])

            def over(v, g):
                return v[:, None, :].to_broadcast([P, g, v.shape[1]])

            def invert(s):
                wait_next(std_ready)
                V(dve.reciprocal(s, s))

            def scale_var(s, width, eps, signal=None):
                V(ts(s, s, 1.0 / width, eps, ALU.mult, ALU.add), signal)

            def norm_heads(dst, src, G, width, gain, sq, signal=None):
                sq = sq[:, 0:G * width].rearrange("p (g d) -> p g d", g=G)
                V(tt(sq, src, src, ALU.mult))
                V(dve.tensor_reduce(stat8[:, 0:G], sq, AX.X, ALU.add))
                scale_var(stat8[:, 0:G], width, EPS, var_ready)
                invert(stat8[:, 0:G])
                V(tt(dst, src, inner(stat8[:, 0:G], width), ALU.mult))
                V(tt(dst, dst, over(gain, G), ALU.mult), signal)

            def turned_in(q, gain, shift=None):
                for hf in range(2):
                    b = take()
                    o = hT[:, 4 * hf:4 * hf + 4, q * P:(q + 1) * P]
                    b4 = b[:, :].rearrange("p (a b) -> p a b", a=4)
                    if shift is None:
                        V(tt(o, b4, inner(gain[:, 4 * hf:4 * hf + 4], P), ALU.mult), dve_free)
                    else:
                        V(tt(o, b4, inner(gain[:, 4 * hf:4 * hf + 4], P), ALU.mult))
                        V(tt(o, o, inner(shift[:, 4 * hf:4 * hf + 4], P), ALU.add), dve_free)

            def norm_x(buf, sq, gain):
                for q in range(NT):
                    V(dve.tensor_tensor_reduce(sq, x[:, q, :], x[:, q, :], 1.0, 0.0, ALU.mult, ALU.add,
                                               stat[:, q:q + 1]))
                scale_var(stat[:, 0:NT], D, EPS, var_ready)
                invert(stat[:, 0:NT])
                for q in range(NT + 1):
                    if q < NT:
                        V(ts(buf[:, q % 2, :], x[:, q, :], stat[:, q:q + 1], None, ALU.mult), tp_ready)
                    if q >= 1:
                        turned_in(q - 1, gain)

            dve.wait_ge(loaded, 16 * n_loads)
            V(dve.memset(eps_col, EPS))
            for j in range(2):
                V(dve.tensor_tensor_reduce(one_hot_free, rows(f"lambda_q{j + 1}"), rows(f"lambda_k{j + 1}"),
                                           1.0, 0.0, ALU.mult, ALU.add, lam[:, j:j + 1]))
            V(ts(rows("diff_out_norm_g"), rows("diff_out_norm_g"), 1.0 - LAM_INIT, None, ALU.mult), to_act)
            for g in range(3):
                n = min(P, N_COLS - g * P)
                V(dve.tensor_copy(col[:, g * P:g * P + n], take()[:, 0:n]), dve_free)
            V(dve.tensor_copy(rel_wide[0:BUCKETS, :, :],
                              rel_table[0:BUCKETS, :, None].to_broadcast([BUCKETS, DIFF_H, P])), to_pe)
            for h in range(DIFF_H):
                for a, n in ((0, 512), (512, 128)):
                    V(dve.tensor_copy(bias_head[:, h, a:a + n], take()[:, 0:n]), dve_free)
            wait_next(from_act)
            V(dve.tensor_copy(cond_b, inner(cond, P)), to_pe)
            V(ts(a_neg, a_neg, -1.0, None, ALU.mult))
            V(tt(lam[:, 2:3], lam[:, 0:1], lam[:, 1:2], ALU.subtract))
            V(ts(lam[:, 2:3], lam[:, 2:3], LAM_INIT, None, ALU.add))

            def modulation(c):
                b = take()
                if c in (4, 5, 10, 11):
                    o = gate_rows[:, c // 10, (c % 2) * 512:(c % 2) * 512 + 512]
                    V(stt(o, b[:, :], 1.0, o, ALU.add, ALU.add), dve_free)
                else:
                    j = {0: 0, 1: 1, 3: 2, 4: 3}[c // 2]
                    V(stt(mod[:, j, (c % 2) * 4:(c % 2) * 4 + 4], b[:, 0:4], float(j % 2),
                          column("b_ada_2")[:, 4 * c:4 * c + 4], ALU.add, ALU.add), dve_free)
            dve.wait_ge(x_loaded, 16)
            dve.wait_ge(line_out, 16)
            norm_x(xn, flat(S1["yT"])[:, 3 * D:4 * D], column("attn_norm_g"))
            lat = S1["lat"]
            dve.wait_ge(act_free, 4)
            for a, w, o in ((0, Q_RANK, 0), (Q_RANK, KV_RANK, 4)):
                sq = square[:, 0:NT * w].rearrange("p (g d) -> p g d", g=NT)
                V(tt(sq, lat[:, :, a:a + w], lat[:, :, a:a + w], ALU.mult))
                V(dve.tensor_reduce(stat8[:, o:o + 4], sq, AX.X, ALU.add))
                scale_var(stat8[:, o:o + 4], w, EPS, var_ready if o else None)
            invert(stat8[:, 0:8])
            V(tt(lat[:, :, 0:Q_RANK], lat[:, :, 0:Q_RANK], inner(stat8[:, 0:4], Q_RANK), ALU.mult))
            V(tt(lat[:, :, Q_RANK:384], lat[:, :, Q_RANK:384], inner(stat8[:, 4:8], KV_RANK), ALU.mult), to_pe)
            a = COLS["q_lat_norm_g"][0]
            for q in range(NT):
                b = take()
                V(tt(latT[:, :, q * P:(q + 1) * P], b[:, 0:384].rearrange("p (a b) -> p a b", a=3),
                     inner(col[:, a:a + 3], P), ALU.mult), dve_free)

            def rope(v, q, signal):
                c = over(const("cos", NT)[:, q, :], 8)
                s = over(const("sin", NT)[:, q, :], 8)
                t1, t2 = v[:, :, 64:80], v[:, :, 80:96]
                r = [rope_t[:, i, :, :] for i in range(4)]
                V(tt(r[0], t1, c, ALU.mult))
                V(tt(r[1], t2, s, ALU.mult))
                V(tt(r[2], t2, c, ALU.mult))
                V(tt(r[3], t1, s, ALU.mult))
                V(tt(t1, r[0], r[1], ALU.subtract))
                V(tt(t2, r[2], r[3], ALU.add), signal)

            def heads_free(u):
                if u >= 2 and ("heads", u - 2) in mark:
                    dve.wait_ge(act_full, mark["heads", u - 2])

            for q in range(NT):
                u = 2 * q
                heads_free(u)
                v = heads[:, 0, :]
                V(dve.tensor_copy(v[:, 0:512], take()[:, :]), dve_free)
                V(dve.tensor_copy(v[:, 512:768], take()[:, 0:256]), dve_free)
                v = v.rearrange("p (g d) -> p g d", g=8)
                norm_heads(v, v, 8, QK, rows("mla_q_norm_g"), square)
                rope(v, q, tp_ready)
                heads_free(u + 1)
                v = heads[:, 1, :].rearrange("p (g d) -> p g d", g=8)
                for a in range(2):
                    b4 = take()[:, :].rearrange("p (a b) -> p a b", a=4)
                    V(dve.tensor_copy(v[:, 4 * a:4 * a + 4, 0:64], b4[:, :, 0:64]))
                    V(dve.tensor_copy(S1["v"][:, q, 256 * a:256 * a + 256].rearrange("p (a b) -> p a b", a=4),
                                      b4[:, :, 64:128]), dve_free)
                V(dve.tensor_copy(v[:, :, 64:96], over(lat[:, q, 384:416], 8)))
                norm_heads(v, v, 8, QK, rows("mla_k_norm_g"), square)
                rope(v, q, tp_ready)
                for j in range(2):
                    modulation(2 * q + j)

            def attention(name, s, scale, bias_of, put, beside=None):
                def score(n):
                    h, q = units[n]
                    w = (q + 1) * P
                    if n >= 3:
                        dve.wait_ge(act_full, mark[name, "T", n - 3])
                    b = take()
                    V(stt(s[:, n % 3, 0:w], b[:, 0:w], scale, bias_of(q), ALU.mult, ALU.add), dve_free)
                    V(dve.tensor_reduce(neg_max[:, n % 4:n % 4 + 1], s[:, n % 3, 0:w], AX.X, ALU.max))
                    V(ts(neg_max[:, n % 4:n % 4 + 1], neg_max[:, n % 4:n % 4 + 1], -1.0, None, ALU.mult), s_ready)

                def share(n):
                    w = (units[n][1] + 1) * P
                    wait_next(e_ready)
                    r = row_sum[:, n % 4:n % 4 + 1]
                    V(dve.reciprocal(r, r))
                    V(ts(s[:, n % 3, 0:w], s[:, n % 3, 0:w], r, None, ALU.mult), p_ready)

                N = len(units)
                score(0)
                for n in range(N + 1):
                    if n + 1 < N:
                        score(n + 1)
                    if beside and n % 4 == 1 and n // 4 < 4:
                        beside(8 + n // 4)
                    if n < N:
                        share(n)
                    if n >= 5 and (n - 5) % 4 == 0:
                        put(take(), (n - 5) // 4)
                put(take(), 7)

            def put_mla(b, h):
                o = slice(64 * (h % 2), 64 * (h % 2) + 64)
                V(dve.tensor_copy(S1["yT"][o, h // 2, :], b[o, :]), dve_free)
            attention("mla", S1["s"], QK ** -0.5, lambda q: const("chunk_mask")[:, 384 - q * P:512], put_mla,
                      modulation)

            for q in range(NT):
                for j, (src, g) in enumerate(((S1["dq"], "diff_q_norm_g"), (S1["dk"], "diff_k_norm_g"))):
                    u = 8 + 2 * q + j
                    heads_free(u)
                    norm_heads(heads[:, j, 0:512].rearrange("p (g d) -> p g d", g=8),
                               src[:, q, :].rearrange("p (g d) -> p g d", g=8), 8, 64, rows(g), square, tp_ready)
            dve.wait_ge(bias_in, 16 * DIFF_H)
            V(tt(diff_bias, diff_bias, over(const("chunk_mask"), DIFF_H), ALU.add))
            s = S1["s"]

            def diff_score(n):
                h, q = diff_units[n]
                w = (q + 1) * P
                if n >= 2:
                    dve.wait_ge(act_full, mark["diff", "T", n - 2])
                for m in range(2):
                    j = 2 * (n % 2) + m
                    V(stt(s[:, j, 0:w], take()[:, 0:w], DIFF_QK ** -0.5, diff_bias[:, h, 384 - q * P:512],
                          ALU.mult, ALU.add), dve_free)
                    V(dve.tensor_reduce(neg_max[:, j:j + 1], s[:, j, 0:w], AX.X, ALU.max))
                    V(ts(neg_max[:, j:j + 1], neg_max[:, j:j + 1], -1.0, None, ALU.mult), s_ready)

            def diff_out(n):
                h, q = diff_units[n]
                V(dve.tensor_copy(diff_o[:, q, h * P:(h + 1) * P], take()[:, 0:P]), dve_free)

            diff_score(0)
            for n, (h, q) in enumerate(diff_units):
                if n + 1 < len(diff_units):
                    diff_score(n + 1)
                w, j = (q + 1) * P, 2 * (n % 2)
                wait_next(e_ready, 2)
                V(dve.reciprocal(row_sum[:, j:j + 2], row_sum[:, j:j + 2]))
                V(ts(s[:, j + 1, 0:w], s[:, j + 1, 0:w], row_sum[:, j + 1:j + 2], lam[:, 2:3], ALU.mult, ALU.mult))
                V(stt(s[:, j, 0:w], s[:, j, 0:w], row_sum[:, j:j + 1], s[:, j + 1, 0:w],
                      ALU.mult, ALU.subtract), p_ready)
                if n >= 1:
                    diff_out(n - 1)
            diff_out(len(diff_units) - 1)
            for q in range(NT):
                v = diff_o[:, q, :].rearrange("p (g d) -> p g d", g=4)
                norm_heads(v, v, 4, P, rows("diff_out_norm_g"), square, tp_ready)

            def add_to_x():
                for c in range(2):
                    for q in range(NT):
                        o = x[:, q, c * 512:(c + 1) * 512]
                        V(tt(o, o, take()[:, :], ALU.add), dve_free)
            add_to_x()

            norm_x(S2["xn"], flat(S2["conv"]), column("ffn_norm_g"))

            def conv(b, gp, dst, taps_, w_col, bias, signal):
                V(dve.tensor_copy(gp[:, taps_ - 1:taps_ - 1 + SEQ], b[:, :]), dve_free)
                if bias is None:
                    V(ts(dst, gp[:, 0:SEQ], w_col(0), None, ALU.mult))
                else:
                    V(ts(dst, gp[:, 0:SEQ], w_col(0), bias, ALU.mult, ALU.add))
                for j in range(1, taps_):
                    V(stt(dst, gp[:, j:j + SEQ], w_col(j), dst, ALU.mult, ALU.add),
                      signal if j == taps_ - 1 else None)

            V(dve.memset(S2["gpad"][:, :, 0:CONV1 - 1], 0.0))
            for a, n in ff_chunks:
                ms = range(a // P, (a + n) // P)
                for m in ms:
                    if m >= 2:
                        dve.wait_ge(silu_out, m - 1)
                    conv(take(), S2["gpad"][:, m % 2, :], S2["conv"][:, m % 2, :], CONV1,
                         lambda j: column("conv_w", j * FT + m), column("conv_b", m), silu_in)
                for m in ms:
                    dve.wait_ge(silu_out, m + 1)
                    V(tt(S2["act"][:, m, :], take()[:, :], S2["act"][:, m, :], ALU.mult), dve_free)
            add_to_x()
            norm_x(S2["xn"], flat(S2["conv"]), column("ple_norm_g"))
            for q in range(NT):
                b = take()
                V(dve.tensor_copy(S2["pleT"][:, :, q * P:(q + 1) * P],
                                  b[:, 0:256].rearrange("p (a b) -> p a b", a=2)), dve_free)
            for i in range(8):
                c, q = divmod(i, NT)
                b = take()
                wait_next(sig_out)
                V(tt(S2["tmp"], b[:, :], S2["sig"][:, i % 2, :], ALU.mult), dve_free)
                o = x[:, q, c * 512:(c + 1) * 512]
                V(tt(o, o, S2["tmp"], ALU.add), sig_used)

            for q in range(NT):
                turned_in(q, mod[:, 1, :], mod[:, 0, :])
            sm = S3["small"]
            for q in range(NT):
                V(dve.tensor_copy(sm[:, q, :], take()[:, 0:344]), dve_free)
            sq = S3["v"][:, 0, :].rearrange("p (g d) -> p g d", g=NT)
            V(tt(sq, sm[:, :, 0:256], sm[:, :, 0:256], ALU.mult))
            V(dve.tensor_reduce(stat[:, 0:NT], sq, AX.X, ALU.add))
            scale_var(stat[:, 0:NT], KV_LAT, EPS, var_ready)
            invert(stat[:, 0:NT])
            V(tt(sm[:, :, 0:256], sm[:, :, 0:256], inner(stat[:, 0:NT], 256), ALU.mult))
            V(ts(w_idx, sm[:, :, 320:328], (IDX_H ** -0.5) * (IDX_D ** -0.5), None, ALU.mult))
            u, au = sm[:, :, 256:264], sm[:, :, 264:272]
            V(tt(u, sm[:, :, 328:336], over(rows("dt_bias_2"), NT), ALU.add))
            V(ts(au, u, -1.0, None, ALU.mult))
            V(tt(au, au, u, ALU.max), to_act)
            wait_next(from_act)
            V(stt(gdec, u, 0.0, au, ALU.max, ALU.add))
            V(tt(gdec, gdec, over(a_neg, NT), ALU.mult), to_pe)
            V(dve.tensor_copy(gsum.rearrange("p a b -> p (a b)"), take()[:, 0:32]), dve_free)
            V(ts(eg, gsum, 1.0, None, ALU.mult), to_act)
            wait_next(from_act)
            V(tt(beg, beta, eg, ALU.mult))
            for q in range(NT):
                b = take()
                V(tt(S3["kvT"][:, :, q * P:(q + 1) * P], b[:, 0:256].rearrange("p (a b) -> p a b", a=2),
                     inner(column("kv_norm_g_2"), P), ALU.mult), dve_free)
            for q in (1, 2, 3):
                w = (q + 1) * P
                sc, tm = S3["score"][:, 0:w], S3["s"][:, 0, 0:w]
                for h in range(IDX_H):
                    V(ts(sc if h == 0 else tm, take()[:, 0:w], 0.0, w_idx[:, q, h:h + 1], ALU.max, ALU.mult),
                      dve_free)
                    if h:
                        V(tt(sc, sc, tm, ALU.add))
                V(tt(sc, sc, const("causal_mask")[:, 384 - q * P:512], ALU.add))
                for _ in range(TOPK // 8):
                    V(dve.max(top8, sc))
                    V(dve.match_replace(sc, top8, sc, BIG))
                V(ts(S3["sel"][:, q - 1, 0:w], sc, BIG / 2, NEG, ALU.is_gt, ALU.mult))

            def put_dsa(b, h):
                V(dve.tensor_copy(S3["qT"][:, h, :], b[:, :]), dve_free)
            attention("dsa", S3["s"], DH ** -0.5,
                      lambda q: const("causal_mask")[:, 384 - q * P:512] if q == 0
                      else S3["sel"][:, q - 1, 0:(q + 1) * P], put_dsa)

            B = S4
            for g in range(2):
                gh = slice(g * HG, g * HG + HG)

                def result_norm(g, ch, step):
                    if step == 0:
                        sq = result_sq.rearrange("p (g d) -> p g d", g=HG)
                        V(tt(sq, result, result, ALU.mult))
                    if step == 1:
                        sq = result_sq.rearrange("p (g d) -> p g d", g=HG)
                        V(dve.tensor_reduce(stat8[:, 0:HG], sq, AX.X, ALU.add))
                        scale_var(stat8[:, 0:HG], P, EPS, var_ready)
                    if step == 2:
                        invert(stat8[:, 0:HG])
                    if step == 3:
                        V(tt(result, result, inner(stat8[:, 0:HG], P), ALU.mult))
                    if step == 4:
                        V(tt(result, result, over(rows("dn_norm_g_2"), HG), ALU.mult))
                    if step == 5:
                        V(tt(result, result, B["z"][:, ch, :].rearrange("p (a b) -> p a b", a=HG), ALU.mult),
                          tp_ready)
                if g:
                    dve.wait_ge(act_full, mark["result", g - 1])
                V(dve.memset(B["gpad"][:, :, 0:CONV2 - 1], 0.0))
                for part, name in enumerate("qkv"):
                    for i in range(4):
                        if part:
                            before = B["qkv"[part - 1]][:, i, :]
                            dve.wait_ge(silu_out, FT + 12 * g + 4 * (part - 1) + i + 1)
                            sq = flat(B[("tmp", "decay")[i % 2]])
                            V(tt(sq, before, before, ALU.mult), to_pe)
                        m = part * 8 + g * 4 + i
                        conv(take(), B["gpad"][:, i % 2, :], B[name][:, i, :], CONV2,
                             lambda j: column("conv_w_2", j * 24 + m), None, silu_in)
                        if part:
                            wait_next(from_act)
                            V(dve.reciprocal(sq, sq))
                            V(stt(before, before, DH ** -0.5 if part == 1 else 1.0, sq, ALU.mult, ALU.mult))

                def decays_spread(ch):
                    V(dve.tensor_copy(B["tmp"], inner(gdec[:, ch, gh], P)), to_pe)

                def decays_differ(ch):
                    b = take()[:, :].rearrange("p (a b) -> p a b", a=HG)
                    V(tt(B["decay"], inner(gsum[:, ch, gh], P), b, ALU.subtract))
                    V(dve.tensor_copy(g_last[ch % 2], b[:, :, P - 1]), dve_free)

                def decays_bound(ch):
                    V(tt(tail, g_last[ch % 2], gsum[:, ch, gh], ALU.subtract))
                    V(ts(B["decay"], B["decay"], 0.0, None, ALU.min), to_act)

                def decays_end():
                    wait_next(from_act)
                    V(tt(B["decay"], B["decay"], over(const("lower"), HG), ALU.mult))

                V(dve.memset(B["state"], 0.0))
                decays_spread(0)
                decays_differ(0)
                decays_bound(0)
                decays_end()
                for ch in range(NT):
                    b = take()[:, :].rearrange("p (a b) -> p a b", a=HG)
                    V(tt(B["A"], b, B["decay"], ALU.mult), dve_free)
                    V(tt(B["A"], B["A"], inner(beta[:, ch, gh], P), ALU.mult), to_pe)
                    V(tt(B["X"], B["A"], over(const("level0"), HG), ALU.mult))
                    V(tt(B["X"], over(ident, HG), B["X"], ALU.subtract))
                    dve.wait_ge(act_free, mark["AT", g, ch])
                    V(tt(B["XT"], B["AT"], over(const("level0_t"), HG), ALU.mult))
                    V(tt(B["XT"], over(ident, HG), B["XT"], ALU.subtract), to_pe)
                    b = take()[:, :].rearrange("p (a b) -> p a b", a=HG)
                    V(tt(B["qk"], b, B["decay"], ALU.mult))
                    V(dve.tensor_copy(stat8[:, 14:15], eps_col), dve_free)
                    V(dve.tensor_copy(stat8[:, 14:15], eps_col), to_pe)
                    b = take()[:, :].rearrange("p (a b) -> p a b", a=HG)
                    V(tt(B["k_tail"], b, inner(tail, P), ALU.mult))
                    V(tt(B["k_bg"], b, inner(beg[:, ch, gh], P), ALU.mult), dve_free)
                    b = take()[:, :].rearrange("p (a b) -> p a b", a=HG)
                    V(tt(B["v_b"], b, inner(beta[:, ch, gh], P), ALU.mult), dve_free)
                    for lv in range(6):
                        for half in HALVES:
                            b = take()[:, 0:2 * P].rearrange("p (a b) -> p a b", a=2)
                            o = B["X" if lv < 5 else "XT"][:, half[0]:half[-1] + 1, :]
                            V(tt(o, o, b, ALU.subtract), dve_free)
                        if ch:
                            result_norm(g, ch - 1, lv)
                        if lv == 0 and ch < NT - 1:
                            decays_spread(ch + 1)
                        if lv == 2 and ch < NT - 1:
                            decays_differ(ch + 1)
                    if ch < NT - 1:
                        decays_bound(ch + 1)
                    b = take()[:, :].rearrange("p (a b) -> p a b", a=HG)
                    V(tt(B["A"], b, inner(eg[:, ch, gh], P), ALU.mult), dve_free)
                    b = take()[:, :].rearrange("p (a b) -> p a b", a=HG)
                    V(tt(B["v_b"], B["u"], b, ALU.subtract), dve_free)
                    if ch < NT - 1:
                        decays_end()
                    b = take()[:, :].rearrange("p (a b) -> p a b", a=HG)
                    V(tt(result, B["A"], b, ALU.add), dve_free)
                    b = take()[:, :].rearrange("p (a b) -> p a b", a=HG)
                    V(tt(B["state"], B["state"], inner(g_last[ch % 2], P), ALU.mult))
                    V(tt(B["state"], B["state"], b, ALU.add), dve_free)
                for step in range(6):
                    result_norm(g, NT - 1, step)
            for c in range(2):
                for part in range(2):
                    for m in range(4):
                        b = take()
                        wait_next(sig_out)
                        o = S5["mg"][:, 4 * c + m, :]
                        if part == 0:
                            V(tt(o, b[:, :], S5["sig"][:, m, :], ALU.mult), dve_free)
                        else:
                            V(tt(S5["tmp"], b[:, :], S5["sig"][:, m, :], ALU.mult))
                            V(tt(o, o, S5["tmp"], ALU.add), dve_free)
            ALPHA = 2.0 ** 0.25

            def spread_of(q, sq):
                V(dve.tensor_reduce(stat[:, q:q + 1], x[:, q, :], AX.X, ALU.add))
                V(ts(stat[:, q:q + 1], stat[:, q:q + 1], -1.0 / D, None, ALU.mult))
                V(ts(x[:, q, :], x[:, q, :], stat[:, q:q + 1], None, ALU.add))
                V(dve.tensor_tensor_reduce(sq, x[:, q, :], x[:, q, :], 1.0, 0.0, ALU.mult, ALU.add,
                                           stat[:, 4 + q:5 + q]))
                scale_var(stat[:, 4 + q:5 + q], D, LN_EPS, var_ready)

            def normalised(q, g, b, signal):
                invert(stat[:, 4 + q:5 + q])
                V(stt(x[:, q, :], x[:, q, :], stat[:, 4 + q:5 + q], g, ALU.mult, ALU.mult))
                V(tt(x[:, q, :], x[:, q, :], b, ALU.add), signal)

            dve.wait_ge(ln_loaded, 32)
            for c in range(2):
                for q in range(NT):
                    o = x[:, q, c * 512:(c + 1) * 512]
                    V(tt(S5["tmp"], take()[:, :], gate_rows[:, 0, c * 512:(c + 1) * 512], ALU.mult), dve_free)
                    V(stt(o, o, ALPHA, S5["tmp"], ALU.mult, ALU.add))
                    if c == 1:
                        spread_of(q, S5["sq"])
                        if q:
                            normalised(q - 1, S5["ln"][:, 0, :], S5["ln"][:, 1, :], to_pe)
            normalised(NT - 1, S5["ln"][:, 0, :], S5["ln"][:, 1, :], to_pe)
            for q in range(NT):
                turned_in(q, mod[:, 3, :], mod[:, 2, :])
            for q in range(NT):
                V(dve.tensor_copy(logit[:, q, :], take()[:, 0:36]), dve_free)

            def first_max(hot_, v, m, width):
                V(dve.tensor_reduce(m, v, AX.X, ALU.max))
                V(tt(hot_, v, inner(m, width), ALU.is_equal))
                V(tt(hot_, hot_, over(rev[:, 0:width], NT), ALU.mult))
                V(dve.tensor_reduce(r_t, hot_, AX.X, ALU.max))
                V(tt(hot_, hot_, inner(r_t, width), ALU.is_equal))

            V(ts(rev, const("iota")[:, 0:8], -1.0, 16.0, ALU.mult, ALU.add))
            V(dve.tensor_copy(e_tmp[:, :, 0:4], logit[:, :, 0:4]))
            first_max(g_hot, e_tmp[:, :, 0:4], r_m1, 4)
            V(tt(e_tmp[:, :, 0:4], e_tmp[:, :, 0:4], inner(r_m1, 4), ALU.subtract), to_act)
            wait_next(from_act)
            V(dve.tensor_reduce(r_m1, e_tmp[:, :, 0:4], AX.X, ALU.add))
            V(dve.reciprocal(gate_of[0], r_m1))
            for j in range(GROUPS):
                lg = logit[:, :, 4 + 8 * j:12 + 8 * j]
                hj = inner_at(g_hot[:, :, j:j + 1], 8)
                V(tt(e_tmp if j else e_in, lg, hj, ALU.mult))
                if j:
                    V(tt(e_in, e_in, e_tmp, ALU.add))
            first_max(hot[0], e_in, r_m1, 8)
            V(stt(e_in, hot[0], -1e30, e_in, ALU.mult, ALU.add))
            first_max(hot[1], e_in, r_m2, 8)
            V(tt(r_m2, r_m2, r_m1, ALU.subtract), to_act)
            wait_next(from_act)
            V(ts(r_m1, r_m2, 1.0, None, ALU.add))
            V(dve.reciprocal(r_m1, r_m1))
            V(tt(gate_of[0], gate_of[0], r_m1, ALU.mult))
            V(tt(gate_of[1], gate_of[0], r_m2, ALU.mult))
            for j in range(2):
                for k in range(GROUPS):
                    V(tt(choice[j][:, :, 8 * k:8 * k + 8], hot[j], inner_at(g_hot[:, :, k:k + 1], 8), ALU.mult))
            V(tt(both, choice[0], choice[1], ALU.add), to_pe)
            V(dve.tensor_copy(rank.rearrange("p a b -> p (a b)"), take()[:, 0:P]), dve_free)
            V(dve.tensor_copy(b_at, take()[:, 0:32]), dve_free)
            V(ts(nb, b_at, 0.0, None, ALU.is_gt))
            for k in range(1, NT):
                V(ts(b_end, b_at, float(k * P), None, ALU.is_gt))
                V(tt(nb, nb, b_end, ALU.add))
            V(dve.tensor_tensor_scan(b_end, const("ones")[:, 0:32], nb, 0.0, ALU.mult, ALU.add))
            V(tt(ebw, over(b_end, BLOCKS), inner(const("iota")[:, 0:BLOCKS], 32), ALU.is_le))
            V(dve.tensor_reduce(eb_f, ebw, AX.X, ALU.add))
            V(ts(eb_f, eb_f, float(EXPERTS - 1), None, ALU.min))
            V(dve.tensor_copy(used_i, b_end[:, EXPERTS - 1:EXPERTS]))
            V(dve.tensor_copy(block_expert, eb_f), experts_known)
            V(tt(b_at, b_end, nb, ALU.subtract))
            V(ts(b_at, b_at, float(P), None, ALU.mult))
            for j in range(2):
                V(tt(wide, rank, over(b_at, NT), ALU.add))
                V(tt(wide, wide, choice[j], ALU.mult))
                V(dve.tensor_reduce(dest[j], wide, AX.X, ALU.add))
                V(dve.tensor_copy(dest_i[j], dest[j]))
            N2 = 2 * NT
            V(tt(ge, over(const("block_start"), N2), inner(dest_all, BLOCKS + 1), ALU.is_le))
            V(dve.tensor_reduce(count, ge[:, :, 1:BLOCKS + 1], AX.X, ALU.add))
            V(tt(in_block, ge[:, :, 0:BLOCKS], ge[:, :, 1:BLOCKS + 1], ALU.subtract))
            for j in range(2):
                o = in_block[:, j * NT:(j + 1) * NT, :]
                V(tt(o, o, inner(const("token"), BLOCKS), ALU.mult))
            V(stt(place_in, count, -float(P), dest_all, ALU.mult, ALU.add))
            V(tt(slot_hot, over(const("iota"), N2), inner(place_in, P), ALU.is_equal), to_pe)
            V(dve.tensor_copy(slot_token, take()[:, 0:BLOCKS]), tables_ready)
            V(dve.tensor_copy(stat8[:, 14:15], eps_col), dve_free)

            def x_in(n, s):
                for hf in range(2):
                    dve.wait_ge(xt_full, 2 * n + hf + 1)
                    o = xgT[:, s, 4 * hf:4 * hf + 4, :]
                    b4 = banks[hf][:, :].rearrange("p (a b) -> p a b", a=4)
                    tt(o, b4, inner(mod[:, 3, 4 * hf:4 * hf + 4], P), ALU.mult).then_inc(x_scaled, 1)
                    dve.wait_ge(x_scaled, 2 * n + hf + 1)
                    tt(o, o, inner(mod[:, 2, 4 * hf:4 * hf + 4], P), ALU.add).then_inc(xt_taken, 1)

            def block_out(i, s, first=False, last=False):
                n = 2 * i + s
                dve.wait_ge(silu_done, n + 1)
                dve.wait_ge(up_full, n + 1)
                tt(hb[:, s, :], hb[:, s, :], banks[3][:, :], ALU.mult).then_inc(hb_ready, 1)
                if not last:
                    x_in(n + 1, 1 - s)
                dve.wait_ge(y_full, 2 * n + 1)
                if not first:
                    dve.wait_ge(y_stored[s], 16 * i)
                dve.tensor_copy(yb[:, s, 0:512], banks[5][:, :]).then_inc(y0_taken, 1)

            x_in(0, 0)
            for s in range(2):
                block_out(0, s, first=True)
            with dve.Fori(1, PAIRS - 1) as i:
                for s in range(2):
                    block_out(i, s)
            for s in range(2):
                block_out(PAIRS - 1, s, last=(s == 1))
            dve.wait_ge(tables_ready, 1)
            with dve.If(blocks_used(dve) > 2 * PAIRS):
                x_in(2 * PAIRS, 0)
                with dve.Fori(PAIRS, ALL_PAIRS - 1) as i:
                    for s in range(2):
                        block_out(i, s)
                for s in range(2):
                    block_out(ALL_PAIRS - 1, s, last=(s == 1))
            dve.wait_ge(ln2_loaded, 32)
            dve.wait_ge(rows_stored, 1)
            for q in range(NT):
                dve.wait_ge(y_back[q], 32)
                y = yb[:, 0, :]
                V(ts(y, y_of[:, 2 * q, :], gate_of[0][:, q:q + 1], None, ALU.mult))
                V(stt(y, y_of[:, 2 * q + 1, :], gate_of[1][:, q:q + 1], y, ALU.mult, ALU.add))
                V(tt(y, y, gate_rows[:, 1, :], ALU.mult))
                V(stt(x[:, q, :], x[:, q, :], ALPHA, y, ALU.mult, ALU.add))
                spread_of(q, yb[:, 1, :])
                if q:
                    normalised(q - 1, ln_rows[:, 0, :], ln_rows[:, 1, :], x_done)
            normalised(NT - 1, ln_rows[:, 0, :], ln_rows[:, 1, :], x_done)

        @block.scalar
        def _(act):
            n_of = Counter()

            def C(ins, signal=None):
                signal = act_step if signal is None else signal
                ins.then_inc(signal, 1)
                n_of[signal] += 1
                act.wait_ge(signal, n_of[signal])

            def take():
                n = n_of["taken"]
                n_of["taken"] += 1
                act.wait_ge(act_full, n + 1)
                return banks[4 + n % 4]

            def wait_next(s, n=1):
                n_of["w", s] += n
                act.wait_ge(s, n_of["w", s])

            def root(s):
                wait_next(var_ready)
                C(act.activation(s, s, ACT.Sqrt), std_ready)

            def copy_out(dst, src):
                C(act.activation(dst, src, ACT.Copy), act_free)

            act.wait_ge(loaded, 16 * n_loads)
            wait_next(to_act)
            C(act.activation(lam[:, 0:2], lam[:, 0:2], ACT.Exp))
            C(act.activation(a_neg, rows("a_log_2"), ACT.Exp))
            act.wait_ge(dve_free, 3)
            C(act.activation(cond, column("c_2"), ACT.Silu), from_act)
            root(stat[:, 0:NT])
            for name, w in (("lat", LAT), ("dq", 512), ("dk", 512), ("dv", 512)):
                for q in range(NT):
                    copy_out(S1[name][:, q, :], take()[:, 0:w])
            root(stat8[:, 0:8])
            for q in range(NT):
                for dst in (hT, S1["kT"]):
                    root(stat8[:, 0:8])
                    for a in range(2):
                        copy_out(dst[0:QK, 4 * a:4 * a + 4, q * P:(q + 1) * P],
                                 take()[0:QK, :].rearrange("p (a b) -> p a b", a=4))

            def attention(name, s, pT):
                nbuf = pT.shape[1]

                def exp(n):
                    w = (units[n][1] + 1) * P
                    wait_next(s_ready)
                    v = s[:, n % 3, 0:w]
                    C(act.activation(v, v, ACT.Exp, bias=neg_max[:, n % 4:n % 4 + 1],
                                     accum_out=row_sum[:, n % 4:n % 4 + 1]), e_ready)

                def turned(n):
                    h, q = units[n]
                    if h >= nbuf and q == 0:
                        act.wait_ge(dve_full, mark[name, "PV", h - nbuf])
                    copy_out(pT[:, h % nbuf, 0:q + 1, q * P:(q + 1) * P],
                             take()[:, 0:(q + 1) * P].rearrange("p (a b) -> p a b", a=q + 1))
                N = len(units)
                for n in range(N + 1):
                    if n < N:
                        exp(n)
                    if n >= 1:
                        turned(n - 1)

            attention("mla", S1["s"], S1["pT"])
            for q in range(NT):
                for j in range(2):
                    root(stat8[:, 0:8])
                    copy_out(hT[:, 4 * j:4 * j + 4, q * P:(q + 1) * P],
                             take()[:, :].rearrange("p (a b) -> p a b", a=4))
            for n in range(len(diff_units) + 1):
                if n < len(diff_units):
                    w = (diff_units[n][1] + 1) * P
                    for m in range(2):
                        j = 2 * (n % 2) + m
                        wait_next(s_ready)
                        v = S1["s"][:, j, 0:w]
                        C(act.activation(v, v, ACT.Exp, bias=neg_max[:, j:j + 1],
                                         accum_out=row_sum[:, j:j + 1]), e_ready)
                if n >= 1:
                    q = diff_units[n - 1][1]
                    if n >= 3:
                        act.wait_ge(dve_full, mark["diff", "PV", n - 3])
                    copy_out(S1["pT"][:, (n - 1) % 2, 0:q + 1, 0:P],
                             take()[:, 0:(q + 1) * P].rearrange("p (a b) -> p a b", a=q + 1))
            for q in range(NT):
                root(stat8[:, 0:4])
                copy_out(S1["yT"][:, 4:8, q * P:(q + 1) * P], take()[:, :].rearrange("p (a b) -> p a b", a=4))
            root(stat[:, 0:NT])
            for m in range(FT):
                wait_next(silu_in)
                C(act.activation(S2["act"][:, m, :], S2["conv"][:, m % 2, :], ACT.Silu), silu_out)
            root(stat[:, 0:NT])
            for i in range(8):
                if i >= 2:
                    act.wait_ge(sig_used, i - 1)
                C(act.activation(S2["sig"][:, i % 2, :], take()[:, :], ACT.Sigmoid), act_free)
                C(act.activation(stat8[:, 15:16], eps_col, ACT.Copy), sig_out)
            copy_out(S3["k_idx"], take()[:, :])
            for m in range(4):
                copy_out(S3["q_idx"][:, m, :], take()[:, :])
            root(stat[:, 0:NT])
            wait_next(to_act)
            sm = S3["small"]
            C(act.activation(beta, sm[:, :, 336:344], ACT.Sigmoid))
            au = sm[:, :, 264:272]
            C(act.activation(au, au, ACT.Exp, scale=-1.0))
            C(act.activation(au, au, ACT.Ln, bias=const("ones")[:, 0:1]), from_act)
            wait_next(to_act)
            C(act.activation(eg, eg, ACT.Exp), from_act)
            for m in range(8):
                copy_out(S3["qT"][:, m, :], take()[:, :])
            for m in range(8):
                copy_out(S3["kT"][:, m, :], take()[:, :])
            for q in range(NT):
                for hf in range(2):
                    copy_out(S3["v"][:, q, hf * 512:(hf + 1) * 512], take()[:, :])
            attention("dsa", S3["s"], S3["pT"])
            B = S4
            for g in range(2):
                for part, name in enumerate("qkv"):
                    for i in range(4):
                        wait_next(silu_in)
                        C(act.activation(B[name][:, i, :], B[name][:, i, :], ACT.Silu), silu_out)
                        if part:
                            C(act.activation(flat(B[("tmp", "decay")[i % 2]]), take()[:, :], ACT.Sqrt,
                                             bias=eps_col), act_free)
                            C(act.activation(stat8[:, 15:16], eps_col, ACT.Copy), from_act)
                for q in range(NT):
                    C(act.activation(B["z"][:, q, :], take()[:, :], ACT.Silu), act_free)

                def four_out(dst):
                    copy_out(dst, take()[:, :].rearrange("p (a b) -> p a b", a=HG))

                def result_out(ch):
                    four_out(B["dnT"][:, g * HG:(g + 1) * HG, ch * P:(ch + 1) * P])
                def decays(ch):
                    wait_next(to_act)
                    C(act.activation(tail, tail, ACT.Exp))
                    C(act.activation(g_last[ch % 2], g_last[ch % 2], ACT.Exp))
                    C(act.activation(B["decay"], B["decay"], ACT.Exp), from_act)
                decays(0)
                for ch in range(NT):
                    four_out(B["AT"])
                    for lv in range(6):
                        for half in HALVES:
                            hs = slice(half[0], half[-1] + 1)
                            for name in (("XT", "u") if lv else ("u",)):
                                copy_out(B[name][:, hs, :], take()[:, 0:2 * P].rearrange("p (a b) -> p a b", a=2))
                        if lv == 0:
                            four_out(B["qkT"])
                        if lv == 1 and ch:
                            root(stat8[:, 0:HG])
                    if ch:
                        result_out(ch - 1)
                    four_out(B["u"])
                    four_out(B["wT"])
                    if ch < NT - 1:
                        decays(ch + 1)
                root(stat8[:, 0:HG])
                result_out(NT - 1)
            for c in range(2):
                for part in range(2):
                    for m in range(4):
                        j = 2 * c + part
                        if j:
                            act.wait_ge(dve_free, mark["branch", j - 1] - 3 + m)
                        C(act.activation(S5["sig"][:, m, :], take()[:, :], ACT.Sigmoid), act_free)
                        C(act.activation(stat8[:, 15:16], eps_col, ACT.Copy), sig_out)
            for q in range(NT):
                root(stat[:, 4 + q:5 + q])
            wait_next(to_act)
            C(act.activation(e_tmp[:, :, 0:4], e_tmp[:, :, 0:4], ACT.Exp), from_act)
            wait_next(to_act)
            C(act.activation(r_m2, r_m2, ACT.Exp), from_act)

            def expert_block(i, s, first=False):
                n = 2 * i + s
                act.wait_ge(gate_full, n + 1)
                act.activation(hb[:, s, :], banks[2][:, :], ACT.Silu).then_inc(silu_done, 1)
                act.wait_ge(ht_full, n + 1)
                act.activation(hbT[:, s, :, :].rearrange("p a b -> p (a b)"), banks[4][:, :], ACT.Copy)\
                    .then_inc(ht_taken, 1)
                act.wait_ge(y_full, 2 * n + 2)
                if not first:
                    act.wait_ge(y_stored[s], 16 * i)
                act.activation(yb[:, s, 512:D], banks[6][:, :], ACT.Copy).then_inc(y1_taken, 1)
                act.wait_ge(y0_taken, n + 1)
                act.wait_ge(y1_taken, n + 1)
                act.dma_start(y_rows[bass.ds(n * P, P), :], yb[:, s, :]).then_inc(y_stored[s], 16)

            act.wait_ge(tables_ready, 1)
            act.wait_ge(zeros_stored, 16)
            for s in range(2):
                expert_block(0, s, first=True)
            with act.Fori(1, PAIRS) as i:
                for s in range(2):
                    expert_block(i, s)
            for s in range(2):
                act.wait_ge(y_stored[s], 16 * PAIRS)
            with act.If(blocks_used(act) > 2 * PAIRS):
                with act.Fori(PAIRS, ALL_PAIRS) as i:
                    for s in range(2):
                        expert_block(i, s)
                for s in range(2):
                    act.wait_ge(y_stored[s], 16 * ALL_PAIRS)
            C(act.activation(stat8[:, 15:16], eps_col, ACT.Copy), rows_stored)
            for q in range(NT):
                root(stat[:, 4 + q:5 + q])

        @block.gpsimd
        def _(pool):
            n_of = Counter()
            pool.wait_ge(dve_free, 3 + 2 * DIFF_H)
            pool.dma_start(bias_line, bias_head).then_inc(line_out, 16)
            pool.wait_ge(line_out, 16)
            pool.wait_ge(dve_full, mark["mla", "PV", 7])
            for h in range(DIFF_H):
                src = bass.AP(tensor=bias_line.tensor, offset=h * 640 + 127,
                              ap=[[DIFF_H * 640 - 1, P], [1, 512]])
                pool.dma_start(diff_bias[:, h, :], src).then_inc(bias_in, 16)
            pool.wait_ge(dve_free, mark["attention added"])
            pool.dma_start(S2["p"], t["p"][0, 0].rearrange("(q p) n -> p q n", p=P)).then_inc(p_loaded, 16)
            for g in range(2):
                for ch in range(NT):
                    pool.wait_ge(act_free, mark["AT", g, ch])
                    for lv in range(6):
                        if lv >= 2:
                            pool.wait_ge(act_full, mark["T", g, ch, lv - 2])
                        mask = const("levels_t", 6)[:, lv, :][:, None, :].to_broadcast([P, HG, P])
                        pool.tensor_tensor(S4[f"L{lv % 2}"], S4["AT"], mask, ALU.mult).then_inc(from_pool, 1)
            pool.wait_ge(dve_full, mark["branch", 0])
            for j, name in enumerate(("ln_g_2", "ln_b_2")):
                src = bass.AP(tensor=t[name].tensor, offset=0, ap=[[0, P], [1, D]])
                pool.dma_start(S5["ln"][:, j, :], src).then_inc(ln_loaded, 16)
            pool.wait_ge(to_pe, mark["x normalised"])
            pool.dma_start(w_route[:, :, 0:4], w3(W["w_route_grp_2"])).then_inc(route_loaded, 16)
            pool.dma_start(w_route[:, :, 4:36], w3(W["w_route_exp_2"])).then_inc(route_loaded, 16)
            pool.dma_start(x_rows.rearrange("(q p) n -> p q n", p=P), x).then_inc(x_spilled, 16)
            for j, name in enumerate(("ln_g_2", "ln_b_2")):
                src = bass.AP(tensor=t[name].tensor, offset=D, ap=[[0, P], [1, D]])
                pool.dma_start(ln_rows[:, j, :], src).then_inc(ln2_loaded, 16)

            pool.memset(zeros, 0.0).then_inc(from_pool, 1)
            pool.wait_ge(from_pool, 6 * 2 * NT + 1)
            pool.dma_start(y_rows[2 * PAIRS * P:, :].rearrange("(b p) n -> p b n", p=P),
                           zeros[:, None, :].to_broadcast([P, BLOCKS - 2 * PAIRS, D])).then_inc(zeros_stored, 16)

            pool.memset(pool_note, 0.0).then_inc(from_pool, 1)

            def gather(i, s, first=False):
                n = 2 * i + s
                if not first:
                    pool.wait_ge(x_gathered[s], 16 * i)
                    pool.wait_ge(xt_full, 2 * n - 2)
                pool.tensor_copy(gather_i[:, s:s + 1], slot_token[:, bass.ds(n, 1)]).then_inc(idx_ready, 1)
                pool.wait_ge(idx_ready, n + 1)
                pool.tensor_tensor(pool_note[:, 0:1], pool_note[:, 1:2], pool_note[:, 1:2], ALU.add)
                pool.indirect_dma_start(out=xg[:, s, :], out_offset=None, in_=x_rows,
                                        in_offset=bass.IndirectOffsetOnAxis(ap=gather_i[:, s:s + 1], axis=0))\
                    .then_inc(x_gathered[s], 16)

            pool.wait_ge(x_spilled, 16)
            pool.wait_ge(from_pool, 6 * 2 * NT + 2)
            pool.wait_ge(tables_ready, 1)
            for s in range(2):
                gather(0, s, first=True)
            with pool.Fori(1, PAIRS) as i:
                for s in range(2):
                    gather(i, s)
            with pool.If(blocks_used(pool) > 2 * PAIRS):
                with pool.Fori(PAIRS, ALL_PAIRS) as i:
                    for s in range(2):
                        gather(i, s)
            pool.wait_ge(rows_stored, 1)
            for q in range(NT):
                for j in range(2):
                    pool.indirect_dma_start(out=y_of[:, 2 * q + j, :], out_offset=None, in_=y_rows,
                                            in_offset=bass.IndirectOffsetOnAxis(ap=dest_i[j][:, q:q + 1], axis=0))\
                        .then_inc(y_back[q], 16)

        @block.sync
        def _(sp):
            for dst, src in first_loads:
                sp.dma_start(dst, src).then_inc(loaded, 16)
            sp.dma_start(x, t["x"][0].rearrange("(q p) n -> p q n", p=P)).then_inc(x_loaded, 16)
            for n, (_, loads) in enumerate(items):
                if n == 4:
                    sp.wait_ge(line_out, 16)
                    sp.dma_start(wq, w3(W["w_uq"])).then_inc(expand_loaded, 16)
                    sp.dma_start(wkv, w3(W["w_ukv"])).then_inc(expand_loaded, 16)
                if n >= SLOTS:
                    sp.wait_ge(*item_done[n - SLOTS])
                for dst, src in loads:
                    sp.dma_start(dst, src).then_inc(w_full[n % SLOTS], 16)

            def load(i, s, first):
                n = 2 * i + s
                e = sp.value_load(block_expert[0:1, bass.ds(n, 1)], min_val=0, max_val=EXPERTS - 1)
                for dst, w, sem_, used_ in ((wg_s[s], "w_gate_2", wg_in[s], gate_full),
                                            (wu_s[s], "w_up_2", wu_in[s], up_full),
                                            (wd_s[s], "w_down_2", wd_in[s], y_full)):
                    if first and s == 0 and w == "w_down_2":
                        sp.wait_ge(x_gathered[1], 16)
                    if not first:
                        sp.wait_ge(used_, 2 * n - 2 if w == "w_down_2" else n - 1)
                    src = t[w][0][bass.ds(e, 1), :, :].rearrange("e (k p) n -> p (e k) n", p=P)
                    sp.dma_start(dst, src).then_inc(sem_, 16)
            sp.wait_ge(experts_known, 1)
            load(0, 0, True)
            load(0, 1, True)
            with sp.Fori(1, PAIRS) as i:
                load(i, 0, False)
                load(i, 1, False)
            with sp.If(blocks_used(sp) > 2 * PAIRS):
                with sp.Fori(PAIRS, ALL_PAIRS) as i:
                    load(i, 0, False)
                    load(i, 1, False)
            for q in range(NT):
                sp.wait_ge(x_done, q + 1)
                sp.dma_start(out[0, q * P:(q + 1) * P, :], x[:, q, :]).then_inc(out_stored, 16)
            sp.wait_ge(out_stored, 16 * NT)


_CONST_NAMES = ("shape_constants", "distance_buckets")
_NAMES = [
    "x", "p", "attn_norm_g", "w_in", "q_lat_norm_g", "w_uq", "kv_lat_norm_g", "w_ukv", "mla_q_norm_g",
    "mla_k_norm_g", "diff_q_norm_g", "diff_k_norm_g", "lambda_q1", "lambda_k1", "lambda_q2", "lambda_k2",
    "diff_out_norm_g", "rel_bias", "w_out", "ffn_norm_g", "w_gate", "w_up", "conv_w", "conv_b", "w_down",
    "ple_norm_g", "w_ple_gate", "w_ple_proj", "c_2", "w_ada_2", "b_ada_2", "w_in_2", "kv_norm_g_2",
    "w_uk_2", "w_uv_2", "conv_w_2", "a_log_2", "dt_bias_2", "dn_norm_g_2", "w_br_att_2", "w_br_dn_2",
    "w_out_2", "w_route_grp_2", "w_route_exp_2", "w_gate_2", "w_up_2", "w_down_2", "ln_g_2", "ln_b_2"]


def program(nc, inputs):
    arrays, t = {}, {}
    consts = dict(zip(_CONST_NAMES, shape_constants()))
    for name in (*_CONST_NAMES, *_NAMES):
        a = np.ascontiguousarray(consts[name] if name in consts else inputs[name])
        arrays[f"in_{name}"] = a
        t[name] = nc.dram_tensor(f"in_{name}", a.shape, F32, kind="ExternalInput").ap()
    out = nc.dram_tensor("out", (1, SEQ, D), F32, kind="ExternalOutput").ap()
    build(nc, t, out)
    return arrays


def kernel(**inputs):
    import concourse.bacc as bacc
    from concourse.bass_utils import run_bass_kernel_spmd
    nc = bacc.Bacc("TRN2", target_bir_lowering=False, num_devices=1)
    arrays = program(nc, inputs)
    r = run_bass_kernel_spmd(nc, [arrays], core_ids=[0])
    return r.results[0]["out"]
```
